# Optimizing a Trainium2 kernel written in Bass

```python
import jax
import jax.numpy as jnp
from jax import lax
import numpy as np

D_MODEL = 1024
BATCH = 1
SEQ = 1024
DEPTH = 2
DEC_BATCH = 8
DEC_SEQ = 16
PAST_LEN = 1024

CHUNK = 64
Q_BLOCK = 128
N_EVEN = (DEPTH + 1) // 2
N_ODD = DEPTH // 2
DN_ALPHA = (2.0 * DEPTH) ** 0.25
DN_BETA = (8.0 * DEPTH) ** -0.25
LN_EPS = 1e-5
NORM_EPS = 1e-6
ROPE_THETA = 500000.0

MLA_HEADS = 8
MLA_Q_LORA = 256
MLA_KV_LORA = 256
MLA_NOPE = 64
MLA_ROPE = 32
MLA_V = 64
MLA_SCALE = (MLA_NOPE + MLA_ROPE) ** -0.5

RET_HEADS = 8
RET_DK = 64
RET_DV = 64
RET_THETA = 10000.0

GLA_HEADS = 4
GLA_DK = 64
GLA_DV = 128
GLA_LOW_RANK = 16
GLA_GATE_NORM = 16.0

SWA_HEADS = 8
SWA_KV_HEADS = 2
SWA_GROUP = SWA_HEADS // SWA_KV_HEADS
SWA_HD = 64
WINDOW = 128
WINDOW_CHUNKS = WINDOW // CHUNK
SWA_ROT = SWA_HD // 4
SWA_SCALE = SWA_HD ** -0.5

D_FF = 2816
CONV_W = 3

EVEN_SIZES = (MLA_Q_LORA, MLA_KV_LORA, MLA_ROPE, RET_HEADS * RET_DK, RET_HEADS * RET_DK, RET_HEADS * RET_DV, RET_HEADS * RET_DV)
ODD_SIZES = (GLA_HEADS * GLA_DK, GLA_HEADS * GLA_DK, GLA_HEADS * GLA_DV, GLA_HEADS * GLA_DV, GLA_LOW_RANK, SWA_HEADS * SWA_HD, SWA_KV_HEADS * SWA_HD, SWA_KV_HEADS * SWA_HD)
IN_EVEN = sum(EVEN_SIZES)
IN_ODD = sum(ODD_SIZES)
MIX_EVEN = MLA_HEADS * MLA_V + RET_HEADS * RET_DV
MIX_ODD = GLA_HEADS * GLA_DV + SWA_HEADS * SWA_HD

kernel_name = 'hybrid_chunk_streaming_encoder_step'

def _split(h, sizes):
    return jnp.split(h, np.cumsum(sizes)[:-1].tolist(), axis=-1)

def layer_norm(x, g, b):
    xf = x.astype(jnp.float32)
    xc = xf - jnp.mean(xf, -1, keepdims=True)
    var = jnp.mean(xc * xc, -1, keepdims=True)
    return (xc * lax.rsqrt(var + LN_EPS) * g.astype(jnp.float32) + b.astype(jnp.float32)).astype(x.dtype)

def rms_norm(x, g):
    xf = x.astype(jnp.float32)
    y = xf * lax.rsqrt(jnp.mean(xf * xf, -1, keepdims=True) + NORM_EPS)
    return (y * g.astype(jnp.float32)).astype(x.dtype)

def head_norm(o, center):
    if center:
        o = o - jnp.mean(o, -1, keepdims=True)
    return o * lax.rsqrt(jnp.mean(o * o, -1, keepdims=True) + NORM_EPS)

def rope_tables(pos, dim, theta):
    inv = 1.0 / (theta ** (jnp.arange(0, dim, 2, dtype=jnp.float32) / dim))
    ang = pos.astype(jnp.float32)[:, None] * inv[None, :]
    return jnp.cos(ang), jnp.sin(ang)

def apply_rope(x, cos, sin):
    x1, x2 = jnp.split(x.astype(jnp.float32), 2, axis=-1)
    c, s = cos[:, None, :], sin[:, None, :]
    return jnp.concatenate([x1 * c - x2 * s, x1 * s + x2 * c], -1).astype(x.dtype)

def chunk_causal_attention(q, k, v, scale):
    B, S, H, Dk = q.shape
    nb = S // Q_BLOCK
    qb = q.reshape(B, nb, Q_BLOCK, H, Dk).swapaxes(0, 1)
    key_chunk = jnp.arange(S) // CHUNK

    def one_block(args):
        i, qi = args
        s = jnp.einsum('bqhd,bkhd->bhqk', qi, k, preferred_element_type=jnp.float32) * scale
        q_chunk = (i * Q_BLOCK + jnp.arange(Q_BLOCK)) // CHUNK
        s = jnp.where(key_chunk[None, :] <= q_chunk[:, None], s, -jnp.inf)
        p = jax.nn.softmax(s, axis=-1).astype(v.dtype)
        return jnp.einsum('bhqk,bkhd->bqhd', p, v)

    out = lax.map(one_block, (jnp.arange(nb), qb))
    return out.swapaxes(0, 1).reshape(B, S, H, v.shape[-1])

def mla_queries(q_lat, pos, q_norm, w_uq):
    B, T, _ = q_lat.shape
    q = (rms_norm(q_lat, q_norm) @ w_uq).reshape(B, T, MLA_HEADS, MLA_NOPE + MLA_ROPE)
    cos, sin = rope_tables(pos, MLA_ROPE, ROPE_THETA)
    return q[..., :MLA_NOPE], apply_rope(q[..., MLA_NOPE:], cos, sin)

def mla_latent_rows(kv_lat, kpe_raw, pos, kv_norm):
    cos, sin = rope_tables(pos, MLA_ROPE, ROPE_THETA)
    return rms_norm(kv_lat, kv_norm), apply_rope(kpe_raw[:, :, None, :], cos, sin)[:, :, 0]

def mla_prompt(q_nope, q_pe, ckv, kpe, w_ukv):
    B, S, _ = ckv.shape
    kv = (ckv @ w_ukv).reshape(B, S, MLA_HEADS, MLA_NOPE + MLA_V)
    k = jnp.concatenate([kv[..., :MLA_NOPE], jnp.broadcast_to(kpe[:, :, None, :], (B, S, MLA_HEADS, MLA_ROPE))], -1)
    q = jnp.concatenate([q_nope, q_pe], -1)
    return chunk_causal_attention(q, k, kv[..., MLA_NOPE:], MLA_SCALE)

def mla_sample(q_nope, q_pe, ckv_all, kpe_all, w_ukv):
    w = w_ukv.reshape(MLA_KV_LORA, MLA_HEADS, MLA_NOPE + MLA_V)
    q_abs = jnp.einsum('bthn,chn->bthc', q_nope, w[..., :MLA_NOPE])
    s = (jnp.einsum('bthc,bkc->bhtk', q_abs, ckv_all, preferred_element_type=jnp.float32)
         + jnp.einsum('bthr,bkr->bhtk', q_pe, kpe_all, preferred_element_type=jnp.float32)) * MLA_SCALE
    p = jax.nn.softmax(s, axis=-1).astype(ckv_all.dtype)
    o_lat = jnp.einsum('bhtk,bkc->bthc', p, ckv_all)
    return jnp.einsum('bthc,chv->bthv', o_lat, w[..., MLA_NOPE:])

def linear_chunk_step(S, q, k, v, g):
    L = q.shape[1]
    qf, kf, vf = q.astype(jnp.float32), k.astype(jnp.float32), v.astype(jnp.float32)
    b = jnp.cumsum(g, axis=1)
    b_last = b[:, -1]
    o_inter = jnp.einsum('blhk,bhkv->blhv', qf * jnp.exp(b), S)
    causal = jnp.tril(jnp.ones((L, L), dtype=bool))
    diff = b[:, :, None] - b[:, None, :]
    if g.shape[-1] == 1:
        decay = jnp.exp(jnp.where(causal[None, :, :, None], diff[..., 0], -jnp.inf))
        A = jnp.einsum('bnhk,bmhk,bnmh->bhnm', qf, kf, decay)
    else:
        decay = jnp.exp(jnp.where(causal[None, :, :, None, None], diff, -jnp.inf))
        A = jnp.einsum('bnhk,bmhk,bnmhk->bhnm', qf, kf, decay)
    o_intra = jnp.einsum('bhnm,bmhv->bnhv', A, vf)
    S_new = jnp.exp(b_last)[..., None] * S + jnp.einsum('bmhk,bmhv->bhkv', kf * jnp.exp(b_last[:, None] - b), vf)
    return S_new, o_inter + o_intra

def linear_attention(q, k, v, g, S0):
    B, T = q.shape[:2]
    if T <= CHUNK:
        return linear_chunk_step(S0, q, k, v, g)
    nc = T // CHUNK
    xs = tuple(t.reshape(B, nc, CHUNK, *t.shape[2:]).swapaxes(0, 1) for t in (q, k, v, g))
    S, o = lax.scan(lambda s, xs_: linear_chunk_step(s, *xs_), S0, xs)
    return S, o.swapaxes(0, 1).reshape(B, T, *o.shape[3:])

def retention(rq, rk, rv, rg, pos, s0, norm_g):
    B, T, _ = rq.shape
    cos, sin = rope_tables(pos, RET_DK, RET_THETA)
    q = apply_rope(rq.reshape(B, T, RET_HEADS, RET_DK), cos, sin)
    k = apply_rope(rk.reshape(B, T, RET_HEADS, RET_DK), cos, sin) * (RET_DK ** -0.5)
    v = rv.reshape(B, T, RET_HEADS, RET_DV)
    log_gamma = jnp.log(1.0 - 2.0 ** (-5.0 - jnp.arange(RET_HEADS, dtype=jnp.float32)))
    g = jnp.broadcast_to(log_gamma[None, None, :, None], (B, T, RET_HEADS, 1))
    s, o = linear_attention(q, k, v, g, s0.astype(jnp.float32))
    y = head_norm(o, True).reshape(B, T, RET_HEADS * RET_DV) * norm_g.astype(jnp.float32)
    return (y * jax.nn.silu(rg.astype(jnp.float32))).astype(rq.dtype), s

def gla(gq, gk, gv, gg, ga, s0, w_a2, b_a, norm_g):
    B, T, _ = gq.shape
    q = gq.reshape(B, T, GLA_HEADS, GLA_DK) * (GLA_DK ** -0.5)
    k = gk.reshape(B, T, GLA_HEADS, GLA_DK)
    v = gv.reshape(B, T, GLA_HEADS, GLA_DV)
    logit = (ga @ w_a2 + b_a).astype(jnp.float32)
    g = (jax.nn.log_sigmoid(logit) / GLA_GATE_NORM).reshape(B, T, GLA_HEADS, GLA_DK)
    s, o = linear_attention(q, k, v, g, s0.astype(jnp.float32))
    y = head_norm(o, False).reshape(B, T, GLA_HEADS * GLA_DV) * norm_g.astype(jnp.float32)
    return (y * jax.nn.silu(gg.astype(jnp.float32))).astype(gq.dtype), s

def partial_rope(x, pos):
    cos, sin = rope_tables(pos, SWA_ROT, ROPE_THETA)
    return jnp.concatenate([apply_rope(x[..., :SWA_ROT], cos, sin), x[..., SWA_ROT:]], -1)

def sink_softmax(s, sinks_hg):
    sk = sinks_hg.astype(jnp.float32)[..., None, None]
    m = jnp.maximum(jnp.max(s, -1, keepdims=True), sk)
    p = jnp.exp(s - m)
    return p / (jnp.sum(p, -1, keepdims=True) + jnp.exp(sk - m))

def swa_prompt(q, k, v, sinks_hg):
    B, S, _, D = q.shape
    nc = S // CHUNK
    nk = (WINDOW_CHUNKS + 1) * CHUNK
    qc = q.reshape(B, nc, CHUNK, SWA_KV_HEADS, SWA_GROUP, D)
    pad = ((0, 0), (WINDOW, 0), (0, 0), (0, 0))
    kp = jnp.pad(k, pad).reshape(B, nc + WINDOW_CHUNKS, CHUNK, SWA_KV_HEADS, D)
    vp = jnp.pad(v, pad).reshape(B, nc + WINDOW_CHUNKS, CHUNK, SWA_KV_HEADS, D)
    kb = jnp.concatenate([kp[:, j:j + nc] for j in range(WINDOW_CHUNKS + 1)], axis=2)
    vb = jnp.concatenate([vp[:, j:j + nc] for j in range(WINDOW_CHUNKS + 1)], axis=2)
    s = jnp.einsum('bcqhgd,bckhd->bchgqk', qc, kb, preferred_element_type=jnp.float32) * SWA_SCALE
    key_chunk = jnp.arange(nc)[:, None] - WINDOW_CHUNKS + (jnp.arange(nk) // CHUNK)[None, :]
    s = jnp.where((key_chunk >= 0)[None, :, None, None, None, :], s, -jnp.inf)
    p = sink_softmax(s, sinks_hg).astype(v.dtype)
    o = jnp.einsum('bchgqk,bckhd->bcqhgd', p, vb)
    return o.reshape(B, S, SWA_HEADS * D)

def swa_sample(q, k_all, v_all, sinks_hg):
    B, T, _, D = q.shape
    qg = q.reshape(B, T, SWA_KV_HEADS, SWA_GROUP, D)
    s = jnp.einsum('bqhgd,bkhd->bhgqk', qg, k_all, preferred_element_type=jnp.float32) * SWA_SCALE
    p = sink_softmax(s, sinks_hg).astype(v_all.dtype)
    return jnp.einsum('bhgqk,bkhd->bqhgd', p, v_all).reshape(B, T, SWA_HEADS * D)

def even_mixer(x, pos, past_ckv, past_kpe, ret_s0, w_in, q_norm, w_uq, kv_norm, w_ukv, ret_norm, w_out):
    B, T, _ = x.shape
    q_lat, kv_lat, kpe_raw, rq, rk, rv, rg = _split(x @ w_in, EVEN_SIZES)
    q_nope, q_pe = mla_queries(q_lat, pos, q_norm, w_uq)
    ckv, kpe = mla_latent_rows(kv_lat, kpe_raw, pos, kv_norm)
    if past_ckv is None:
        a = mla_prompt(q_nope, q_pe, ckv, kpe, w_ukv)
    else:
        ckv_all = jnp.concatenate([past_ckv.astype(ckv.dtype), ckv], 1)
        kpe_all = jnp.concatenate([past_kpe.astype(kpe.dtype), kpe], 1)
        a = mla_sample(q_nope, q_pe, ckv_all, kpe_all, w_ukv)
    r, ret_s = retention(rq, rk, rv, rg, pos, ret_s0, ret_norm)
    out = jnp.concatenate([a.reshape(B, T, MLA_HEADS * MLA_V), r], -1) @ w_out
    return out, ckv, kpe, ret_s

def odd_mixer(x, pos, gla_s0, past_k, past_v, w_in, w_a2, b_a, gla_norm, sinks, w_out):
    B, T, _ = x.shape
    gq, gk, gv, gg, ga, sq, sk, sv = _split(x @ w_in, ODD_SIZES)
    y_gla, gla_s = gla(gq, gk, gv, gg, ga, gla_s0, w_a2, b_a, gla_norm)
    q = partial_rope(sq.reshape(B, T, SWA_HEADS, SWA_HD), pos)
    k = partial_rope(sk.reshape(B, T, SWA_KV_HEADS, SWA_HD), pos)
    v = sv.reshape(B, T, SWA_KV_HEADS, SWA_HD)
    sinks_hg = sinks.reshape(SWA_KV_HEADS, SWA_GROUP)
    if past_k is None:
        a = swa_prompt(q, k, v, sinks_hg)
        k_buf, v_buf = k[:, -WINDOW:], v[:, -WINDOW:]
    else:
        rows = past_k.shape[1]
        k_all = jnp.concatenate([past_k.astype(k.dtype), k], 1)
        v_all = jnp.concatenate([past_v.astype(v.dtype), v], 1)
        a = swa_sample(q, k_all, v_all, sinks_hg)
        k_buf, v_buf = k_all[:, -rows:], v_all[:, -rows:]
    out = jnp.concatenate([y_gla, a], -1) @ w_out
    return out, gla_s, k_buf, v_buf

def conv_ffn(x, conv_prev, w_up, conv_w, conv_b, w_down):
    B, T, _ = x.shape
    u = x @ w_up
    if conv_prev is None:
        conv_prev = jnp.zeros((B, CONV_W - 1, u.shape[-1]), u.dtype)
    ue = jnp.concatenate([conv_prev.astype(u.dtype), u], 1)
    c = conv_b
    for j in range(CONV_W):
        c = c + ue[:, j:j + T] * conv_w[j]
    a, b = jnp.split(c, 2, axis=-1)
    y = (jax.nn.silu(a) * b) @ w_down
    return y, ue[:, -(CONV_W - 1):]

def run_trunk(x, pos, st, w):
    B = x.shape[0]
    ckvs, kpes, rets, glas, kbufs, vbufs, convs = [], [], [], [], [], [], []
    for layer in range(DEPTH):
        t = layer // 2
        if layer % 2 == 0:
            if st is None:
                past_ckv, past_kpe = None, None
                s0 = jnp.zeros((B, RET_HEADS, RET_DK, RET_DV), jnp.float32)
            else:
                past_ckv, past_kpe, s0 = st['ckv'][t], st['kpe'][t], st['ret'][t]
            m, ckv, kpe, s = even_mixer(x, pos, past_ckv, past_kpe, s0, w['w_in_even'][t], w['mla_q_norm'][t],
                                        w['mla_w_uq'][t], w['mla_kv_norm'][t], w['mla_w_ukv'][t],
                                        w['ret_norm'][t], w['w_out_even'][t])
            ckvs.append(ckv)
            kpes.append(kpe)
            rets.append(s)
        else:
            if st is None:
                past_k, past_v = None, None
                s0 = jnp.zeros((B, GLA_HEADS, GLA_DK, GLA_DV), jnp.float32)
            else:
                past_k, past_v, s0 = st['swa_k'][t], st['swa_v'][t], st['gla'][t]
            m, s, kb, vb = odd_mixer(x, pos, s0, past_k, past_v, w['w_in_odd'][t], w['gla_w_a2'][t],
                                     w['gla_b_a'][t], w['gla_norm'][t], w['swa_sinks'][t], w['w_out_odd'][t])
            glas.append(s)
            kbufs.append(kb)
            vbufs.append(vb)
        x = layer_norm(DN_ALPHA * x + m, w['ln_mix_g'][layer], w['ln_mix_b'][layer])
        f, c = conv_ffn(x, None if st is None else st['conv'][layer], w['ffn_w_up'][layer],
                        w['ffn_conv_w'][layer], w['ffn_conv_b'][layer], w['ffn_w_down'][layer])
        convs.append(c)
        x = layer_norm(DN_ALPHA * x + f, w['ln_ffn_g'][layer], w['ln_ffn_b'][layer])
    return (x, jnp.stack(ckvs), jnp.stack(kpes), jnp.stack(rets), jnp.stack(glas),
            jnp.stack(kbufs), jnp.stack(vbufs), jnp.stack(convs))

def setup_inputs(seed: int = 0) -> dict:
    key = jax.random.key(seed)
    keys = list(jax.random.split(key, 40))

    def nrm(shape, scale):
        return jax.random.normal(keys.pop(), shape, jnp.float32) * scale

    def gain(shape):
        return 1.0 + nrm(shape, 0.02)

    swa_rows = min(WINDOW, PAST_LEN)
    return {
        'x_prompt': nrm((BATCH, SEQ, D_MODEL), 1.0),
        'x_sample': nrm((DEC_BATCH, DEC_SEQ, D_MODEL), 1.0),
        'cache_mla_ckv': nrm((N_EVEN, DEC_BATCH, PAST_LEN, MLA_KV_LORA), 1.0),
        'cache_mla_kpe': nrm((N_EVEN, DEC_BATCH, PAST_LEN, MLA_ROPE), 1.0),
        'state_ret': nrm((N_EVEN, DEC_BATCH, RET_HEADS, RET_DK, RET_DV), 0.3),
        'state_gla': nrm((N_ODD, DEC_BATCH, GLA_HEADS, GLA_DK, GLA_DV), 0.3),
        'cache_swa_k': nrm((N_ODD, DEC_BATCH, swa_rows, SWA_KV_HEADS, SWA_HD), 1.0),
        'cache_swa_v': nrm((N_ODD, DEC_BATCH, swa_rows, SWA_KV_HEADS, SWA_HD), 1.0),
        'state_ffn_conv': nrm((DEPTH, DEC_BATCH, CONV_W - 1, 2 * D_FF), 1.0),
        'w_in_even': nrm((N_EVEN, D_MODEL, IN_EVEN), D_MODEL ** -0.5),
        'mla_q_norm': gain((N_EVEN, MLA_Q_LORA)),
        'mla_w_uq': nrm((N_EVEN, MLA_Q_LORA, MLA_HEADS * (MLA_NOPE + MLA_ROPE)), MLA_Q_LORA ** -0.5),
        'mla_kv_norm': gain((N_EVEN, MLA_KV_LORA)),
        'mla_w_ukv': nrm((N_EVEN, MLA_KV_LORA, MLA_HEADS * (MLA_NOPE + MLA_V)), MLA_KV_LORA ** -0.5),
        'ret_norm': gain((N_EVEN, RET_HEADS * RET_DV)),
        'w_out_even': nrm((N_EVEN, MIX_EVEN, D_MODEL), DN_BETA * MIX_EVEN ** -0.5),
        'w_in_odd': nrm((N_ODD, D_MODEL, IN_ODD), D_MODEL ** -0.5),
        'gla_w_a2': nrm((N_ODD, GLA_LOW_RANK, GLA_HEADS * GLA_DK), GLA_LOW_RANK ** -0.5),
        'gla_b_a': nrm((N_ODD, GLA_HEADS * GLA_DK), 0.1),
        'gla_norm': gain((N_ODD, GLA_HEADS * GLA_DV)),
        'swa_sinks': nrm((N_ODD, SWA_HEADS), 0.5),
        'w_out_odd': nrm((N_ODD, MIX_ODD, D_MODEL), DN_BETA * MIX_ODD ** -0.5),
        'ffn_w_up': nrm((DEPTH, D_MODEL, 2 * D_FF), D_MODEL ** -0.5),
        'ffn_conv_w': nrm((DEPTH, CONV_W, 2 * D_FF), CONV_W ** -0.5),
        'ffn_conv_b': nrm((DEPTH, 2 * D_FF), 0.02),
        'ffn_w_down': nrm((DEPTH, D_FF, D_MODEL), DN_BETA * D_FF ** -0.5),
        'ln_mix_g': gain((DEPTH, D_MODEL)),
        'ln_mix_b': nrm((DEPTH, D_MODEL), 0.02),
        'ln_ffn_g': gain((DEPTH, D_MODEL)),
        'ln_ffn_b': nrm((DEPTH, D_MODEL), 0.02),
    }

def reference(x_prompt, x_sample, cache_mla_ckv, cache_mla_kpe, state_ret, state_gla, cache_swa_k, cache_swa_v,
              state_ffn_conv, w_in_even, mla_q_norm, mla_w_uq, mla_kv_norm, mla_w_ukv, ret_norm, w_out_even,
              w_in_odd, gla_w_a2, gla_b_a, gla_norm, swa_sinks, w_out_odd, ffn_w_up, ffn_conv_w, ffn_conv_b,
              ffn_w_down, ln_mix_g, ln_mix_b, ln_ffn_g, ln_ffn_b):
    w = {'w_in_even': w_in_even, 'mla_q_norm': mla_q_norm, 'mla_w_uq': mla_w_uq, 'mla_kv_norm': mla_kv_norm,
         'mla_w_ukv': mla_w_ukv, 'ret_norm': ret_norm, 'w_out_even': w_out_even, 'w_in_odd': w_in_odd,
         'gla_w_a2': gla_w_a2, 'gla_b_a': gla_b_a, 'gla_norm': gla_norm, 'swa_sinks': swa_sinks,
         'w_out_odd': w_out_odd, 'ffn_w_up': ffn_w_up, 'ffn_conv_w': ffn_conv_w, 'ffn_conv_b': ffn_conv_b,
         'ffn_w_down': ffn_w_down, 'ln_mix_g': ln_mix_g, 'ln_mix_b': ln_mix_b, 'ln_ffn_g': ln_ffn_g,
         'ln_ffn_b': ln_ffn_b}
    st = {'ckv': cache_mla_ckv, 'kpe': cache_mla_kpe, 'ret': state_ret, 'gla': state_gla,
          'swa_k': cache_swa_k, 'swa_v': cache_swa_v, 'conv': state_ffn_conv}
    pos_p = jnp.arange(x_prompt.shape[1])
    pos_s = cache_mla_ckv.shape[2] + jnp.arange(x_sample.shape[1])
    y_prompt, p_ckv, p_kpe, p_ret, p_gla, p_k, p_v, p_conv = run_trunk(x_prompt, pos_p, None, w)
    y_sample, s_ckv, s_kpe, s_ret, s_gla, s_k, s_v, s_conv = run_trunk(x_sample, pos_s, st, w)
    return (y_prompt, y_sample, p_ckv, p_kpe, p_ret, p_gla, p_k, p_v, p_conv,
            s_ckv, s_kpe, s_ret, s_gla, s_k, s_v, s_conv)


_drawn_inputs = setup_inputs


def setup_inputs(seed=0):
    import zlib

    import numpy as np

    out = dict(_drawn_inputs(seed))
    spreads = {}
    factors = {'cache_mla_ckv': 3.099,
     'cache_mla_kpe': 5.708,
     'mla_q_norm': 8.0,
     'mla_kv_norm': 2.811,
     'ret_norm': 8.0,
     'gla_norm': 8.0,
     'swa_sinks': 8.0,
     'ffn_conv_b': 6.437}
    for name, (base, spread) in spreads.items():
        noise = np.random.default_rng([zlib.crc32(name.encode()), seed]).standard_normal(out[name].shape)
        drawn = base * np.exp(spread * noise) if base else spread * noise
        out[name] = jnp.asarray(drawn.astype(out[name].dtype))
    for name, factor in factors.items():
        out[name] = (out[name] * factor).astype(out[name].dtype)
    return out
```

```python
from contextlib import contextmanager

import numpy as np
import concourse.bass as bass
from concourse import mybir

F = mybir.dt.float32
R = mybir.dt.float32r
ACT = mybir.ActivationFunctionType
ALU = mybir.AluOpType
AX = mybir.AxisListType

P = 128
D = 1024
KD = D // P
SEQ = 1024
TP = SEQ // P
NT = TP + 1
TOK = NT * P
NB = 8
ST = 16
PAST = 1024
ALPHA = 4.0 ** 0.25
LN_EPS = 1e-5
NORM_EPS = 1e-6
NEG = -1e30
MLA_H, MLA_C, NOPE, ROPE = 8, 256, 64, 32
MLA_SCALE = (NOPE + ROPE) ** -0.5
HD = 64
FF = 2816
NJ = FF // P
GRP = 384
UW = 2 + SEQ + NB * (2 + ST)
US = 2 + SEQ


class Chain:

    def __init__(self, eng, sem):
        self.eng, self.sem, self.done, self.n, self.i, self.per = eng, sem, 0, 0, None, 0

    def __call__(self, ins):
        self.n += 1
        ins.then_inc(self.sem, 1)
        self.eng.wait_ge(self.sem, self.done + self.n + (0 if self.i is None else self.i * self.per))

    @contextmanager
    def loop(self, count, per):
        self.done, self.n, self.per = self.done + self.n, 0, per
        with self.eng.Fori(0, count) as i:
            self.i = i
            yield i
        assert self.n == per, (str(self.sem), "links in a turn:", self.n)
        self.done, self.n, self.i = self.done + count * per, 0, None


class Ctx:

    def __init__(self, nc, A):
        self.nc, self.A = nc, A

    def sb(self, name, shape, dt=F):
        return self.nc.alloc_sbuf_tensor(name, shape, dt)

    def sem(self, name):
        return self.nc.alloc_semaphore(name=name)


def one(ap, i):
    return ap[bass.ds(i, 1)].squeeze(0)



class Split:

    def __init__(self, c, name, n, width, src, ring=4):
        self.c, self.n, self.width, self.src, self.ring = c, n, width, src, ring
        self.raw = c.sb(name + "_raw", [P, ring, width])
        self.hi = c.sb(name + "_hi", [P, n, width], R)
        self.lo = c.sb(name + "_lo", [P, n, width], R)
        self.ld = [c.sem(f"{name}_loaded{s}") for s in range(ring)]
        self.w_hi = c.sem(name + "_hi_done")
        self.w_split = [c.sem(f"{name}_split_{e}") for e in ("pool", "dve")]

    def load(self, sp, i=0):
        for k in range(self.n):
            sp.wait_ge(self.w_split[k % 2], i * (self.n // 2) + k // 2 + 1)
            sp.dma_start(self.raw[:, k % self.ring, :], self.src(i, k)).then_inc(self.ld[k % self.ring], 16)

    def make_hi(self, act, i=0, ks=None):
        for k in ks or range(self.n):
            act.wait_ge(self.ld[k % self.ring], i * (self.n // self.ring) * 16 + (k // self.ring + 1) * 16)
            self.c.nc.scalar.activation(self.hi[:, k, :], self.raw[:, k % self.ring, :], ACT.Copy).then_inc(self.w_hi, 1)

    def free_slots(self, pool):
        for split in self.w_split:
            pool.sem_inc(split, self.ring // 2)

    def make_lo(self, eng, ops, half, i=0):
        for k in range(half, self.n, 2):
            eng.wait_ge(self.w_hi, i * self.n + k + 1)
            ops.tensor_tensor(self.lo[:, k, :], self.raw[:, k % self.ring, :],
                              self.hi[:, k, :].bitcast(F), ALU.subtract).then_inc(self.w_split[half], 1)

    def wait(self, pe, k, i=0):
        pe.wait_ge(self.w_split[k % 2], i * (self.n // 2) + k // 2 + 1 + self.ring // 2)


def mm3(nc, out, a, b, first, last):
    nc.tensor.matmul(out, a[0], b[0], start=first, stop=False)
    nc.tensor.matmul(out, a[0], b[1], start=False, stop=False)
    return nc.tensor.matmul(out, a[1], b[0], start=False, stop=last)


def project_tile(c, pe, w, t, out, cols, i=0):
    for k in range(KD):
        if t == 0:
            w.wait(pe, k, i)
        xs = slice(t * P, (t + 1) * P)
        last = mm3(c.nc, out, (c.xTh[:, k, xs], c.xTl[:, k, xs]), (w.hi[:, k, cols], w.lo[:, k, cols]),
                   k == 0, k == KD - 1)
    return last



def phase_start(c):
    nc, A = c.nc, c.A
    ld, hi, ms = c.sem("start_loaded"), c.sem("start_hi"), c.sem("start_done")
    raw = c.XM
    rawf = raw[:].rearrange("p t d -> p (t d)")
    hif = c.xTh[:].rearrange("p k t -> p (k t)")
    lof = c.xTl[:].rearrange("p k t -> p (k t)")
    with nc.Block() as block:
        @block.sync
        def _(sp):
            sp.dma_start(c.ident[:], A["ident"]).then_inc(ms, 16)
            sp.dma_start(c.masks[:], A["masks"]).then_inc(ms, 16)
            sp.dma_start(rawf, A["xT"]).then_inc(ld, 16)
            sp.wait_ge(ms, 32)

        @block.scalar
        def _(act):
            act.wait_ge(ld, 16)
            for k in range(KD):
                s = slice(k * TOK, (k + 1) * TOK)
                nc.scalar.activation(hif[:, s], rawf[:, s], ACT.Copy).then_inc(hi, 1)

        @block.vector
        def _(dve):
            for k in range(KD):
                dve.wait_ge(hi, k + 1)
                s = slice(k * TOK, (k + 1) * TOK)
                nc.vector.tensor_tensor(lof[:, s], rawf[:, s], hif[:, s].bitcast(F), ALU.subtract)


def phase_latents(c, M):
    nc, A, PS = c.nc, c.A, c.PS
    w = Split(c, "wlat", KD, 640, lambda i, k: A["w_lat"][k], ring=2)
    lat = c.sb("lat", [P, NT, 512])
    sq = c.sb("lat_sq", [P, 256])
    ss = c.sb("lat_ss", [P, NT * 2])
    nrm = c.sb("lat_norm", [P, 512])
    tmp = c.sb("kpe_tmp", [P, GRP])
    prj, ev, tr, tev, kp = (c.sem("lat_" + s) for s in ("projected", "evacuated", "transposed", "latT_ready", "kpe_projected"))
    rs_in, rs_out, nd, ld, outs, dch, ach = (c.sem("lat_" + s) for s in
                                       ("squares", "rstd", "normed", "consts", "stored", "dve", "act"))
    with nc.Block() as block:
        @block.sync
        def _(sp):
            w.load(sp)
            sp.dma_start(nrm[:], A["lat_norm"].partition_broadcast(P)).then_inc(ld, 16)
            sp.dma_start(M.T[64:128, :], A["kpe_tab"]).then_inc(ld, 16)
            sp.wait_ge(nd, 1)
            sp.dma_start(A["o_ckv_p"].rearrange("(t p) c -> p t c", p=P), lat[:, 0:TP, 256:512]).then_inc(outs, 16)
            sp.dma_start(A["o_ckv_s"], lat[:, TP, 256:512]).then_inc(outs, 16)
            sp.wait_ge(kp, 4)
            sp.dma_start(A["o_kpe"], M.KT[64:96, :]).then_inc(outs, 16)
            sp.wait_ge(outs, 48)

        @block.gpsimd
        def _(pool):
            w.free_slots(pool)
            w.make_lo(pool, nc.gpsimd, 0)

        @block.tensor
        def _(pe):
            for t in range(NT):
                if t >= 2:
                    pe.wait_ge(ev, t - 1)
                project_tile(c, pe, w, t, PS[:, t % 2, :], slice(0, 512)).then_inc(prj, 1)
            for g in range(3):
                for k in range(KD):
                    xs = slice(g * GRP, (g + 1) * GRP)
                    last = mm3(nc, PS[:, 2 + g, 0:GRP], (w.hi[:, k, 512:640], w.lo[:, k, 512:640]),
                               (c.xTh[:, k, xs], c.xTl[:, k, xs]), k == 0, k == KD - 1)
                last.then_inc(kp, 1)
            pe.wait_ge(nd, 1)
            for t in range(NT):
                if t >= 2:
                    pe.wait_ge(tev, t - 1)
                for q in range(4):
                    last = nc.tensor.transpose(PS[:, 6 + t % 2, q * P:(q + 1) * P], lat[:, t, q * P:(q + 1) * P], c.ident[:])
                last.then_inc(tr, 1)

        @block.scalar
        def _(act):
            w.make_hi(act)
            for t in range(NT):
                act.wait_ge(prj, t + 1)
                for s in range(2):
                    if t or s:
                        act.wait_ge(ach, 2 * t + s)
                    nc.scalar.activation(sq[:], PS[:, t % 2, s * 256:(s + 1) * 256], ACT.Square,
                                         accum_out=ss[:, 2 * t + s:2 * t + s + 1]).then_inc(ach, 1)
                nc.scalar.activation(lat[:, t, :], PS[:, t % 2, :], ACT.Copy).then_inc(ev, 1)
            act.wait_ge(rs_in, 1)
            nc.scalar.activation(ss[:], ss[:], ACT.Ln).then_inc(ach, 1)
            act.wait_ge(ach, 2 * NT + 1)
            nc.scalar.activation(ss[:], ss[:], ACT.Exp, scale=-0.5).then_inc(rs_out, 1)
            for t in range(NT):
                act.wait_ge(tr, t + 1)
                nc.scalar.activation(M.latT[:, :, t * P:(t + 1) * P],
                                     PS[:, 6 + t % 2, :].rearrange("p (q n) -> p q n", q=4), ACT.Copy).then_inc(tev, 1)

        @block.vector
        def _(dve):
            link = Chain(dve, dch)
            w.make_lo(dve, nc.vector, 1)
            dve.wait_ge(ld, 32)
            dve.wait_ge(ev, NT)
            nc.vector.tensor_scalar(ss[:], ss[:], 1.0 / 256, NORM_EPS, ALU.mult, ALU.add).then_inc(rs_in, 1)
            dve.wait_ge(rs_out, 1)
            for t in range(NT):
                for s in range(2):
                    x = lat[:, t, s * 256:(s + 1) * 256]
                    last = nc.vector.scalar_tensor_tensor(x, x, ss[:, 2 * t + s:2 * t + s + 1],
                                                          nrm[:, s * 256:(s + 1) * 256], ALU.mult, ALU.mult)
            last.then_inc(nd, 1)
            for g in range(3):
                dve.wait_ge(kp, g + 1)
                xs = slice(g * GRP, (g + 1) * GRP)
                nc.vector.tensor_tensor(M.KT[64:96, xs], PS[64:96, 2 + g, 0:GRP], M.T[64:96, xs], ALU.mult)
                link(nc.vector.tensor_tensor(tmp[64:96, :], PS[96:128, 2 + g, 0:GRP], M.T[96:128, xs], ALU.mult))
                link(nc.vector.tensor_tensor(M.KT[64:96, xs], M.KT[64:96, xs], tmp[64:96, :], ALU.add))
            nc.vector.tensor_copy(M.ckv_s[:], lat[:, TP, 256:512]).then_inc(kp, 1)


def softmax_max(nc, dve, link, mx, nm, scores, scale):
    link(nc.vector.tensor_reduce(out=mx, in_=scores, axis=AX.X, op=ALU.max))
    return nc.vector.tensor_scalar(nm, mx, -scale, None, ALU.mult)


def phase_mla_prompt(c, M):
    nc, A, PS = c.nc, c.A, c.PS
    V = c.sb("mla_v", [P, TP, 512])
    QH = c.sb("mla_qT", [P, TOK])
    wq = c.sb("mla_wq", [P, 2, P])
    wk = c.sb("mla_wk", [P, 2, NOPE])
    wkT = c.sb("mla_wkT", [NOPE, 256])
    tmp = c.sb("rope_tmp", [P, GRP])
    Pb = c.sb("mla_p", [P, 2, D])
    PTs = c.sb("mla_pT", [P, 2, TP, P])
    mx = c.sb("mla_mx", [P, 2])
    nm = c.sb("mla_nm", [P, 2])
    rs = c.sb("mla_rs", [P, 2])
    ri = c.sb("mla_ri", [P, 2])
    names = ("wv_loaded", "w_loaded", "v_projected", "v_ready", "q_projected", "k_projected", "q_nope", "q_rope", "k_ready",
             "abs_projected", "abs_ready", "scored", "max_ready", "exp_done", "transposed", "pT_dve", "pT_act", "pv_done", "o_written", "dve")
    (wvl, wl, vp, vr, qp, kp, qn, qr, kr, ap_, ar, sc, nms, ex, tr, ptd, pta, pv, ow, dch) = (c.sem("mla_" + s) for s in names)

    def tok(i):
        return slice(i * P, (i + 1) * P)

    with nc.Block() as block:
        @block.gpsimd
        def _(pool):
            for started in (ap_, ow):
                pool.sem_inc(started, 1)

        @block.sync
        def _(sp):
            sp.dma_start(M.wuv[:], A["w_uv"]).then_inc(wvl, 16)
            sp.dma_start(M.rows[:], A["mla_rows"]).then_inc(wvl, 16)
            with sp.Fori(0, MLA_H) as h:
                sp.wait_ge(ap_, h + 1)
                sp.dma_start(wq[:], one(A["w_uq"], h)).then_inc(wl, 16)
                sp.dma_start(wk[:], one(A["w_uk"], h)).then_inc(wl, 16)
                sp.dma_start(wkT[:], one(A["w_ukT"], h)).then_inc(wl, 16)

        @block.tensor
        def _(pe):
            pe.wait_ge(wvl, 32)
            for t in range(TP):
                if t >= 2:
                    pe.wait_ge(vr, t - 1)
                for s in range(2):
                    last = nc.tensor.matmul(PS[:, t % 2, :], M.latT[:, 2 + s, tok(t)], M.wuv[:, s, :], start=s == 0, stop=s == 1)
                last.then_inc(vp, 1)
            pe.wait_ge(vr, TP)
            with pe.Fori(0, MLA_H) as h:
                pe.wait_ge(wl, 48 * h + 48)
                for g in range(3):
                    for s in range(2):
                        last = nc.tensor.matmul(PS[:, g, 0:GRP], wq[:, s, :], M.latT[:, s, g * GRP:(g + 1) * GRP], start=s == 0, stop=s == 1)
                    last.then_inc(qp, 1)
                for g in range(2):
                    for s in range(2):
                        last = nc.tensor.matmul(PS[0:64, 3 + g, :], wk[:, s, :], M.latT[:, 2 + s, g * 512:(g + 1) * 512], start=s == 0, stop=s == 1)
                    last.then_inc(kp, 1)
                pe.wait_ge(qn, 3 * h + 3)
                for s in range(2):
                    last = nc.tensor.matmul(PS[:, 5, tok(s)], wkT[:, s * P:(s + 1) * P], QH[0:64, TP * P:], start=s == 0, stop=s == 1,
                                            skip_group_check=True)
                last.then_inc(ap_, 1)
                pe.wait_ge(qr, 3 * h + 3)
                pe.wait_ge(kr, 2 * h + 2)
                pe.wait_ge(ar, h + 1)

                def scores(i):
                    n = (i + 1) * P
                    for a in range(0, n, 512):
                        b = min(a + 512, n)
                        bank = 2 * (i % 2) + a // 512
                        nc.tensor.matmul(PS[:, bank, 0:b - a], QH[0:96, tok(i)], M.KT[0:96, a:b], start=True, stop=b < n)
                    nc.tensor.matmul(PS[:, bank, b - a - P:b - a], M.rows[0:1, c.at["ROW"]:c.at["ROW"] + P],
                                     M.rows[0:1, c.at["NEG"]:c.at["NEG"] + P], start=False, stop=True).then_inc(sc, 1)

                scores(0)
                for i in range(TP):
                    if i + 1 < TP:
                        scores(i + 1)
                    pe.wait_ge(ex, TP * h + i + 1)
                    for b in range(i + 1):
                        last = nc.tensor.transpose(PS[:, 4 + b // 4, tok(b % 4)], Pb[:, i % 2, tok(b)], c.ident[:])
                    last.then_inc(tr, 1)
                    pe.wait_ge(ptd, TP * h + i + 1)
                    if i >= 4:
                        pe.wait_ge(pta, 4 * h + i - 3)
                    pe.wait_ge(ow, TP * h + i + 1)
                    for b in range(i + 1):
                        last = nc.tensor.matmul(PS[:, 6, 0:64], PTs[:, i % 2, b, :], V[:, b, bass.ds(h * 64, 64)], start=b == 0, stop=b == i)
                    last.then_inc(pv, 1)

        @block.scalar
        def _(act):
            for t in range(TP):
                act.wait_ge(vp, t + 1)
                nc.scalar.activation(V[:, t, :], PS[:, t % 2, :], ACT.Copy).then_inc(vr, 1)
            with act.Fori(0, MLA_H) as h:
                for g in range(3):
                    act.wait_ge(qp, 3 * h + g + 1)
                    nc.scalar.activation(QH[0:64, g * GRP:(g + 1) * GRP], PS[0:64, g, 0:GRP], ACT.Copy).then_inc(qn, 1)
                for g in range(2):
                    act.wait_ge(kp, 2 * h + g + 1)
                    nc.scalar.activation(M.KT[0:64, g * 512:(g + 1) * 512], PS[0:64, 3 + g, :], ACT.Copy).then_inc(kr, 1)
                act.wait_ge(ap_, h + 2)
                nc.scalar.activation(M.qabs[:, :, bass.ds(h, 1), :].squeeze(2), PS[:, 5, 0:256].rearrange("p (s n) -> p s n", s=2),
                                     ACT.Copy).then_inc(ar, 1)
                for i in range(TP):
                    n = (i + 1) * P
                    act.wait_ge(nms, TP * h + i + 1)
                    src = PS[:, 2 * (i % 2):2 * (i % 2) + 2, :].rearrange("p b n -> p (b n)")[:, 0:n]
                    nc.scalar.activation(Pb[:, i % 2, 0:n], src, ACT.Exp, bias=nm[:, i % 2:i % 2 + 1], scale=MLA_SCALE,
                                         accum_out=rs[:, i % 2:i % 2 + 1]).then_inc(ex, 1)
                    if i >= 4:
                        act.wait_ge(tr, TP * h + i + 1)
                        nc.scalar.activation(PTs[:, i % 2, 4:i + 1, :], PS[:, 5, 0:(i - 3) * P].rearrange("p (b n) -> p b n", n=P),
                                             ACT.Copy).then_inc(pta, 1)

        @block.vector
        def _(dve):
            link = Chain(dve, dch)
            with link.loop(MLA_H, 39) as h:
                for g in range(3):
                    dve.wait_ge(qp, 3 * h + g + 1)
                    xs = slice(g * GRP, (g + 1) * GRP)
                    nc.vector.tensor_tensor(QH[64:96, xs], PS[64:96, g, 0:GRP], M.T[64:96, xs], ALU.mult)
                    link(nc.vector.tensor_tensor(tmp[64:96, :], PS[96:128, g, 0:GRP], M.T[96:128, xs], ALU.mult))
                    link(nc.vector.tensor_tensor(QH[64:96, xs], QH[64:96, xs], tmp[64:96, :], ALU.add))
                    dve.sem_inc(qr, 1)
                link(nc.vector.tensor_copy(M.qpe[64:96, bass.ds(h, 1), :].squeeze(1), QH[64:96, TP * P:]))

                def largest(i):
                    n = (i + 1) * P
                    dve.wait_ge(sc, TP * h + i + 1)
                    src = PS[:, 2 * (i % 2):2 * (i % 2) + 2, :].rearrange("p b n -> p (b n)")[:, 0:n]
                    link(softmax_max(nc, dve, link, mx[:, i % 2:i % 2 + 1], nm[:, i % 2:i % 2 + 1], src, MLA_SCALE))
                    dve.sem_inc(nms, 1)

                largest(0)
                for i in range(TP):
                    if i + 1 < TP:
                        largest(i + 1)
                    m = min(i + 1, 4)
                    dve.wait_ge(tr, TP * h + i + 1)
                    nc.vector.tensor_copy(PTs[:, i % 2, 0:m, :], PS[:, 4, 0:m * P].rearrange("p (b n) -> p b n", n=P)).then_inc(ptd, 1)
                    link(nc.vector.reciprocal(ri[:, i % 2:i % 2 + 1], rs[:, i % 2:i % 2 + 1]))
                    dve.wait_ge(pv, TP * h + i + 1)
                    link(nc.vector.tensor_scalar(c.XM[:, i, bass.ds(h * 64, 64)], PS[:, 6, 0:64], ri[:, i % 2:i % 2 + 1], None, ALU.mult))
                    dve.sem_inc(ow, 1)


def phase_mla_sample(c, M):
    nc, A, PS = c.nc, c.A, c.PS
    NK = PAST // P + 1
    ckv = c.sb("s_ckv", [P, NK - 1, 256])
    ckvT = c.sb("s_ckvT", [P, 2, 2, PAST])
    kpeT = c.sb("s_kpeT", [P, 2, PAST])
    qb = c.sb("s_qb", [P, 2, 2, P])
    qpb = c.sb("s_qpb", [P, 2, P])
    Pb = c.sb("s_p", [P, NK * P])
    PTs = c.sb("s_pT", [P, NK, P])
    ol = c.sb("s_olat", [P, 256])
    olT = M.qabs
    mx, nm, rs, ri = (c.sb("s_" + s, [P, 1]) for s in ("mx", "nm", "rs", "ri"))
    names = ("k_loaded", "v_loaded", "q_ready", "scored", "max_ready", "exp_done", "transposed", "pT_ready", "pv_done", "o_ready",
             "o_transposed", "oT_ready", "uv_done", "dve")
    (kl, vl, qd, sc, nms, ex, tr, pt, pv, orr, otr, otd, uv, dch) = (c.sem("ms_" + s) for s in names)
    kl = [kl, c.sem("ms_k_loaded1")]
    ol_ = c.sem("ms_own_loaded")
    HALF = NB // 2
    with nc.Block() as block:
        @block.gpsimd
        def _(pool):
            for started in (sc, pv, otd):
                pool.sem_inc(started, 1)

        @block.sync
        def _(sp):
            sp.dma_start(M.KT[96:97, 0:NB * P], A["mla_own"]).then_inc(ol_, 16)
            with sp.Fori(0, HALF) as i:
                for s in range(2):
                    b = 2 * i + s
                    sp.wait_ge(sc, 2 * i + 1)
                    sp.dma_start(ckvT[:, s], one(A["c_ckvT"], b)).then_inc(kl[s], 16)
                    sp.dma_start(kpeT[64:96, s, :], one(A["c_kpeT"], b)).then_inc(kl[s], 16)
                    sp.wait_ge(pv, b + 1)
                    sp.dma_start(ckv[:], one(A["c_ckv"], b)).then_inc(vl, 16)

        @block.tensor
        def _(pe):
            with pe.Fori(0, HALF) as i:
                for s in range(2):
                    b = 2 * i + s
                    pe.wait_ge(kl[s], 32 * i + 32)
                    pe.wait_ge(qd, b + 1)
                    for g in range(3):
                        n = P if g == 2 else 512
                        for q in range(2):
                            rhs = M.latT[:, 2 + q, TP * P:] if g == 2 else ckvT[:, s, q, g * 512:(g + 1) * 512]
                            nc.tensor.matmul(PS[:, g, 0:n], qb[:, s, q, :], rhs, start=q == 0, stop=False)
                        rhs = M.KT[64:97, TP * P:] if g == 2 else kpeT[64:96, s, g * 512:(g + 1) * 512]
                        last = nc.tensor.matmul(PS[:, g, 0:n], qpb[64:97 if g == 2 else 96, s, :], rhs, start=False, stop=True)
                    last.then_inc(sc, 1)
                    pe.wait_ge(ex, b + 1)
                    for k in range(NK):
                        last = nc.tensor.transpose(PS[:, 3 + k // 4, (k % 4) * P:(k % 4 + 1) * P], Pb[:, k * P:(k + 1) * P], c.ident[:])
                    last.then_inc(tr, 1)
                    pe.wait_ge(pt, 2 * b + 2)
                    pe.wait_ge(vl, 16 * b + 16)
                    for k in range(NK):
                        rhs = M.ckv_s[:] if k == NK - 1 else ckv[:, k, :]
                        last = nc.tensor.matmul(PS[:, 6, 0:256], PTs[:, k, :], rhs, start=k == 0, stop=k == NK - 1)
                    last.then_inc(pv, 1)
                    pe.wait_ge(orr, b + 1)
                    pe.wait_ge(otd, b + 1)
                    for q in range(2):
                        last = nc.tensor.transpose(PS[:, 7, q * P:(q + 1) * P], ol[:, q * P:(q + 1) * P], c.ident[:])
                    last.then_inc(otr, 1)
            pe.wait_ge(otd, NB + 1)
            for h in range(MLA_H):
                for q in range(2):
                    last = nc.tensor.matmul(PS[:, 0, h * 64:(h + 1) * 64], olT[:, q, h, :], M.wuv[:, q, h * 64:(h + 1) * 64],
                                            start=q == 0, stop=q == 1, skip_group_check=True)
            last.then_inc(uv, 1)

        @block.scalar
        def _(act):
            with act.Fori(0, HALF) as i:
                for s in range(2):
                    b = 2 * i + s
                    act.wait_ge(nms, b + 1)
                    nc.scalar.activation(Pb[:], PS[:, 0:3, :].rearrange("p b n -> p (b n)")[:, 0:NK * P], ACT.Exp, bias=nm[:],
                                         scale=MLA_SCALE, accum_out=rs[:]).then_inc(ex, 1)
                    act.wait_ge(tr, b + 1)
                    nc.scalar.activation(PTs[:, 4:NK, :], PS[:, 4:6, :].rearrange("p b n -> p (b n)")[:, 0:(NK - 4) * P]
                                         .rearrange("p (b n) -> p b n", n=P), ACT.Copy).then_inc(pt, 1)
                    act.wait_ge(otr, b + 1)
                    for q in range(2):
                        last = nc.scalar.activation(olT[:, q, :, bass.ds(b * ST, ST)],
                                                    PS[:, 7, q * P:(q + 1) * P].rearrange("p (h t) -> p h t", h=MLA_H), ACT.Copy)
                    last.then_inc(otd, 1)

        @block.vector
        def _(dve):
            link = Chain(dve, dch)
            nc.vector.memset(qpb[96:97], 1.0)
            dve.wait_ge(ol_, 16)
            with link.loop(HALF, 8) as i:
                for s in range(2):
                    b = 2 * i + s
                    nc.vector.tensor_copy(M.KT[96:97, TP * P:], M.KT[96:97, bass.ds(b * P, P)])
                    for q in range(2):
                        nc.vector.tensor_copy(qb[:, s, q, :].rearrange("p (h t) -> p h t", h=MLA_H), M.qabs[:, q, :, bass.ds(b * ST, ST)])
                    nc.vector.tensor_copy(qpb[64:96, s, :].rearrange("p (h t) -> p h t", h=MLA_H),
                                          M.qpe[64:96, :, bass.ds(b * ST, ST)]).then_inc(qd, 1)
                    dve.wait_ge(sc, b + 2)
                    link(softmax_max(nc, dve, link, mx[:], nm[:], PS[:, 0:3, :].rearrange("p b n -> p (b n)")[:, 0:NK * P], MLA_SCALE))
                    dve.sem_inc(nms, 1)
                    dve.wait_ge(tr, b + 1)
                    nc.vector.tensor_copy(PTs[:, 0:4, :], PS[:, 3, :].rearrange("p (b n) -> p b n", n=P)).then_inc(pt, 1)
                    link(nc.vector.reciprocal(ri[:], rs[:]))
                    dve.wait_ge(pv, b + 2)
                    link(nc.vector.tensor_scalar(ol[:], PS[:, 6, 0:256], ri[:], None, ALU.mult))
                    dve.sem_inc(orr, 1)
            dve.wait_ge(uv, 1)
            nc.vector.tensor_copy(c.XM[:, TP, 0:512], PS[:, 0, :])


def phase_linear(c, ret, G=None):
    nc, A, PS = c.nc, c.A, c.PS
    tag = "ret" if ret else "gla"
    DK = P if ret else 64
    HH = 2 if ret else 1
    W = 2 * DK + 2 * P
    w = Split(c, tag + "w", KD, W, lambda i, k: one(A["w_" + tag], i)[k] if not isinstance(i, int) else A["w_" + tag][i, k])
    qk = c.sb(tag + "_qk", [P, 3, 2 * DK])
    vz = c.sb(tag + "_v", [P, 4, HH * P])

    def values(t):
        return vz[:, t % 4, :].rearrange("p (b d) -> p b d", d=64)[:, 0::3, :] if ret else vz[:, t % 4, :]

    sg = c.sb(tag + "_gate", [P, NT, P])
    QK = c.sb(tag + "_qkT", [DK, 3, 2, P])
    PT = c.sb(tag + "_pT", [P, 2, HH, P])
    S = c.sb(tag + "_state", [DK, 3, P])
    tS = c.sb(tag + "_kv", [DK, P])
    os_ = c.sb(tag + "_o", [P, NT, P])
    S0 = c.sb(tag + "_s0", [DK, NB, P])
    SN = c.sb(tag + "_s1", [DK, NB, P])
    Qm = c.sb(tag + "_qTm", [DK, NB, P])
    vm = c.sb(tag + "_vm", [P, NB, P])
    squares = c.sb(tag + "_squares", [P, NT * P])
    st = c.sb(tag + "_stat", [P, NT * HH])
    nrm = c.sb(tag + "_normw", [P, 512])
    if ret:
        rC = c.sb("ret_cos", [P, NT, HD])
        rS = c.sb("ret_sin", [P, NT, HD])
        rp = c.sb("ret_pow", [P, 2, 4 * 4])
        rG = c.sb("ret_decay", [P, 4, 2, P])
        ta = c.sb("ret_ta", [P, 4, HD])
        tb = c.sb("ret_tb", [P, 4, HD])
    else:
        Sc = c.sb("gla_sc", [DK, 2, P])
    names = ("consts", "projected", "qk_ready", "vg_ready", "transposed", "qkT_ready", "scored", "pT_ready", "kv_done", "state_ready",
             "pv_done", "o_ready", "stats", "rstd", "turn_done", "vm_ready", "s0_loaded", "stored", "s1_ready", "dve", "act", "qm_zero", "s0_free", "sc_ready")
    (cl, prj, qkr, vgr, tr, qkT, sc, ptr, kv, sr, pv, orr, sti, sto, td, vmr, s0l, outs, s1r, dch, ach, qz, s0f, scr) = (c.sem(f"{tag}_{s}") for s in names)
    TURNS = 4
    N_OUT = 4 if ret else 2
    tri = c.masks[:, c.at["TRI"]:c.at["TRI"] + P]
    tris = c.masks[:, c.at["TRIS"]:c.at["TRIS"] + P]

    with nc.Block() as block:
        @block.sync
        def _(sp):
            sp.dma_start(nrm[:], A[tag + "_norm"].partition_broadcast(P)).then_inc(cl, 16)
            if ret:
                sp.dma_start(rC[:], A["ret_cos"]).then_inc(cl, 16)
                sp.dma_start(rS[:], A["ret_sin"]).then_inc(cl, 16)
                sp.dma_start(rp[:], A["ret_pow"]).then_inc(cl, 16)
                sp.dma_start(rG[:], A["ret_decay"]).then_inc(cl, 16)
            with sp.Fori(0, TURNS) as i:
                w.load(sp, i)
            sp.wait_ge(outs, 16 * N_OUT * TURNS + 1)

        @block.gpsimd
        def _(pool):
            for started in (prj, td, s0f, qkT, ptr, orr, outs):
                pool.sem_inc(started, 1)
            nc.gpsimd.memset(S0[:], 0.0)
            nc.gpsimd.memset(vz[:], 0.0)
            nc.gpsimd.memset(Qm[:], 0.0).then_inc(qz, 1)
            w.free_slots(pool)
            with pool.Fori(0, TURNS) as i:
                w.make_lo(pool, nc.gpsimd, 0, i)
                pool.wait_ge(vgr, 9 * i + 9)
                for b in range(NB):
                    dst = vm[:, b, :].rearrange("p (h d) -> p h d", h=2) if ret else vm[:, b, :]
                    own = c.masks[:, c.at["OWN8"] + b:c.at["OWN8"] + b + 1]
                    own = own.unsqueeze(2).broadcast_to([P, 2, 64]) if ret else own.broadcast_to([P, P])
                    last = nc.gpsimd.tensor_tensor(dst, values(TP), own, ALU.mult)
                last.then_inc(vmr, 1)

        @block.tensor
        def _(pe):
            with pe.Fori(0, TURNS) as i:
                def transposes(t):
                    pe.wait_ge(qkr, 9 * i + t + 1)
                    pe.wait_ge(qkT, 9 * i + t + 1)
                    for q in range(HH):
                        last = nc.tensor.transpose(PS[:, 2, q * P:(q + 1) * P], qk[:, t % 3, q * P:(q + 1) * P], c.ident[:])
                    last.then_inc(tr, 1)

                def scores(t):
                    pe.wait_ge(qkT, 9 * i + t + 2)
                    pe.wait_ge(ptr, 9 * i + t + 1)
                    for h in range(HH):
                        r = slice(64 * h, 64 * h + 64)
                        last = nc.tensor.matmul(PS[:, 3 + h, 0:P], QK[r, t % 3, 1, :], QK[r, t % 3, 0, :], start=True, stop=True)
                    last.then_inc(sc, 1)
                    pe.wait_ge(vgr, 9 * i + t + 1)
                    kt = qk[:, t % 3, DK:2 * DK]
                    if t < TP:
                        pe.wait_ge(sr, 9 * i + t + 1 if t else 9 * i + 1)
                        nc.tensor.matmul(PS[0:DK, 6, 0:P], kt, values(t), start=True, stop=True).then_inc(kv, 1)
                    else:
                        pe.wait_ge(vmr, i + 1)
                        pe.wait_ge(sr, 9 * i + 9)
                        for g in range(2):
                            last = nc.tensor.matmul(PS[0:DK, 6 + g, :], kt, vm[:, 4 * g:4 * g + 4, :].rearrange("p b v -> p (b v)"),
                                                    start=True, stop=True)
                        last.then_inc(kv, 1)

                def outputs(t):
                    pe.wait_ge(ptr, 9 * i + t + 2)
                    pe.wait_ge(orr, 9 * i + t + 1)
                    if t < TP:
                        if ret:
                            nc.tensor.matmul(PS[:, 5, 0:P], QK[:, t % 3, 0, :], S[:, t % 3, :], start=True, stop=False)
                        else:
                            pe.wait_ge(scr, 8 * i + t + 1)
                            nc.tensor.matmul(PS[:, 5, 0:P], QK[:, t % 3, 0, :], Sc[:, t % 2, :], start=True, stop=False)
                    else:
                        pe.wait_ge(s0l, 16 * HH * (i + 1))
                        for b in range(NB):
                            nc.tensor.matmul(PS[:, 5, 0:P], Qm[:, b, :], S0[:, b, :], start=b == 0, stop=False)
                    for h in range(HH):
                        last = nc.tensor.matmul(PS[:, 5, 0:P], PT[:, t % 2, h, :], vz[:, t % 4, h * P:(h + 1) * P],
                                                start=False, stop=h == HH - 1)
                    last.then_inc(pv, 1)

                for s in range(NT + 3):
                    if s < NT:
                        if s >= 2:
                            pe.wait_ge(qkr, 9 * i + s - 1)
                            pe.wait_ge(vgr, 9 * i + s - 1)
                        project_tile(c, pe, w, s, PS[:, s % 2, 0:W], slice(0, W), i).then_inc(prj, 1)
                    if 0 <= s - 1 < NT:
                        transposes(s - 1)
                    if 0 <= s - 2 < NT:
                        scores(s - 2)
                    if 0 <= s - 3 < NT:
                        outputs(s - 3)

        @block.scalar
        def _(act):
            act.wait_ge(qz, 1)
            with act.Fori(0, TURNS) as i:
                act.wait_ge(prj, 9 * i + 1)
                w.make_hi(act, i)
                act.wait_ge(s0f, i + 1)
                if ret:
                    for h in range(2):
                        act.dma_start(S0[64 * h:64 * h + 64, :, 64 * h:64 * h + 64],
                                      A["state_ret"][:, bass.ds(2 * i + h, 1)].squeeze(1).rearrange("b k v -> k b v")).then_inc(s0l, 16)
                else:
                    act.dma_start(S0[:], A["state_gla"][:, bass.ds(i, 1)].squeeze(1).rearrange("b k v -> k b v")).then_inc(s0l, 16)
                act.wait_ge(td, i + 1)
                for s in range(NT + 3):
                    if s < NT:
                        act.wait_ge(prj, 9 * i + s + 2)
                        src = PS[:, s % 2, 2 * DK:2 * DK + P]
                        nc.scalar.activation(values(s), src.rearrange("p (h d) -> p h d", h=2) if ret else src, ACT.Copy)
                        nc.scalar.activation(sg[:, s, :], PS[:, s % 2, 2 * DK + P:W], ACT.Silu).then_inc(vgr, 1)
                    if 0 <= s - 1 < NT:
                        t = s - 1
                        act.wait_ge(tr, 9 * i + t + 1)
                        if t == TP:
                            nc.scalar.activation(Qm[:].rearrange("p b (c t) -> p (b c) t", t=ST)[:, 0::NB + 1, :],
                                                 PS[0:DK, 2, 0:P].rearrange("p (b t) -> p b t", t=ST), ACT.Copy)
                        if ret:
                            nc.scalar.activation(QK[:, t % 3], PS[:, 2, 0:2 * P].rearrange("p (q n) -> p q n", q=2), ACT.Copy).then_inc(qkT, 1)
                        else:
                            nc.scalar.activation(QK[:, t % 3, 0, :], PS[0:64, 2, 0:P], ACT.Copy)
                            nc.scalar.activation(QK[:, t % 3, 1, :], PS[64:128, 2, 0:P], ACT.Copy).then_inc(qkT, 1)
                    if 0 <= s - 3 < NT:
                        t = s - 3
                        act.wait_ge(pv, 9 * i + t + 1)
                        nc.scalar.activation(os_[:, t, :], PS[:, 5, 0:P], ACT.Copy).then_inc(orr, 1)
                act.wait_ge(sti, i + 1)
                nc.scalar.activation(st[:], st[:], ACT.Ln).then_inc(ach, 1)
                act.wait_ge(ach, i + 1)
                nc.scalar.activation(st[:], st[:], ACT.Exp, scale=-0.5).then_inc(sto, 1)
                act.wait_ge(sr, 9 * i + 9)
                if ret:
                    for h in range(2):
                        act.dma_start(one(A["o_ret_p"], 2 * i + h), S[64 * h:64 * h + 64, TP % 3, 64 * h:64 * h + 64]).then_inc(outs, 16)
                else:
                    act.dma_start(one(A["o_gla_p"], i), S[:, TP % 3, :]).then_inc(outs, 16)
                act.wait_ge(s1r, i + 1)
                if ret:
                    for h in range(2):
                        act.dma_start(A["o_ret_s"][:, bass.ds(2 * i + h, 1)].squeeze(1).rearrange("b k v -> k b v"),
                                      SN[64 * h:64 * h + 64, :, 64 * h:64 * h + 64]).then_inc(outs, 16)
                else:
                    act.dma_start(A["o_gla_s"][:, bass.ds(i, 1)].squeeze(1).rearrange("b k v -> k b v"), SN[:]).then_inc(outs, 16)

        @block.vector
        def _(dve):
            link = Chain(dve, dch)
            dve.wait_ge(cl, 80 if ret else 16)
            with link.loop(TURNS, 55 if ret else 42) as i:
                w.make_lo(dve, nc.vector, 1, i)
                hs = lambda ap: ap.unsqueeze(1).broadcast_to([P, 4, ap.shape[-1]])

                def rotate(t):
                    dve.wait_ge(vgr, 9 * i + t + 1)
                    if ret:
                        src = PS[:, t % 2, 0:256].rearrange("p (h d) -> p h d", h=4)
                        nc.vector.tensor_tensor(ta[:], src, hs(rC[:, t, :]), ALU.mult)
                        nc.vector.tensor_tensor(tb[:, :, 0:32], src[:, :, 32:64], hs(rS[:, t, 0:32]), ALU.mult)
                        link(nc.vector.tensor_tensor(tb[:, :, 32:64], src[:, :, 0:32], hs(rS[:, t, 32:64]), ALU.mult))
                        link(nc.vector.tensor_tensor(ta[:], ta[:], tb[:], ALU.add))
                        pw = rp[:, t // TP, bass.ds(4 * i, 4)].unsqueeze(2).broadcast_to([P, 4, HD])
                        link(nc.vector.tensor_tensor(qk[:, t % 3, :].rearrange("p (h d) -> p h d", h=4), ta[:], pw, ALU.mult))
                        dve.sem_inc(qkr, 1)
                    else:
                        nc.vector.scalar_tensor_tensor(qk[:, t % 3, 0:64], PS[:, t % 2, 0:64], 64 ** -0.5,
                                                       G.eB[:, t, bass.ds(64 * i, 64)], ALU.mult, ALU.mult)
                        link(nc.vector.tensor_tensor(qk[:, t % 3, 64:128], PS[:, t % 2, 64:128],
                                                G.eN[:, t, bass.ds(64 * i, 64)], ALU.mult))
                        dve.sem_inc(qkr, 1)

                def scale_state(t):
                    link(nc.vector.tensor_scalar(Sc[:, t % 2, :], S[:, t % 3, :], G.dec[:, bass.ds(i * 24 + 3 * t, 1)], None, ALU.mult))
                    dve.sem_inc(scr, 1)

                def mask_and_state(t):
                    dve.wait_ge(sc, 9 * i + t + 1)
                    m = (tris if t == TP else tri).unsqueeze(1).broadcast_to([P, HH, P])
                    nc.vector.tensor_tensor(PT[:, t % 2], PS[:, 3:3 + HH, 0:P], m, ALU.mult).then_inc(ptr, 1)
                    if t < TP:
                        if not ret:
                            scale_state(t)
                        dve.wait_ge(kv, 9 * i + t + 1)
                        if ret:
                            link(nc.vector.tensor_tensor(tS[:], PS[:, 6, 0:P], S[:, t % 3, :], ALU.add))
                            link(nc.vector.tensor_tensor(S[:, (t + 1) % 3, :], tS[:], rG[:, bass.ds(i, 1), 0, :].squeeze(1), ALU.mult))
                        else:
                            link(nc.vector.tensor_scalar(tS[:], PS[0:DK, 6, 0:P], G.dec[:, bass.ds(i * 24 + 3 * t + 1, 1)], None, ALU.mult))
                            link(nc.vector.scalar_tensor_tensor(S[:, (t + 1) % 3, :], S[:, t % 3, :], G.dec[:, bass.ds(i * 24 + 3 * t + 2, 1)],
                                                                tS[:], ALU.mult, ALU.add))
                        dve.sem_inc(sr, 1)
                    else:
                        dve.wait_ge(kv, 9 * i + 9)
                        dve.wait_ge(s0l, 16 * HH * (i + 1))
                        dve.wait_ge(outs, 16 * N_OUT * i + 1)
                        link(nc.vector.tensor_tensor(SN[:].rearrange("p b v -> p (b v)"), PS[0:DK, 6:8, :].rearrange("p b n -> p (b n)"),
                                                     S0[:].rearrange("p b v -> p (b v)"), ALU.add))
                        if ret:
                            g = rG[:, bass.ds(i, 1), 1, :].broadcast_to([P, NB, P])
                        else:
                            g = G.decs[:, bass.ds(NB * i, NB)].unsqueeze(2).broadcast_to([DK, NB, P])
                        link(nc.vector.tensor_tensor(SN[:], SN[:], g, ALU.mult))
                        dve.sem_inc(s1r, 1)
                        dve.wait_ge(pv, 9 * i + 9)
                        dve.sem_inc(s0f, 1)

                dve.wait_ge(outs, 16 * N_OUT * i + 1)
                link(nc.vector.memset(S[:, 0, :], 0.0))
                dve.sem_inc(sr, 1)
                for s in range(NT + 2):
                    if s < NT:
                        rotate(s)
                    if s >= 2:
                        mask_and_state(s - 2)
                dve.wait_ge(orr, 9 * i + 9 + 1)
                o = os_[:].rearrange("p t (h d) -> p (t h) d", h=HH)
                dv = P // HH
                stb = st[:].unsqueeze(2).broadcast_to([P, NT * HH, dv])
                if ret:
                    link(nc.vector.tensor_reduce(out=st[:], in_=o, axis=AX.X, op=ALU.add))
                    link(nc.vector.tensor_scalar(st[:], st[:], -1.0 / dv, None, ALU.mult))
                    link(nc.vector.tensor_tensor(o, o, stb, ALU.add))
                big = squares[:].rearrange("p (h d) -> p h d", d=dv)
                link(nc.vector.tensor_tensor(big, o, o, ALU.mult))
                link(nc.vector.tensor_reduce(out=st[:], in_=big, axis=AX.X, op=ALU.add))
                link(nc.vector.tensor_scalar(st[:], st[:], 1.0 / dv, NORM_EPS, ALU.mult, ALU.add))
                dve.sem_inc(sti, 1)
                dve.wait_ge(sto, i + 1)
                link(nc.vector.tensor_tensor(o, o, stb, ALU.mult))
                nw = nrm[:, bass.ds(P * i, P)].unsqueeze(1).broadcast_to([P, NT, P])
                link(nc.vector.tensor_tensor(os_[:], os_[:], nw, ALU.mult))
                base = 512 if ret else 0
                link(nc.vector.tensor_tensor(c.XM[:, :, bass.ds(P * i + base, P)], os_[:], sg[:], ALU.mult))
                dve.sem_inc(td, 1)


def phase_gates(c, G):
    nc, A, PS = c.nc, c.A, c.PS
    w = Split(c, "wga", KD, P, lambda i, k: A["w_ga"][k])
    gaT = c.sb("gaT", [32, TOK])
    wa = c.sb("w_a2", [17, 256])
    g = c.sb("g_log", [P, NT, 256])
    a = c.sb("g_abs", [P, NT, 256])
    names = ("consts", "projected", "gaT_ready", "ones", "logits", "gates", "sums", "sum_read", "steps", "dve", "act", "x")
    (cl, prj, gr, on, lg, gt, su, srd, dn, dch, ach, _) = (c.sem("gate_" + s) for s in names)
    with nc.Block() as block:
        @block.sync
        def _(sp):
            sp.dma_start(wa[:], A["w_a2b"]).then_inc(cl, 16)
            w.load(sp)
            sp.wait_ge(cl, 16)

        @block.gpsimd
        def _(pool):
            w.free_slots(pool)
            w.make_lo(pool, nc.gpsimd, 0)
            nc.gpsimd.memset(gaT[:], 1.0).then_inc(on, 1)

        @block.tensor
        def _(pe):
            for q in range(3):
                xs = slice(q * GRP, (q + 1) * GRP)
                for k in range(KD):
                    w.wait(pe, k)
                    last = mm3(nc, PS[:, q, 0:GRP], (w.hi[:, k, :], w.lo[:, k, :]), (c.xTh[:, k, xs], c.xTl[:, k, xs]), k == 0, k == KD - 1)
                last.then_inc(prj, 1)
            pe.wait_ge(cl, 16)
            pe.wait_ge(gr, 3)
            for t in range(NT):
                last = nc.tensor.matmul(PS[:, 3 + t // 2, (t % 2) * 256:(t % 2) * 256 + 256], gaT[0:17, t * P:(t + 1) * P], wa[:],
                                        start=True, stop=True, skip_group_check=True)
            last.then_inc(lg, 1)
            pe.wait_ge(gt, 1)
            for t in range(NT):
                o = c.at["TRIS"] if t == TP else c.at["MID"]
                last = nc.tensor.matmul(PS[:, 3 + t // 2, (t % 2) * 256:(t % 2) * 256 + 256], c.masks[:, o:o + P], g[:, t, :],
                                        start=True, stop=True, skip_group_check=True)
            for h in range(4):
                for t in range(TP):
                    nc.tensor.matmul(PS[0:64, 0, 24 * h + 3 * t:24 * h + 3 * t + 3], g[:, t, 64 * h:64 * h + 64],
                                     c.masks[:, c.at["SEL"]:c.at["SEL"] + 3], start=True, stop=True, skip_group_check=True)
                last = nc.tensor.matmul(PS[0:64, 1, NB * h:NB * h + NB], g[:, TP, 64 * h:64 * h + 64], c.masks[:, c.at["OWN8"]:c.at["OWN8"] + NB],
                                        start=True, stop=True, skip_group_check=True)
            last.then_inc(su, 1)

        lgp = PS[:, 3:8, :].rearrange("p b n -> p (b n)")[:, 0:NT * 256]

        @block.scalar
        def _(act):
            w.make_hi(act)
            act.wait_ge(on, 1)
            for q in range(3):
                act.wait_ge(prj, q + 1)
                nc.scalar.activation(gaT[0:16, q * GRP:(q + 1) * GRP], PS[0:16, q, 0:GRP], ACT.Copy).then_inc(gr, 1)
            act.wait_ge(lg, 1)
            af = a[:].rearrange("p t n -> p (t n)")
            nc.scalar.activation(af, lgp, ACT.Abs).then_inc(ach, 1)
            act.wait_ge(ach, 1)
            nc.scalar.activation(af, af, ACT.Exp, scale=-1.0).then_inc(ach, 1)
            act.wait_ge(ach, 2)
            nc.scalar.activation(af, af, ACT.Ln, bias=1.0).then_inc(ach, 1)
            act.wait_ge(su, 1)
            eB = G.eB[:].rearrange("p t n -> p (t n)")
            eN = G.eN[:].rearrange("p t n -> p (t n)")
            act.wait_ge(dn, 1)
            nc.scalar.activation(eB, a[:].rearrange("p t n -> p (t n)"), ACT.Exp)
            nc.scalar.activation(eN, a[:].rearrange("p t n -> p (t n)"), ACT.Exp, scale=-1.0)
            nc.scalar.activation(G.dec[:], PS[0:64, 0, 0:96], ACT.Exp)
            nc.scalar.activation(G.decs[:], PS[0:64, 1, 0:32], ACT.Exp)

        @block.vector
        def _(dve):
            link = Chain(dve, dch)
            w.make_lo(dve, nc.vector, 1)
            dve.wait_ge(lg, 1)
            dve.wait_ge(ach, 1)
            gf = g[:].rearrange("p t n -> p (t n)")
            af = a[:].rearrange("p t n -> p (t n)")
            link(nc.vector.tensor_scalar(gf, lgp, 0.0, None, ALU.min))
            dve.wait_ge(ach, 3)
            link(nc.vector.tensor_tensor(gf, gf, af, ALU.subtract))
            nc.vector.tensor_scalar(gf, gf, 1.0 / 16.0, None, ALU.mult).then_inc(gt, 1)
            dve.wait_ge(su, 1)
            nc.vector.tensor_scalar(af, lgp, -80.0, 80.0, ALU.max, ALU.min).then_inc(dn, 1)


def phase_swa(c):
    nc, A, PS = c.nc, c.A, c.PS
    W = 384
    NK = NB + 1
    w = Split(c, "swaw", KD, W, lambda i, k: one(A["w_swa"], i)[k])
    qk = c.sb("swa_qk", [P, 4, 320])
    kro = c.sb("swa_kro", [P, 2, HD])
    v = c.sb("swa_v", [P, NT, HD])
    KT = c.sb("swa_kT", [HD, TOK])
    QT = c.sb("swa_qT", [HD, 4, 4, P])
    Pb = c.sb("swa_p", [P, NK * P])
    PTs = c.sb("swa_pT", [P, NK, P])
    cK = c.sb("swa_cachekT", [HD, NB * P])
    cV = c.sb("swa_cachev", [P, NB, HD])
    rows = c.sb("swa_rows", list(A["swa_rows"].shape))
    tab = c.sb("swa_tab", [P, NT, 32])
    ta = c.sb("swa_ta", [P, 5, 16])
    tb = c.sb("swa_tb", [P, 5, 16])
    sk = c.sb("swa_sink", [P, 8])
    mx, nm, rs, es, ri = (c.sb("swa_" + s, [P, 4]) for s in ("mx", "nm", "rs", "es", "ri"))
    names = ("consts", "cache_loaded", "projected", "qk_ready", "v_ready", "transposed", "qkT_ready", "scored", "max_ready", "exp_done",
             "p_transposed", "pT_ready", "pv_done", "o_written", "stored", "dve", "copied", "kout")
    (cl, chl, prj, qkr, vr, tr, qkT, sc, nms, ex, ptt, ptr, pv, ow, outs, dch, cpy, ko) = (c.sem("swa_" + s) for s in names)
    SCALE = HD ** -0.5
    UN = TP + 4
    with nc.Block() as block:
        @block.sync
        def _(sp):
            sp.dma_start(tab[:], A["swa_tab"]).then_inc(cl, 16)
            sp.dma_start(sk[:], A["sinks"].partition_broadcast(P)).then_inc(cl, 16)
            sp.dma_start(rows[:], A["swa_rows"]).then_inc(cl, 16)
            for n in ("k", "v"):
                sp.dma_start(A[f"o_swa_{n}_old"], A[f"c_swa_{n}_old"]).then_inc(cpy, 16)
            with sp.Fori(0, 2) as i:
                w.load(sp, i)
                sp.wait_ge(pv, UN * i + 1)
                sp.dma_start(cK[:], one(A["c_swa_kT"], i)).then_inc(chl, 16)
                sp.dma_start(cV[:], one(A["c_swa_v"], i)).then_inc(chl, 16)
            sp.wait_ge(outs, 64 + 1)
            sp.wait_ge(cpy, 32)

        @block.gpsimd
        def _(pool):
            for started in (pv, qkT, ow, prj, outs):
                pool.sem_inc(started, 1)
            w.free_slots(pool)
            with pool.Fori(0, 2) as i:
                w.make_lo(pool, nc.gpsimd, 0, i)

        @block.tensor
        def _(pe):
            pe.wait_ge(cl, 48)
            with pe.Fori(0, 2) as i:
                def transposes(t):
                    pe.wait_ge(qkr, 9 * i + t + 1)
                    pe.wait_ge(qkT, 9 * i + t + 1)
                    for q in range(2):
                        nc.tensor.transpose(PS[:, 2, q * P:(q + 1) * P], qk[:, t % 4, q * P:(q + 1) * P], c.ident[:])
                    last = nc.tensor.transpose(PS[0:64, 3, 0:P], qk[:, t % 4, 256:320], c.ident[:])
                    last.then_inc(tr, 1)

                def scores(t):
                    pe.wait_ge(qkT, 9 * i + t + 2)
                    if t < TP:
                        for h in range(4):
                            o = PS[:, 4 + h // 2, (h % 2) * 256:(h % 2) * 256 + 256]
                            if t == 0:
                                nc.tensor.matmul(o[:, 0:P], QT[:, 0, h, :], KT[:, 0:P], start=True, stop=False, skip_group_check=True)
                                last = nc.tensor.matmul(o[:, 0:P], rows[0:2, c.at["WROW"]:c.at["WROW"] + P],
                                                        rows[0:2, c.at["WNEG"] + P:c.at["WNEG"] + 2 * P], start=False, stop=True, skip_group_check=True)
                            else:
                                nc.tensor.matmul(o, QT[:, t % 4, h, :], KT[:, (t - 1) * P:(t + 1) * P], start=True, stop=False, skip_group_check=True)
                                last = nc.tensor.matmul(o, rows[0:2, c.at["WROW"]:c.at["WROW"] + P], rows[0:2, c.at["WNEG"]:c.at["WNEG"] + 2 * P],
                                                        start=False, stop=True, skip_group_check=True)
                        last.then_inc(sc, 1)

                def values(t):
                    pe.wait_ge(ex, UN * i + t + 1)
                    pe.wait_ge(ow, UN * i + t + 1)
                    nb = 1 if t == 0 else 2
                    for h in range(4):
                        for b in range(nb):
                            n = h * nb + b
                            last = nc.tensor.transpose(PS[:, 6 + n // 4, (n % 4) * P:(n % 4 + 1) * P], Pb[:, h * 256 + b * P:h * 256 + b * P + P], c.ident[:])
                    last.then_inc(ptt, 1)
                    pe.wait_ge(ptr, UN * i + t + 1)
                    pe.wait_ge(vr, 9 * i + t + 1)
                    for h in range(4):
                        for b in range(nb):
                            last = nc.tensor.matmul(PS[:, 6, h * 64:(h + 1) * 64], PTs[:, h * nb + b, :], v[:, t - nb + 1 + b, :],
                                                    start=b == 0, stop=b == nb - 1, skip_group_check=True)
                    last.then_inc(pv, 1)

                def sample_head(h):
                    n = TP + h
                    pe.wait_ge(chl, 32 * i + 32)
                    pe.wait_ge(ow, UN * i + n + 1)
                    for g in range(3):
                        wd = P if g == 2 else 512
                        rhs = KT[:, TP * P:] if g == 2 else cK[:, g * 512:(g + 1) * 512]
                        nc.tensor.matmul(PS[:, g, 0:wd], QT[:, TP % 4, h, :], rhs, start=True, stop=False)
                        last = nc.tensor.matmul(PS[:, g, 0:wd], rows[0:NB, c.at["STR"]:c.at["STR"] + P],
                                                rows[0:NB, c.at["SNEG"] + 512 * g:c.at["SNEG"] + 512 * g + wd], start=False, stop=True)
                    last.then_inc(sc, 1)
                    pe.wait_ge(ex, UN * i + n + 1)
                    for k in range(NK):
                        last = nc.tensor.transpose(PS[:, 3 + k // 4, (k % 4) * P:(k % 4 + 1) * P], Pb[:, k * P:(k + 1) * P], c.ident[:])
                    last.then_inc(ptt, 1)
                    pe.wait_ge(ptr, UN * i + n + 1)
                    for k in range(NK):
                        rhs = v[:, TP, :] if k == NK - 1 else cV[:, k, :]
                        last = nc.tensor.matmul(PS[:, 6, 0:64], PTs[:, k, :], rhs, start=k == 0, stop=k == NK - 1)
                    last.then_inc(pv, 1)

                pe.wait_ge(ow, UN * i + 1)
                for s in range(NT + 3):
                    if s < NT:
                        if s >= 2:
                            pe.wait_ge(qkr, 9 * i + s - 1)
                            pe.wait_ge(vr, 9 * i + s - 1)
                        project_tile(c, pe, w, s, PS[:, s % 2, 0:W], slice(0, W), i).then_inc(prj, 1)
                    if 0 <= s - 1 < NT:
                        transposes(s - 1)
                    if 0 <= s - 3 < TP:
                        values(s - 3)
                    if 0 <= s - 2 < NT:
                        scores(s - 2)
                for h in range(4):
                    sample_head(h)

        @block.scalar
        def _(act):
            with act.Fori(0, 2) as i:
                act.wait_ge(prj, 9 * i + 1)
                w.make_hi(act, i)
                act.wait_ge(outs, 32 * i + 1)

                def softmax(n, heads, cols):
                    act.wait_ge(nms, UN * i + n + 1)
                    if heads == 4:
                        for h in range(4):
                            nc.scalar.activation(Pb[:, h * 256:h * 256 + cols], PS[:, 4 + h // 2, (h % 2) * 256:(h % 2) * 256 + cols], ACT.Exp,
                                                 bias=nm[:, h:h + 1], scale=SCALE, accum_out=rs[:, h:h + 1])
                        last = nc.scalar.activation(es[:], es[:], ACT.Exp)
                    else:
                        h = n - TP
                        nc.scalar.activation(Pb[:], PS[:, 0:3, :].rearrange("p b n -> p (b n)")[:, 0:NK * P], ACT.Exp, bias=nm[:, h:h + 1],
                                             scale=SCALE, accum_out=rs[:, h:h + 1])
                        last = nc.scalar.activation(es[:, h:h + 1], es[:, h:h + 1], ACT.Exp)
                    last.then_inc(ex, 1)

                for s in range(NT + 3):
                    if s < NT:
                        act.wait_ge(prj, 9 * i + s + 2)
                        nc.scalar.activation(v[:, s, :], PS[:, s % 2, 320:384], ACT.Copy).then_inc(vr, 1)
                    if 0 <= s - 1 < NT:
                        t = s - 1
                        act.wait_ge(tr, 9 * i + t + 1)
                        for odd in range(2):
                            nc.scalar.activation(QT[:, t % 4, odd::2, :], PS[64 * odd:64 * odd + 64, 2, 0:2 * P].rearrange("p (q n) -> p q n", q=2), ACT.Copy)
                        nc.scalar.activation(KT[:, t * P:(t + 1) * P], PS[0:64, 3, 0:P], ACT.Copy).then_inc(qkT, 1)
                    if 0 <= s - 2 < TP:
                        softmax(s - 2, 4, P if s == 2 else 256)
                act.wait_ge(ko, 2 * i + 2)
                act.wait_ge(vr, 9 * i + 9)
                act.dma_start(one(A["o_swa_k"], i), kro[:]).then_inc(outs, 16)
                act.dma_start(one(A["o_swa_v"], i), v[:, TP - 1:NT, :]).then_inc(outs, 16)
                for h in range(4):
                    softmax(TP + h, 1, 0)

        @block.vector
        def _(dve):
            link = Chain(dve, dch)
            dve.wait_ge(cl, 48)
            with link.loop(2, 104) as i:
                w.make_lo(dve, nc.vector, 1, i)
                hs = lambda ap: ap.unsqueeze(1).broadcast_to([P, 5, ap.shape[-1]])

                def rotate(t):
                    dve.wait_ge(vr, 9 * i + t + 1)
                    src = PS[:, t % 2, 0:320].rearrange("p (h d) -> p h d", h=5)
                    dst = qk[:, t % 4, :].rearrange("p (h d) -> p h d", h=5)
                    nc.vector.tensor_copy(dst[:, :, 16:64], src[:, :, 16:64])
                    nc.vector.tensor_tensor(ta[:], src[:, :, 0:16], hs(tab[:, t, 0:16]), ALU.mult)
                    nc.vector.tensor_tensor(tb[:, :, 0:8], src[:, :, 8:16], hs(tab[:, t, 16:24]), ALU.mult)
                    link(nc.vector.tensor_tensor(tb[:, :, 8:16], src[:, :, 0:8], hs(tab[:, t, 24:32]), ALU.mult))
                    link(nc.vector.tensor_tensor(dst[:, :, 0:16], ta[:], tb[:], ALU.add))
                    dve.sem_inc(qkr, 1)
                    if t >= TP - 1:
                        if t == TP - 1:
                            dve.wait_ge(outs, 32 * i + 1)
                        link(nc.vector.tensor_copy(kro[:, t - TP + 1, :], qk[:, t % 4, 256:320]))
                        dve.sem_inc(ko, 1)

                def attend(n):
                    dve.wait_ge(sc, UN * i + n + 1)
                    if n < TP:
                        cols, hh = (P if n == 0 else 256), slice(0, 4)
                        src = PS[:, 4:6, :].rearrange("p b (h n) -> p (b h) n", h=2)[:, :, 0:cols]
                        sks = sk[:, bass.ds(4 * i, 4)]
                    else:
                        h = n - TP
                        hh = slice(h, h + 1)
                        src = PS[:, 0:3, :].rearrange("p b n -> p (b n)")[:, 0:NK * P]
                        sks = sk[:, bass.ds(4 * i + h, 1)]
                    link(nc.vector.tensor_reduce(out=mx[:, hh], in_=src, axis=AX.X, op=ALU.max))
                    link(nc.vector.tensor_scalar(mx[:, hh], mx[:, hh], SCALE, None, ALU.mult))
                    link(nc.vector.tensor_tensor(mx[:, hh], mx[:, hh], sks, ALU.max))
                    nc.vector.tensor_tensor(es[:, hh], sks, mx[:, hh], ALU.subtract)
                    link(nc.vector.tensor_scalar(nm[:, hh], mx[:, hh], -1.0, None, ALU.mult))
                    dve.sem_inc(nms, 1)

                def finish(n):
                    dve.wait_ge(ptt, UN * i + n + 1)
                    if n < TP:
                        hh = slice(0, 4)
                        nb = 4 if n == 0 else 8
                    else:
                        hh = slice(n - TP, n - TP + 1)
                        nb = NK
                    first = 6 if n < TP else 3
                    nc.vector.tensor_copy(PTs[:, 0:nb, :], PS[:, first:8 if n < TP else 6, :].rearrange("p b n -> p (b n)")[:, 0:nb * P]
                                          .rearrange("p (b n) -> p b n", n=P)).then_inc(ptr, 1)
                    link(nc.vector.tensor_tensor(rs[:, hh], rs[:, hh], es[:, hh], ALU.add))
                    link(nc.vector.reciprocal(ri[:, hh], rs[:, hh]))
                    dve.wait_ge(pv, UN * i + n + 2)
                    if n < TP:
                        link(nc.vector.tensor_tensor(c.XM[:, n, bass.ds(256 * i + 512, 256)].rearrange("p (h d) -> p h d", h=4),
                                                     PS[:, 6, 0:256].rearrange("p (h d) -> p h d", h=4),
                                                     ri[:].unsqueeze(2).broadcast_to([P, 4, 64]), ALU.mult))
                    else:
                        h = n - TP
                        link(nc.vector.tensor_scalar(c.XM[:, TP, bass.ds(256 * i + 512 + 64 * h, 64)], PS[:, 6, 0:64], ri[:, hh], None, ALU.mult))
                    dve.sem_inc(ow, 1)

                for s in range(NT + 2):
                    if s < NT:
                        rotate(s)
                    if 3 <= s:
                        finish(s - 3)
                    if 2 <= s < TP + 2:
                        attend(s - 2)
                for n in range(TP, TP + 4):
                    attend(n)
                    finish(n)


class Norm:

    def __init__(self, c, tag, gain, bias):
        self.c, self.nc, self.gain, self.bias = c, c.nc, gain, bias
        self.sts = c.sb(tag + "sts", [P, 2, 6])
        self.mv = c.sb(tag + "mv", [P, 2, 2])
        self.nb = c.sb(tag + "negmean", [P, 2])
        self.eps = c.sb(tag + "eps", [P, 1])
        names = ("eps", "stats", "std", "rstd", "normed", "scaled", "x_ready")
        self.ep, self.var, self.std, self.rs, self.nd, self.gd, self.xr = (c.sem(tag + s) for s in names)

    def set_eps(self, dve):
        self.nc.vector.memset(self.eps[:], LN_EPS).then_inc(self.ep, 1)

    def stats(self, dve, link, t):
        x, nc = self.c.XM[:, t, :], self.nc
        for q in range(2):
            last = nc.vector.bn_stats(self.sts[:, q, :], x[:, q * 512:(q + 1) * 512])
        link(last)
        link(nc.vector.bn_aggr(self.mv[:, t % 2, :], self.sts[:].rearrange("p a b -> p (a b)")))
        dve.sem_inc(self.var, 1)

    def root(self, act, t):
        if t == 0:
            act.wait_ge(self.ep, 1)
        act.wait_ge(self.var, t + 1)
        v = self.mv[:, t % 2, 1:2]
        self.nc.scalar.activation(v, v, ACT.Sqrt, bias=self.eps[:]).then_inc(self.std, 1)

    def rstd(self, dve, link, t):
        nc, mv = self.nc, self.mv
        dve.wait_ge(self.std, t + 1)
        link(nc.vector.reciprocal(mv[:, t % 2, 1:2], mv[:, t % 2, 1:2]))
        link(nc.vector.tensor_scalar(self.nb[:, t % 2:t % 2 + 1], mv[:, t % 2, 0:1], mv[:, t % 2, 1:2], -1.0, ALU.mult, ALU.mult))
        dve.sem_inc(self.rs, 1)

    def normalise(self, act, t):
        act.wait_ge(self.rs, t + 1)
        x = self.c.XM[:, t, :]
        self.nc.scalar.activation(x, x, ACT.Identity, bias=self.nb[:, t % 2:t % 2 + 1], scale=self.mv[:, t % 2, 1:2]).then_inc(self.nd, 1)

    def scale(self, pool, t):
        pool.wait_ge(self.nd, t + 1)
        x = self.c.XM[:, t, :]
        self.nc.gpsimd.tensor_tensor(x, x, self.gain, ALU.mult).then_inc(self.gd, 1)

    def add_bias(self, dve, t):
        dve.wait_ge(self.gd, t + 1)
        x = self.c.XM[:, t, :]
        self.nc.vector.tensor_tensor(x, x, self.bias, ALU.add).then_inc(self.xr, 1)


def phase_mix_out(c, layer):
    nc, A, PS = c.nc, c.A, c.PS
    tag = f"mo{layer}_"
    w = Split(c, tag + "w", KD, D, lambda i, k: A[f"w_out{layer}"][k])
    xin, gb = w.raw[:, 0:2, :], w.raw[:, 2:4, :]
    norm = Norm(c, tag, gb[:, 0, :], gb[:, 1, :])
    mTh = c.sb(tag + "mTh", [P, 2, KD, P], R)
    mTl = c.sb(tag + "mTl", [P, 2, KD, P], R)
    names = ("gb_loaded", "x_loaded", "x_used", "mix_transposed", "mixT_hi", "mixT_ready", "projected",
             "x_transposed", "xT_hi", "xT_ready", "dve")
    (gl, xl, xu, mt, mh, ml, om, xt, xh, xlo, dch) = (c.sem(tag + s) for s in names)
    xl = (xl, c.sem(tag + "x_loaded1"))
    resid = A["x_in"] if layer == 0 else A["x1"]
    flat = lambda a, b: PS[:, a:b, :].rearrange("p b n -> p (b n)")
    with nc.Block() as block:
        @block.sync
        def _(sp):
            w.load(sp)
            for t in range(NT):
                if t < 2:
                    sp.wait_ge(w.w_split[t], 6)
                if t >= 2:
                    sp.wait_ge(xu, t - 1)
                sp.dma_start(xin[:, t % 2, :], resid[t]).then_inc(xl[t % 2], 16)
                if t == 1:
                    for half, n in enumerate(("ln_mix_g", "ln_mix_b")):
                        w.wait(sp, 6 + half)
                        sp.dma_start(gb[:, half, :], A[n][layer].partition_broadcast(P)).then_inc(gl, 16)

        @block.gpsimd
        def _(pool):
            w.free_slots(pool)
            w.make_lo(pool, nc.gpsimd, 0)
            pool.wait_ge(gl, 32)
            for t in range(NT):
                norm.scale(pool, t)

        @block.tensor
        def _(pe):
            def mix_t(t):
                if t:
                    pe.wait_ge(ml, t)
                for k in range(KD):
                    last = nc.tensor.transpose(PS[:, k // 4, (k % 4) * P:(k % 4 + 1) * P], c.XM[:, t, k * P:(k + 1) * P], c.ident[:])
                last.then_inc(mt, 1)

            def x_t(t):
                pe.wait_ge(norm.xr, t + 1)
                if t:
                    pe.wait_ge(xlo, t)
                for k in range(KD):
                    last = nc.tensor.transpose(PS[:, 6 + k // 4, (k % 4) * P:(k % 4 + 1) * P], c.XM[:, t, k * P:(k + 1) * P], c.ident[:])
                last.then_inc(xt, 1)

            mix_t(0)
            for t in range(NT):
                pe.wait_ge(ml, t + 1)
                if t >= 2:
                    pe.wait_ge(xu, t - 1)
                for half in range(2):
                    cs = slice(half * 512, half * 512 + 512)
                    for k in range(KD):
                        if t == 0:
                            w.wait(pe, k)
                        last = mm3(nc, PS[:, 2 + 2 * (t % 2) + half, :], (mTh[:, t % 2, k, :], mTl[:, t % 2, k, :]), (w.hi[:, k, cs], w.lo[:, k, cs]),
                                   k == 0, k == KD - 1)
                    if half == 0 and t + 1 < NT:
                        mix_t(t + 1)
                last.then_inc(om, 1)
                if t >= 2:
                    x_t(t - 2)
            x_t(NT - 2)
            x_t(NT - 1)

        @block.scalar
        def _(act):
            def mix_hi(t):
                act.wait_ge(mt, t + 1)
                if t >= 2:
                    act.wait_ge(om, t - 1)
                nc.scalar.activation(mTh[:, t % 2].rearrange("p k n -> p (k n)"), flat(0, 2), ACT.Copy).then_inc(mh, 1)

            def x_hi(t):
                act.wait_ge(xt, t + 1)
                nc.scalar.activation(c.xTh[:, :, t * P:(t + 1) * P], flat(6, 8).rearrange("p (k n) -> p k n", n=P), ACT.Copy).then_inc(xh, 1)
                nc.scalar.activation(c.XM[:, t, :], c.XM[:, t, :], ACT.Copy, scale=ALPHA)

            mix_hi(0)
            w.make_hi(act)
            for t in range(NT):
                if t + 1 < NT:
                    mix_hi(t + 1)
                if t >= 3:
                    x_hi(t - 3)
                norm.root(act, t)
                norm.normalise(act, t)
            for t in range(NT - 3, NT):
                x_hi(t)

        @block.vector
        def _(dve):
            link = Chain(dve, dch)
            norm.set_eps(dve)

            def mix_lo(t):
                dve.wait_ge(mh, t + 1)
                nc.vector.tensor_tensor(mTl[:, t % 2].rearrange("p k n -> p (k n)"), flat(0, 2), mTh[:, t % 2].rearrange("p k n -> p (k n)").bitcast(F),
                                        ALU.subtract).then_inc(ml, 1)

            def x_lo(t):
                dve.wait_ge(xh, t + 1)
                ts = slice(t * P, (t + 1) * P)
                nc.vector.tensor_tensor(c.xTl[:, :, ts], flat(6, 8).rearrange("p (k n) -> p k n", n=P), c.xTh[:, :, ts].bitcast(F),
                                        ALU.subtract).then_inc(xlo, 1)

            mix_lo(0)
            w.make_lo(dve, nc.vector, 1)
            for t in range(NT):
                if t + 1 < NT:
                    mix_lo(t + 1)
                if t >= 3:
                    x_lo(t - 3)
                if t >= 1:
                    norm.add_bias(dve, t - 1)
                dve.wait_ge(om, t + 1)
                dve.wait_ge(xl[t % 2], 16 * (t // 2 + 1))
                link(nc.vector.scalar_tensor_tensor(c.XM[:, t, :], xin[:, t % 2, :], ALPHA, flat(2 + 2 * (t % 2), 4 + 2 * (t % 2)), ALU.mult, ALU.add))
                dve.sem_inc(xu, 1)
                norm.stats(dve, link, t)
                norm.rstd(dve, link, t)
            x_lo(NT - 3)
            norm.add_bias(dve, NT - 1)
            x_lo(NT - 2)
            x_lo(NT - 1)


def phase_ffn(c, layer):
    nc, A, PS = c.nc, c.A, c.PS
    tag = f"ff{layer}_"
    wraw = c.sb(tag + "wraw", [P, 2, D])
    whi = c.sb(tag + "whi", [P, 2, KD, P], R)
    wlo = c.sb(tag + "wlo", [P, 2, KD, P], R)
    draw = c.sb(tag + "draw", [P, D])
    dhi = c.sb(tag + "dhi", [P, 2, D], R)
    dlo = c.sb(tag + "dlo", [P, 2, D], R)
    u = c.sb(tag + "u", [P, 2, UW])
    cv = c.sb(tag + "c", [P, 2, UW])
    gf = c.sb(tag + "g", [P, TOK])
    gh = c.sb(tag + "gh", [P, 2, TOK], R)
    gl = c.sb(tag + "gl", [P, 2, TOK], R)
    cw = c.sb(tag + "cw", [P, 2, NJ * 4])
    old = c.sb(tag + "old", [P, 2, NJ * 16])
    new = c.sb(tag + "new", [P, 2, NJ * 18])
    names = ("consts", "a_loaded", "b_loaded", "d_loaded", "up_hi", "up_split", "d_hi", "d_split", "up_done", "u_ready", "c0_ready", "conv_done",
             "halo_ready", "state_kept", "silu_done", "g_ready", "g_hi", "g_split", "down_done", "added", "stored", "dve")
    (cl, la, lb, ld, uh, us, dh, dsp, um, ur, c0, cvd, hl, sk, si, gr, ghd, gs, dm, ad, outs, dch) = (c.sem(tag + s) for s in names)
    lab = (la, lb)

    def ge(eng, sem, v):
        if not isinstance(v, int) or v > 0:
            eng.wait_ge(sem, v)

    def chunks(eng, step):
        step(0, 0)
        with eng.Fori(0, (NJ - 2) // 2) as r:
            step(2 * r + 1, 1)
            step(2 * r + 2, 0)
        step(NJ - 1, 1)

    def pick(ap, j):
        return ap[j] if isinstance(j, int) else one(ap, j)

    def cols(j, a, n):
        return slice(j * a, j * a + n) if isinstance(j, int) else bass.ds(j * a, n)

    with nc.Block() as block:
        @block.sync
        def _(sp):
            def step(j, par):
                for ab in range(2):
                    ge(sp, us, 2 * j + ab - 1)
                    sp.dma_start(wraw[:, ab, :], pick(A["w_up"][layer, :, ab], j)).then_inc(lab[ab], 16)
                if isinstance(j, int) and j == 0:
                    sp.dma_start(cw[:], A["conv_w"][layer]).then_inc(cl, 16)
                    sp.dma_start(old[:], A["conv_old"][layer]).then_inc(cl, 16)
                ge(sp, dsp, j)
                sp.dma_start(draw[:], pick(A["w_down"][layer], j)).then_inc(ld, 16)

            chunks(sp, step)
            sp.wait_ge(sk, 2 * NJ)
            sp.dma_start(A["o_conv"][layer], new[:]).then_inc(outs, 16)
            sp.wait_ge(outs, 16)

        @block.gpsimd
        def _(pool):
            for started in (ad, dm):
                pool.sem_inc(started, 1)
            def split_up(j, ab):
                pool.wait_ge(uh, 2 * j + ab + 1)
                nc.gpsimd.tensor_tensor(wlo[:, ab].rearrange("p k n -> p (k n)"), wraw[:, ab, :],
                                        whi[:, ab].rearrange("p k n -> p (k n)").bitcast(F), ALU.subtract).then_inc(us, 1)

            def step(j, par):
                for ab in range(2):
                    ge(pool, cvd, 2 * j + ab - 1)
                    halo = u[:, ab, US:].rearrange("p (b t) -> p b t", b=NB)[:, :, 0:2]
                    nc.gpsimd.tensor_copy(halo, old[:, ab, cols(j, 16, 16)].rearrange("p (b t) -> p b t", b=NB)).then_inc(hl, 1)
                pool.wait_ge(dh, j + 1)
                nc.gpsimd.tensor_tensor(dlo[:, par, :], draw[:], dhi[:, par, :].bitcast(F), ALU.subtract).then_inc(dsp, 1)
                for ab in range(2):
                    pool.wait_ge(ur, 6 * j + 3 * ab + 3)
                    keep = new[:, ab, cols(j, 18, 18)]
                    nc.gpsimd.tensor_copy(keep[:, 0:2], u[:, ab, SEQ:SEQ + 2])
                    nc.gpsimd.tensor_copy(keep[:, 2:18].rearrange("p (b t) -> p b t", b=NB),
                                          u[:, ab, US:].rearrange("p (b t) -> p b t", b=NB)[:, :, ST:ST + 2]).then_inc(sk, 1)
                    if not isinstance(j, int) or j + 1 < NJ:
                        split_up(j + 1, ab)
                pool.wait_ge(ghd, j + 1)
                nc.gpsimd.tensor_tensor(gl[:, par, :], gf[:], gh[:, par, :].bitcast(F), ALU.subtract).then_inc(gs, 1)

            nc.gpsimd.memset(u[:, :, 0:2], 0.0)
            split_up(0, 0)
            split_up(0, 1)
            pool.wait_ge(cl, 32)
            chunks(pool, step)

        @block.tensor
        def _(pe):
            def up(j):
                for ab in range(2):
                    pe.wait_ge(us, 2 * j + ab + 1)
                    for q in range(3):
                        ge(pe, ur, 6 * j + 3 * ab + q - 2)
                        xs = slice(q * GRP, (q + 1) * GRP)
                        for k in range(KD):
                            last = mm3(nc, PS[:, q, 0:GRP], (whi[:, ab, k, :], wlo[:, ab, k, :]), (c.xTh[:, k, xs], c.xTl[:, k, xs]),
                                       k == 0, k == KD - 1)
                        last.then_inc(um, 1)

            def down(j, par):
                pe.wait_ge(gs, j + 1)
                pe.wait_ge(dsp, j + 1)
                for t in range(NT):
                    ge(pe, ad, 9 * j + max(t - 1, 0) + 1)
                    a = tuple(g[:, par, t * P:(t + 1) * P] for g in (gh, gl))
                    for half in range(2):
                        cs = slice(half * 512, half * 512 + 512)
                        last = mm3(nc, PS[:, 3 + 2 * ((t + par) % 2) + half, :], a, (dhi[:, par, cs], dlo[:, par, cs]), True, True)
                    last.then_inc(dm, 1)

            up(0)
            with pe.Fori(0, (NJ - 2) // 2) as r:
                up(2 * r + 1)
                down(2 * r, 0)
                up(2 * r + 2)
                down(2 * r + 1, 1)
            up(NJ - 1)
            down(NJ - 2, 0)
            down(NJ - 1, 1)

        @block.scalar
        def _(act):
            def hi_up(j, ab):
                act.wait_ge(lab[ab], 16 * j + 16)
                ge(act, um, 6 * j + 3 * ab - 3)
                nc.scalar.activation(whi[:, ab].rearrange("p k n -> p (k n)"), wraw[:, ab, :], ACT.Copy).then_inc(uh, 1)

            def step(j, par):
                act.wait_ge(ld, 16 * j + 16)
                ge(act, dm, 9 * j - 9 + 1)
                nc.scalar.activation(dhi[:, par, :], draw[:], ACT.Copy).then_inc(dh, 1)
                for ab in range(2):
                    ge(act, cvd, 2 * j + ab - 1)
                    ge(act, sk, 2 * j + ab - 1)
                    for q in range(3):
                        act.wait_ge(um, 6 * j + 3 * ab + q + 1)
                        if q < 2:
                            last = nc.scalar.activation(u[:, ab, 2 + q * GRP:2 + (q + 1) * GRP], PS[:, q, 0:GRP], ACT.Copy)
                        else:
                            nc.scalar.activation(u[:, ab, 2 + 2 * GRP:US], PS[:, 2, 0:SEQ - 2 * GRP], ACT.Copy)
                            last = nc.scalar.activation(u[:, ab, US:].rearrange("p (b t) -> p b t", b=NB)[:, :, 2:],
                                                        PS[:, 2, SEQ - 2 * GRP:GRP].rearrange("p (b t) -> p b t", b=NB), ACT.Copy)
                        last.then_inc(ur, 1)
                    act.wait_ge(ur, 6 * j + 3 * ab + 3)
                    act.wait_ge(hl, 2 * j + ab + 1)
                    ge(act, gr, j)
                    nc.scalar.activation(cv[:, ab, 2:], u[:, ab, 2:], ACT.Identity, bias=cw[:, ab, cols4(j, 3)], scale=cw[:, ab, cols4(j, 2)]).then_inc(c0, 1)
                    if not isinstance(j, int) or j + 1 < NJ:
                        hi_up(j + 1, ab)
                act.wait_ge(cvd, 2 * j + 1)
                nc.scalar.activation(cv[:, 0, 2:], cv[:, 0, 2:], ACT.Silu).then_inc(si, 1)
                act.wait_ge(gr, j + 1)
                nc.scalar.activation(gh[:, par, :], gf[:], ACT.Copy).then_inc(ghd, 1)

            def cols4(j, n):
                return slice(4 * j + n, 4 * j + n + 1) if isinstance(j, int) else bass.ds(4 * j + n, 1)

            hi_up(0, 0)
            hi_up(0, 1)
            act.wait_ge(cl, 32)
            chunks(act, step)

        @block.vector
        def _(dve):
            def col4(j, n):
                return slice(4 * j + n, 4 * j + n + 1) if isinstance(j, int) else bass.ds(4 * j + n, 1)

            def conv(j, ab):
                dve.wait_ge(c0, 2 * j + ab + 1)
                nc.vector.scalar_tensor_tensor(cv[:, ab, 2:], u[:, ab, 1:UW - 1], cw[:, ab, col4(j, 1)], cv[:, ab, 2:], ALU.mult, ALU.add).then_inc(dch, 1)
                dve.wait_ge(dch, 2 * j + ab + 1)
                nc.vector.scalar_tensor_tensor(cv[:, ab, 2:], u[:, ab, 0:UW - 2], cw[:, ab, col4(j, 0)], cv[:, ab, 2:], ALU.mult, ALU.add).then_inc(cvd, 1)

            def gate(j):
                dve.wait_ge(si, j + 1)
                dve.wait_ge(cvd, 2 * j + 2)
                ge(dve, gs, j)
                nc.vector.tensor_tensor(gf[:, 0:SEQ], cv[:, 0, 2:US], cv[:, 1, 2:US], ALU.mult)
                new_a, new_b = (cv[:, ab, US:].rearrange("p (b t) -> p b t", b=NB)[:, :, 2:] for ab in range(2))
                nc.vector.tensor_tensor(gf[:, SEQ:].rearrange("p (b t) -> p b t", b=NB), new_a, new_b, ALU.mult).then_inc(gr, 1)

            def add(j, t, par):
                dve.wait_ge(dm, 9 * j + t + 2)
                b = 3 + 2 * ((t + par) % 2)
                nc.vector.tensor_tensor(c.XM[:, t, :], c.XM[:, t, :], PS[:, b:b + 2, :].rearrange("p b n -> p (b n)"), ALU.add).then_inc(ad, 1)

            def step(j, par):
                conv(j, 0)
                for t in range(NT):
                    add(j - 1, t, 1 - par)
                conv(j, 1)
                gate(j)

            conv(0, 0)
            conv(0, 1)
            gate(0)
            with dve.Fori(0, (NJ - 2) // 2) as r:
                step(2 * r + 1, 1)
                step(2 * r + 2, 0)
            conv(NJ - 1, 0)
            conv(NJ - 1, 1)
            add(NJ - 2, 0, 0)
            add(NJ - 2, 1, 0)
            gate(NJ - 1)
            for t in range(2, NT):
                add(NJ - 2, t, 0)
            for t in range(NT):
                add(NJ - 1, t, 1)


def phase_ffn_norm(c, layer):
    nc, A, PS = c.nc, c.A, c.PS
    tag = f"fn{layer}_"
    gb = c.sb(tag + "gb", [P, 2, D])
    norm = Norm(c, tag, gb[:, 0, :], gb[:, 1, :])
    names = ("consts", "x_transposed", "xT_hi", "xT_ready", "dve", "stored")
    (cl, xt, xh, xlo, dch, outs) = (c.sem(tag + s) for s in names)
    dst = A["x1"] if layer == 0 else A["o_y"]
    flat = lambda a, b: PS[:, a:b, :].rearrange("p b n -> p (b n)")
    more = layer == 0
    with nc.Block() as block:
        @block.sync
        def _(sp):
            sp.dma_start(gb[:, 0, :], A["ln_ffn_g"][layer].partition_broadcast(P)).then_inc(cl, 16)
            sp.dma_start(gb[:, 1, :], A["ln_ffn_b"][layer].partition_broadcast(P)).then_inc(cl, 16)
            for t in range(NT):
                sp.wait_ge(norm.xr, t + 1)
                sp.dma_start(dst[t], c.XM[:, t, :]).then_inc(outs, 16)
            sp.wait_ge(outs, 16 * NT)

        @block.gpsimd
        def _(pool):
            pool.wait_ge(cl, 32)
            for t in range(NT):
                norm.scale(pool, t)

        if more:
            @block.tensor
            def _(pe):
                for t in range(NT):
                    pe.wait_ge(norm.xr, t + 1)
                    if t >= 2:
                        pe.wait_ge(xlo, t - 1)
                    for k in range(KD):
                        last = nc.tensor.transpose(PS[:, 2 * (t % 2) + k // 4, (k % 4) * P:(k % 4 + 1) * P], c.XM[:, t, k * P:(k + 1) * P], c.ident[:])
                    last.then_inc(xt, 1)

        @block.scalar
        def _(act):
            for t in range(NT + 3):
                if more and t >= 3:
                    s = t - 3
                    act.wait_ge(xt, s + 1)
                    nc.scalar.activation(c.xTh[:, :, s * P:(s + 1) * P], flat(2 * (s % 2), 2 * (s % 2) + 2).rearrange("p (k n) -> p k n", n=P),
                                         ACT.Copy).then_inc(xh, 1)
                if t < NT:
                    norm.root(act, t)
                    norm.normalise(act, t)

        @block.vector
        def _(dve):
            link = Chain(dve, dch)
            norm.set_eps(dve)
            for t in range(NT + 3):
                if t < NT:
                    norm.stats(dve, link, t)
                if 2 <= t < NT + 2:
                    norm.add_bias(dve, t - 2)
                if more and t >= 3:
                    s = t - 3
                    ts = slice(s * P, (s + 1) * P)
                    dve.wait_ge(xh, s + 1)
                    nc.vector.tensor_tensor(c.xTl[:, :, ts], flat(2 * (s % 2), 2 * (s % 2) + 2).rearrange("p (k n) -> p k n", n=P),
                                            c.xTh[:, :, ts].bitcast(F), ALU.subtract).then_inc(xlo, 1)
                if t < NT:
                    norm.rstd(dve, link, t)


class Bag:
    pass


def build(nc, A, mask_columns, stages=99):
    c = Ctx(nc, A)
    c.at = mask_columns
    c.xTh = c.sb("xT_hi", [P, KD, TOK], R)
    c.xTl = c.sb("xT_lo", [P, KD, TOK], R)
    c.XM = c.sb("x_or_mix", [P, NT, D])
    c.ident = c.sb("ident", [P, P])
    c.PS = nc.alloc_psum_tensor("psum", [P, 8, 512], F)
    c.masks = c.sb("masks", list(A["masks"].shape))

    def run(phase, *args):
        with nc.cleanup_on_exit():
            phase(c, *args)

    run(phase_start)
    with nc.cleanup_on_exit():
        M = Bag()
        M.latT = c.sb("latT", [P, 4, TOK])
        M.KT = c.sb("mla_kT", [P, TOK])
        M.T = c.sb("mla_tab", [P, TOK])
        M.ckv_s = c.sb("ckv_new", [P, 256])
        run(phase_latents, M)
        M.rows = c.sb("mla_rows", list(A["mla_rows"].shape))
        M.qabs = c.sb("q_abs", [P, 2, MLA_H, P])
        M.qpe = c.sb("q_pe", [P, MLA_H, P])
        M.wuv = c.sb("w_uv", [P, 2, 512])
        if stages > 1:
            run(phase_mla_prompt, M)
        if stages > 2:
            run(phase_mla_sample, M)
    if stages > 3:
        run(phase_linear, True)
    if stages > 4:
        run(phase_mix_out, 0)
    if stages > 5:
        run(phase_ffn, 0)
    if stages > 6:
        run(phase_ffn_norm, 0)
    if stages > 7:
        with nc.cleanup_on_exit():
            G = Bag()
            G.eB = c.sb("gla_eB", [P, NT, 256])
            G.eN = c.sb("gla_eN", [P, NT, 256])
            G.dec = c.sb("gla_dec", [64, 96])
            G.decs = c.sb("gla_decs", [64, 32])
            run(phase_gates, G)
            run(phase_linear, False, G)
    if stages > 8:
        run(phase_swa)
    if stages > 9:
        run(phase_mix_out, 1)
        run(phase_ffn, 1)
        run(phase_ffn_norm, 1)



def rope_angles(pos, dim, theta):
    inv = (np.float32(1.0) / (np.float32(theta) ** (np.arange(0, dim, 2, dtype=np.float32) / np.float32(dim)))).astype(np.float32)
    ang = pos.astype(np.float32)[:, None] * inv[None, :]
    return np.cos(ang).astype(np.float32), np.sin(ang).astype(np.float32)


def constants():
    tok = np.arange(P)
    pos = np.concatenate([np.arange(SEQ), np.tile(PAST + np.arange(ST), NB)])
    stream = tok // ST
    out = {"ident": np.eye(P, dtype=np.float32)}
    m = {}
    tri = (tok[:, None] <= tok[None, :]).astype(np.float32)
    m["TRI"] = tri
    m["TRIS"] = tri * (stream[:, None] == stream[None, :])
    m["MID"] = tri - (tok[:, None] < 64).astype(np.float32)
    m["OWN8"] = (stream[:, None] == np.arange(NB)[None, :]).astype(np.float32)
    m["SEL"] = np.stack([tok < 64, tok >= 64, tok >= 0], 1).astype(np.float32)
    m["ROW"] = (tok[None, :] < 64) * np.ones((1, 1), np.float32)
    m["NEG"] = NEG * (tok[None, :] >= 64)
    m["OWN"] = NEG * (stream[None, :] != np.arange(NB)[:, None]).reshape(1, NB * P)
    m["WROW"] = np.stack([tok < 64, tok >= 64]).astype(np.float32)
    k2 = np.arange(2 * P)
    m["WNEG"] = NEG * np.stack([k2 >= 192, k2 < 64]).astype(np.float32)
    m["STR"] = (np.arange(NB)[:, None] == stream[None, :]).astype(np.float32)
    key_stream = np.concatenate([np.repeat(np.arange(NB), P), stream])
    m["SNEG"] = NEG * (np.arange(NB)[:, None] != key_stream[None, :])
    groups = {"masks": ("TRI", "TRIS", "MID", "OWN8", "SEL"), "mla_rows": ("ROW", "NEG"), "mla_own": ("OWN",),
              "swa_rows": ("WROW", "WNEG", "STR", "SNEG")}
    cols = {}
    for group, members in groups.items():
        rows = max(m[n].shape[0] for n in members)
        parts, at = [], 0
        for n in members:
            full = np.zeros((rows, m[n].shape[1]), np.float32)
            full[:m[n].shape[0]] = m[n]
            cols[n] = at
            at += full.shape[1]
            parts.append(full)
        out[group] = np.concatenate(parts, 1)
    cos, sin = rope_angles(pos, ROPE, 500000.0)
    out["kpe_tab"] = np.concatenate([cos.T, cos.T, -sin.T, sin.T], 0)
    tiles = lambda a: np.ascontiguousarray(a.reshape(NT, P, -1).transpose(1, 0, 2))
    cos, sin = rope_angles(pos, HD, 10000.0)
    out["ret_cos"] = tiles(np.concatenate([cos, cos], 1))
    out["ret_sin"] = tiles(np.concatenate([-sin, sin], 1))
    cos, sin = rope_angles(pos, HD // 4, 500000.0)
    out["swa_tab"] = tiles(np.concatenate([cos, cos, -sin, sin], 1))
    gamma = np.log(1.0 - 2.0 ** (-5.0 - np.arange(8)))
    pw = np.zeros((P, 2, 4, 4))
    gd = np.zeros((P, 4, 2, P))
    for kind, (local, length) in enumerate(((tok, P), (tok % ST, ST))):
        for pair in range(4):
            for h in range(2):
                g = gamma[2 * pair + h]
                pw[:, kind, pair, h] = np.exp(g * (local + 1))
                pw[:, kind, pair, 2 + h] = np.exp(-g * (local + 1)) * HD ** -0.5
                gd[64 * h:64 * h + 64, pair, kind, 64 * h:64 * h + 64] = np.exp(g * length)
    out["ret_pow"] = pw.reshape(P, 2, 16)
    out["ret_decay"] = gd
    return {n: np.ascontiguousarray(a, dtype=np.float32) for n, a in out.items()}, cols


def layout(x):
    f = {n: np.asarray(a) for n, a in x.items()}
    out = {}
    xs = np.concatenate([f["x_prompt"].reshape(SEQ, D), f["x_sample"].reshape(P, D)])
    out["x_in"] = xs.reshape(NT, P, D)
    out["xT"] = xs.T.reshape(KD, P, TOK).transpose(1, 0, 2).reshape(P, KD * TOK)
    we = f["w_in_even"][0]
    kpe = we[:, 512:544]
    sw = np.concatenate([kpe[:, 16:], kpe[:, :16]], 1)
    out["w_lat"] = np.concatenate([we[:, :512], kpe, sw, kpe, sw], 1).reshape(KD, P, 640)
    parts = [we[:, 544 + 512 * n:544 + 512 * (n + 1)].reshape(D, 4, P) for n in range(4)]
    out["w_ret"] = np.stack(parts, 2).transpose(1, 0, 2, 3).reshape(4, KD, P, 512)
    uq = f["mla_w_uq"][0].reshape(2, P, MLA_H, 96)
    uq = np.concatenate([uq, uq[..., 80:96], uq[..., 64:80]], -1)
    out["w_uq"] = uq.transpose(2, 1, 0, 3)
    ukv = f["mla_w_ukv"][0].reshape(2, P, MLA_H, 128)
    out["w_uk"] = ukv[..., :64].transpose(2, 1, 0, 3)
    out["w_ukT"] = ukv[..., :64].transpose(2, 3, 0, 1).reshape(MLA_H, 64, 256)
    out["w_uv"] = ukv[..., 64:].transpose(1, 0, 2, 3).reshape(P, 2, 512)
    out["lat_norm"] = np.concatenate([f["mla_q_norm"][0], f["mla_kv_norm"][0]])
    ckv = f["cache_mla_ckv"][0]
    out["c_ckv"] = ckv.reshape(NB, PAST // P, P, 256).transpose(0, 2, 1, 3)
    out["c_ckvT"] = ckv.transpose(0, 2, 1).reshape(NB, 2, P, PAST).transpose(0, 2, 1, 3)
    out["c_kpeT"] = f["cache_mla_kpe"][0].transpose(0, 2, 1)
    out["state_ret"] = f["state_ret"][0]
    out["state_gla"] = f["state_gla"][0]
    out["ret_norm"] = f["ret_norm"][0]
    out["gla_norm"] = f["gla_norm"][0]
    out["w_out0"] = f["w_out_even"][0].reshape(KD, P, D)
    out["w_out1"] = f["w_out_odd"][0].reshape(KD, P, D)
    wo = f["w_in_odd"][0]
    q, k = (wo[:, 256 * n:256 * (n + 1)].reshape(D, 4, 64) for n in range(2))
    v, g = (wo[:, 512 * n:512 * (n + 1)].reshape(D, 4, P) for n in (1, 2))
    out["w_gla"] = np.concatenate([q, k, v, g], 2).transpose(1, 0, 2).reshape(4, KD, P, 384)
    out["w_ga"] = np.tile(wo[:, 1536:1552], (1, 8)).reshape(KD, P, P)
    out["w_a2b"] = np.concatenate([f["gla_w_a2"][0], f["gla_b_a"]], 0)
    q = wo[:, 1552:2064].reshape(D, 2, 256)
    k = wo[:, 2064:2192].reshape(D, 2, 64)
    v = wo[:, 2192:2320].reshape(D, 2, 64)
    out["w_swa"] = np.concatenate([q, k, v], 2).transpose(1, 0, 2).reshape(2, KD, P, 384)
    out["sinks"] = f["swa_sinks"][0]
    ck, cv = f["cache_swa_k"][0], f["cache_swa_v"][0]
    out["c_swa_kT"] = ck.transpose(2, 3, 0, 1).reshape(2, 64, NB * P)
    out["c_swa_v"] = cv.transpose(2, 1, 0, 3)
    out["c_swa_k_old"] = ck[:, ST:].reshape(NB, -1)
    out["c_swa_v_old"] = cv[:, ST:].reshape(NB, -1)
    up = f["ffn_w_up"].reshape(2, KD, P, 2, NJ, P)
    out["w_up"] = up.transpose(0, 4, 3, 2, 1, 5).reshape(2, NJ, 2, P, D)
    out["w_down"] = f["ffn_w_down"].reshape(2, NJ, P, D)
    cw = np.concatenate([f["ffn_conv_w"], f["ffn_conv_b"][:, None]], 1).reshape(2, 4, 2, NJ, P)
    out["conv_w"] = cw.transpose(0, 4, 2, 3, 1).reshape(2, P, 2, NJ * 4)
    old = f["state_ffn_conv"].reshape(2, NB * 2, 2, NJ, P)
    out["conv_old"] = old.transpose(0, 4, 2, 3, 1).reshape(2, P, 2, NJ * 16)
    for n in ("ln_mix_g", "ln_mix_b", "ln_ffn_g", "ln_ffn_b"):
        out[n] = f[n]
    return {n: np.ascontiguousarray(a) for n, a in out.items()}


OUTPUTS = {
    "o_y": (NT, P, D), "o_ckv_p": (SEQ, 256), "o_ckv_s": (P, 256), "o_kpe": (ROPE, TOK),
    "o_ret_p": (8, 64, 64), "o_ret_s": (NB, 8, 64, 64), "o_gla_p": (4, 64, P), "o_gla_s": (NB, 4, 64, P),
    "o_swa_k": (2, P, 2, HD), "o_swa_v": (2, P, 2, HD), "o_swa_k_old": (NB, 112 * 128), "o_swa_v_old": (NB, 112 * 128),
    "o_conv": (2, P, 2, NJ * 18),
}


def returned(o):
    y = o["o_y"].reshape(TOK, D)
    kpe = o["o_kpe"].T
    conv = o["o_conv"].reshape(2, P, 2, NJ, 18)
    conv = conv.transpose(0, 4, 2, 3, 1).reshape(2, 18, 2 * FF)
    kv = []
    for n in ("k", "v"):
        new = o["o_swa_" + n]
        kv.append(new[:, :, 0].transpose(1, 0, 2)[None, None])
        s = new[:, :, 1].transpose(1, 0, 2).reshape(NB, ST, 2, HD)
        kv.append(np.concatenate([o[f"o_swa_{n}_old"].reshape(NB, P - ST, 2, HD), s], 1)[None])
    kp, ks, vp, vs = kv
    c = np.ascontiguousarray
    return (c(y[:SEQ].reshape(1, SEQ, D)), c(y[SEQ:].reshape(NB, ST, D)), o["o_ckv_p"].reshape(1, 1, SEQ, 256),
            c(kpe[:SEQ]).reshape(1, 1, SEQ, ROPE), o["o_ret_p"][None, None], o["o_gla_p"][None, None], c(kp), c(vp),
            c(conv[:, :2]).reshape(2, 1, 2, 2 * FF), o["o_ckv_s"].reshape(1, NB, ST, 256), c(kpe[SEQ:]).reshape(1, NB, ST, ROPE),
            o["o_ret_s"][None], o["o_gla_s"][None], c(ks), c(vs), c(conv[:, 2:]).reshape(2, NB, 2, 2 * FF))


def kernel(**inputs):
    import concourse.bacc as bacc
    from concourse.bass_utils import run_bass_kernel_spmd as run

    nc = bacc.Bacc("TRN2", target_bir_lowering=False, num_devices=1)
    const, cols = constants()
    arrays = {"in_" + n: a for n, a in (layout(inputs) | const).items()}
    A = {n[3:]: nc.dram_tensor(n, a.shape, mybir.dt.from_np(a.dtype), kind="ExternalInput").ap() for n, a in arrays.items()}
    for n, shape in OUTPUTS.items():
        A[n] = nc.dram_tensor(n, shape, F, kind="ExternalOutput").ap()
    A["x1"] = nc.dram_tensor("x_between_layers", (NT, P, D), F, kind="Internal").ap()
    build(nc, A, cols)
    r = run(nc, [arrays], core_ids=[0])
    return returned({n: np.asarray(r.results[0][n]) for n in OUTPUTS})
```

```python
from contextlib import contextmanager

import numpy as np
import concourse.bass as bass
from concourse import mybir

F = mybir.dt.float32
R = mybir.dt.float32r
ACT = mybir.ActivationFunctionType
ALU = mybir.AluOpType
AX = mybir.AxisListType

P = 128
D = 1024
KD = D // P
SEQ = 1024
TP = SEQ // P
NT = TP + 1
TOK = NT * P
NB = 8
ST = 16
PAST = 1024
ALPHA = 4.0 ** 0.25
LN_EPS = 1e-5
NORM_EPS = 1e-6
NEG = -1e30
MLA_H, MLA_C, NOPE, ROPE = 8, 256, 64, 32
MLA_SCALE = (NOPE + ROPE) ** -0.5
HD = 64
FF = 2816
NJ = FF // P
GRP = 384
UW = 2 + SEQ + NB * (2 + ST)
US = 2 + SEQ


class Chain:

    def __init__(self, eng, sem):
        self.eng, self.sem, self.done, self.n, self.i, self.per = eng, sem, 0, 0, None, 0

    def __call__(self, ins):
        self.n += 1
        ins.then_inc(self.sem, 1)
        self.eng.wait_ge(self.sem, self.done + self.n + (0 if self.i is None else self.i * self.per))

    @contextmanager
    def loop(self, count, per):
        self.done, self.n, self.per = self.done + self.n, 0, per
        with self.eng.Fori(0, count) as i:
            self.i = i
            yield i
        assert self.n == per, (str(self.sem), "links in a turn:", self.n)
        self.done, self.n, self.i = self.done + count * per, 0, None


class Ctx:

    def __init__(self, nc, A):
        self.nc, self.A = nc, A

    def sb(self, name, shape, dt=F):
        return self.nc.alloc_sbuf_tensor(name, shape, dt)

    def sem(self, name):
        return self.nc.alloc_semaphore(name=name)


def one(ap, i):
    return ap[bass.ds(i, 1)].squeeze(0)



class Split:

    def __init__(self, c, name, n, width, src, ring=4):
        self.c, self.n, self.width, self.src, self.ring = c, n, width, src, ring
        self.raw = c.sb(name + "_raw", [P, ring, width])
        self.hi = c.sb(name + "_hi", [P, n, width], R)
        self.lo = c.sb(name + "_lo", [P, n, width], R)
        self.ld = [c.sem(f"{name}_loaded{s}") for s in range(ring)]
        self.w_hi = c.sem(name + "_hi_done")
        self.w_split = [c.sem(f"{name}_split_{e}") for e in ("pool", "dve")]

    def load(self, sp, i=0):
        for k in range(self.n):
            sp.wait_ge(self.w_split[k % 2], i * (self.n // 2) + k // 2 + 1)
            sp.dma_start(self.raw[:, k % self.ring, :], self.src(i, k)).then_inc(self.ld[k % self.ring], 16)

    def make_hi(self, act, i=0, ks=None):
        for k in ks or range(self.n):
            act.wait_ge(self.ld[k % self.ring], i * (self.n // self.ring) * 16 + (k // self.ring + 1) * 16)
            self.c.nc.scalar.activation(self.hi[:, k, :], self.raw[:, k % self.ring, :], ACT.Copy).then_inc(self.w_hi, 1)

    def free_slots(self, pool):
        for split in self.w_split:
            pool.sem_inc(split, self.ring // 2)

    def make_lo(self, eng, ops, half, i=0):
        for k in range(half, self.n, 2):
            eng.wait_ge(self.w_hi, i * self.n + k + 1)
            ops.tensor_tensor(self.lo[:, k, :], self.raw[:, k % self.ring, :],
                              self.hi[:, k, :].bitcast(F), ALU.subtract).then_inc(self.w_split[half], 1)

    def wait(self, pe, k, i=0):
        pe.wait_ge(self.w_split[k % 2], i * (self.n // 2) + k // 2 + 1 + self.ring // 2)


def mm3(nc, out, a, b, first, last):
    nc.tensor.matmul(out, a[0], b[0], start=first, stop=False)
    nc.tensor.matmul(out, a[0], b[1], start=False, stop=False)
    return nc.tensor.matmul(out, a[1], b[0], start=False, stop=last)


def project_tile(c, pe, w, t, out, cols, i=0):
    for k in range(KD):
        if t == 0:
            w.wait(pe, k, i)
        xs = slice(t * P, (t + 1) * P)
        last = mm3(c.nc, out, (c.xTh[:, k, xs], c.xTl[:, k, xs]), (w.hi[:, k, cols], w.lo[:, k, cols]),
                   k == 0, k == KD - 1)
    return last



def phase_start(c):
    nc, A = c.nc, c.A
    ld, hi, ms = c.sem("start_loaded"), c.sem("start_hi"), c.sem("start_done")
    raw = c.XM
    rawf = raw[:].rearrange("p t d -> p (t d)")
    hif = c.xTh[:].rearrange("p k t -> p (k t)")
    lof = c.xTl[:].rearrange("p k t -> p (k t)")
    with nc.Block() as block:
        @block.sync
        def _(sp):
            sp.dma_start(c.ident[:], A["ident"]).then_inc(ms, 16)
            sp.dma_start(c.masks[:], A["masks"]).then_inc(ms, 16)
            sp.dma_start(rawf, A["xT"]).then_inc(ld, 16)
            sp.wait_ge(ms, 32)

        @block.scalar
        def _(act):
            act.wait_ge(ld, 16)
            for k in range(KD):
                s = slice(k * TOK, (k + 1) * TOK)
                nc.scalar.activation(hif[:, s], rawf[:, s], ACT.Copy).then_inc(hi, 1)

        @block.vector
        def _(dve):
            for k in range(KD):
                dve.wait_ge(hi, k + 1)
                s = slice(k * TOK, (k + 1) * TOK)
                nc.vector.tensor_tensor(lof[:, s], rawf[:, s], hif[:, s].bitcast(F), ALU.subtract)


def phase_latents(c, M):
    nc, A, PS = c.nc, c.A, c.PS
    w = Split(c, "wlat", KD, 640, lambda i, k: A["w_lat"][k], ring=2)
    lat = c.sb("lat", [P, NT, 512])
    sq = c.sb("lat_sq", [P, 256])
    ss = c.sb("lat_ss", [P, NT * 2])
    nrm = c.sb("lat_norm", [P, 512])
    tmp = c.sb("kpe_tmp", [P, GRP])
    prj, ev, tr, tev, kp = (c.sem("lat_" + s) for s in ("projected", "evacuated", "transposed", "latT_ready", "kpe_projected"))
    rs_in, rs_out, nd, ld, outs, dch, ach = (c.sem("lat_" + s) for s in
                                       ("squares", "rstd", "normed", "consts", "stored", "dve", "act"))
    with nc.Block() as block:
        @block.sync
        def _(sp):
            w.load(sp)
            sp.dma_start(nrm[:], A["lat_norm"].partition_broadcast(P)).then_inc(ld, 16)
            sp.dma_start(M.T[64:128, :], A["kpe_tab"]).then_inc(ld, 16)
            sp.wait_ge(nd, 1)
            sp.dma_start(A["o_ckv_p"].rearrange("(t p) c -> p t c", p=P), lat[:, 0:TP, 256:512]).then_inc(outs, 16)
            sp.dma_start(A["o_ckv_s"], lat[:, TP, 256:512]).then_inc(outs, 16)
            sp.wait_ge(kp, 4)
            sp.dma_start(A["o_kpe"], M.KT[64:96, :]).then_inc(outs, 16)
            sp.wait_ge(outs, 48)

        @block.gpsimd
        def _(pool):
            w.free_slots(pool)
            w.make_lo(pool, nc.gpsimd, 0)

        @block.tensor
        def _(pe):
            for t in range(NT):
                if t >= 2:
                    pe.wait_ge(ev, t - 1)
                project_tile(c, pe, w, t, PS[:, t % 2, :], slice(0, 512)).then_inc(prj, 1)
            for g in range(3):
                for k in range(KD):
                    xs = slice(g * GRP, (g + 1) * GRP)
                    last = mm3(nc, PS[:, 2 + g, 0:GRP], (w.hi[:, k, 512:640], w.lo[:, k, 512:640]),
                               (c.xTh[:, k, xs], c.xTl[:, k, xs]), k == 0, k == KD - 1)
                last.then_inc(kp, 1)
            pe.wait_ge(nd, 1)
            for t in range(NT):
                if t >= 2:
                    pe.wait_ge(tev, t - 1)
                for q in range(4):
                    last = nc.tensor.transpose(PS[:, 6 + t % 2, q * P:(q + 1) * P], lat[:, t, q * P:(q + 1) * P], c.ident[:])
                last.then_inc(tr, 1)

        @block.scalar
        def _(act):
            w.make_hi(act)
            for t in range(NT):
                act.wait_ge(prj, t + 1)
                for s in range(2):
                    if t or s:
                        act.wait_ge(ach, 2 * t + s)
                    nc.scalar.activation(sq[:], PS[:, t % 2, s * 256:(s + 1) * 256], ACT.Square,
                                         accum_out=ss[:, 2 * t + s:2 * t + s + 1]).then_inc(ach, 1)
                nc.scalar.activation(lat[:, t, :], PS[:, t % 2, :], ACT.Copy).then_inc(ev, 1)
            act.wait_ge(rs_in, 1)
            nc.scalar.activation(ss[:], ss[:], ACT.Ln).then_inc(ach, 1)
            act.wait_ge(ach, 2 * NT + 1)
            nc.scalar.activation(ss[:], ss[:], ACT.Exp, scale=-0.5).then_inc(rs_out, 1)
            for t in range(NT):
                act.wait_ge(tr, t + 1)
                nc.scalar.activation(M.latT[:, :, t * P:(t + 1) * P],
                                     PS[:, 6 + t % 2, :].rearrange("p (q n) -> p q n", q=4), ACT.Copy).then_inc(tev, 1)

        @block.vector
        def _(dve):
            link = Chain(dve, dch)
            w.make_lo(dve, nc.vector, 1)
            dve.wait_ge(ld, 32)
            dve.wait_ge(ev, NT)
            nc.vector.tensor_scalar(ss[:], ss[:], 1.0 / 256, NORM_EPS, ALU.mult, ALU.add).then_inc(rs_in, 1)
            dve.wait_ge(rs_out, 1)
            for t in range(NT):
                for s in range(2):
                    x = lat[:, t, s * 256:(s + 1) * 256]
                    last = nc.vector.scalar_tensor_tensor(x, x, ss[:, 2 * t + s:2 * t + s + 1],
                                                          nrm[:, s * 256:(s + 1) * 256], ALU.mult, ALU.mult)
            last.then_inc(nd, 1)
            for g in range(3):
                dve.wait_ge(kp, g + 1)
                xs = slice(g * GRP, (g + 1) * GRP)
                nc.vector.tensor_tensor(M.KT[64:96, xs], PS[64:96, 2 + g, 0:GRP], M.T[64:96, xs], ALU.mult)
                link(nc.vector.tensor_tensor(tmp[64:96, :], PS[96:128, 2 + g, 0:GRP], M.T[96:128, xs], ALU.mult))
                link(nc.vector.tensor_tensor(M.KT[64:96, xs], M.KT[64:96, xs], tmp[64:96, :], ALU.add))
            nc.vector.tensor_copy(M.ckv_s[:], lat[:, TP, 256:512]).then_inc(kp, 1)


def softmax_max(nc, dve, link, mx, nm, scores, scale):
    link(nc.vector.tensor_reduce(out=mx, in_=scores, axis=AX.X, op=ALU.max))
    return nc.vector.tensor_scalar(nm, mx, -scale, None, ALU.mult)


def phase_mla_prompt(c, M):
    nc, A, PS = c.nc, c.A, c.PS
    V = c.sb("mla_v", [P, TP, 512])
    QH = c.sb("mla_qT", [P, 2, TOK])
    KTb = c.sb("mla_kTb", [P, SEQ])
    KT = (M.KT, KTb)
    wq = c.sb("mla_wq", [P, 2, 2, P])
    wk = c.sb("mla_wk", [P, 2, 2, NOPE])
    wkT = c.sb("mla_wkT", [NOPE, 2, 256])
    tmp = c.sb("rope_tmp", [P, GRP])
    Pb = c.sb("mla_p", [P, 2, D])
    PTs = c.sb("mla_pT", [P, 2, TP, P])
    mx, nm, rs, ri = (c.sb("mla_" + s, [P, 4]) for s in ("mx", "nm", "rs", "ri"))
    names = ("wv_loaded", "wA_loaded", "wB_loaded", "v_projected", "v_ready", "projected", "chunk_act", "chunk_dve", "key_rope",
             "abs_projected", "abs_ready", "scored", "max_ready", "exp_done", "transposed", "pT_dve", "pT_act", "pv_done", "o_written", "dve")
    (wvl, wla, wlb, vp, vr, prj, ca, cd, kcp, ap_, ar, sc, nms, ex, tr, ptd, pta, pv, ow, dch) = (c.sem("mla_" + s) for s in names)
    wl = (wla, wlb)
    U = 2 * TP
    CHUNKS = (2, 0, 1, 3, 4)
    BANKS = (0, 1, 2, 3, 7)

    def tok(i):
        return slice(i * P, (i + 1) * P)

    def scored(u):
        return PS[:, 2 * (u % 2):2 * (u % 2) + 2, :].rearrange("p b n -> p (b n)")[:, 0:(u % TP + 1) * P]

    def bank(x, n):
        return BANKS[n] if x == 0 else 7

    with nc.Block() as block:
        @block.gpsimd
        def _(pool):
            pool.sem_inc(ap_, 2)
            pool.sem_inc(ow, 1)

        @block.sync
        def _(sp):
            sp.dma_start(M.wuv[:], A["w_uv"]).then_inc(wvl, 16)
            sp.dma_start(M.rows[:], A["mla_rows"]).then_inc(wvl, 16)
            with sp.Fori(0, MLA_H // 2) as r:
                for x in range(2):
                    h = 2 * r + x
                    sp.wait_ge(ap_, h + 1)
                    sp.dma_start(wq[:, x], one(A["w_uq"], h)).then_inc(wl[x], 16)
                    sp.dma_start(wk[:, x], one(A["w_uk"], h)).then_inc(wl[x], 16)
                    sp.dma_start(wkT[:, x], one(A["w_ukT"], h)).then_inc(wl[x], 16)

        @block.tensor
        def _(pe):
            pe.wait_ge(wvl, 32)
            for t in range(TP):
                if t >= 2:
                    pe.wait_ge(vr, t - 1)
                for s in range(2):
                    last = nc.tensor.matmul(PS[:, t % 2, :], M.latT[:, 2 + s, tok(t)], M.wuv[:, s, :], start=s == 0, stop=s == 1)
                last.then_inc(vp, 1)
            pe.wait_ge(vr, TP)
            with pe.Fori(0, MLA_H // 2) as r:
                def project(x, n):
                    g = CHUNKS[n]
                    if x == 1 and n:
                        pe.wait_ge(ca, 10 * r + 5 + n)
                        pe.wait_ge(cd, 6 * r + 3 + min(n, 3))
                    for s in range(2):
                        if g < 3:
                            last = nc.tensor.matmul(PS[:, bank(x, n), 0:GRP], wq[:, x, s, :], M.latT[:, s, g * GRP:(g + 1) * GRP], start=s == 0, stop=s == 1)
                        else:
                            ks = slice((g - 3) * 512, (g - 2) * 512)
                            last = nc.tensor.matmul(PS[0:64, bank(x, n), :], wk[:, x, s, :], M.latT[:, 2 + s, ks], start=s == 0, stop=s == 1)
                    last.then_inc(prj, 1)

                def absorb(x):
                    pe.wait_ge(ca, 10 * r + 5 * x + (5 if x else 1))
                    for s in range(2):
                        last = nc.tensor.matmul(PS[:, 7 if x else 5, tok(s)], wkT[:, x, tok(s)], QH[0:64, x, TP * P:], start=s == 0, stop=s == 1,
                                                skip_group_check=True)
                    last.then_inc(ap_, 1)

                def scores(u):
                    x, i = u // TP, u % TP
                    if i == 0:
                        pe.wait_ge(ca, 10 * r + 5 * x + 5)
                        pe.wait_ge(cd, 6 * r + 3 * x + 3)
                        if x:
                            pe.wait_ge(kcp, 1)
                    n = (i + 1) * P
                    for a in range(0, n, 512):
                        b = min(a + 512, n)
                        bk = 2 * (u % 2) + a // 512
                        nc.tensor.matmul(PS[:, bk, 0:b - a], QH[0:96, x, tok(i)], KT[x][0:96, a:b], start=True, stop=b < n)
                    nc.tensor.matmul(PS[:, bk, b - a - P:b - a], M.rows[0:1, c.at["ROW"]:c.at["ROW"] + P],
                                     M.rows[0:1, c.at["NEG"]:c.at["NEG"] + P], start=False, stop=True).then_inc(sc, 1)

                def evacuated(u):
                    pe.wait_ge(ptd, U * r + u + 1)
                    if u % TP >= 4:
                        pe.wait_ge(pta, TP * r + 4 * (u // TP) + u % TP - 3)

                def transposes(u):
                    pe.wait_ge(ex, U * r + u + 1)
                    if u:
                        evacuated(u - 1)
                    for b in range(u % TP + 1):
                        last = nc.tensor.transpose(PS[:, 4 + b // 4, tok(b % 4)], Pb[:, u % 2, tok(b)], c.ident[:])
                    last.then_inc(tr, 1)

                def values(u):
                    x, i = u // TP, u % TP
                    pe.wait_ge(ow, U * r + u + 1)
                    for b in range(i + 1):
                        last = nc.tensor.matmul(PS[:, 6, 0:64], PTs[:, u % 2, b, :], V[:, b, bass.ds((2 * r + x) * 64, 64)],
                                                start=b == 0, stop=b == i)
                    last.then_inc(pv, 1)

                pe.wait_ge(wl[0], 48 * r + 48)
                for n in range(5):
                    project(0, n)
                absorb(0)
                scores(0)
                for u in range(U):
                    if u + 1 < U:
                        scores(u + 1)
                    if u == 0:
                        pe.wait_ge(wl[1], 48 * r + 48)
                        pe.wait_ge(ar, 2 * r + 1)
                    if u < 5:
                        project(1, u)
                    if u == 5:
                        absorb(1)
                    if u == 6:
                        pe.wait_ge(ar, 2 * r + 2)
                    transposes(u)
                    if u:
                        values(u - 1)
                evacuated(U - 1)
                values(U - 1)

        @block.scalar
        def _(act):
            for t in range(TP):
                act.wait_ge(vp, t + 1)
                nc.scalar.activation(V[:, t, :], PS[:, t % 2, :], ACT.Copy).then_inc(vr, 1)
            with act.Fori(0, MLA_H // 2) as r:
                def chunk(x, n):
                    g = CHUNKS[n]
                    act.wait_ge(prj, 10 * r + 5 * x + n + 1)
                    if g < 3:
                        last = nc.scalar.activation(QH[0:64, x, g * GRP:(g + 1) * GRP], PS[0:64, bank(x, n), 0:GRP], ACT.Copy)
                    else:
                        last = nc.scalar.activation(KT[x][0:64, (g - 3) * 512:(g - 2) * 512], PS[0:64, bank(x, n), :], ACT.Copy)
                    last.then_inc(ca, 1)

                def absorbed(x):
                    act.wait_ge(ap_, 2 * r + x + 3)
                    nc.scalar.activation(M.qabs[:, :, bass.ds(2 * r + x, 1), :].squeeze(2),
                                         PS[:, 7 if x else 5, 0:256].rearrange("p (s n) -> p s n", s=2), ACT.Copy).then_inc(ar, 1)

                def softmax(u):
                    if u >= 2:
                        act.wait_ge(tr, U * r + u - 1)
                    act.wait_ge(nms, U * r + u + 1)
                    nc.scalar.activation(Pb[:, u % 2, 0:(u % TP + 1) * P], scored(u), ACT.Exp, bias=nm[:, u % 4:u % 4 + 1], scale=MLA_SCALE,
                                         accum_out=rs[:, u % 4:u % 4 + 1]).then_inc(ex, 1)

                for n in range(5):
                    chunk(0, n)
                absorbed(0)
                softmax(0)
                for u in range(U):
                    i = u % TP
                    if u + 1 < U:
                        softmax(u + 1)
                    if u < 5:
                        chunk(1, u)
                    if u == 5:
                        absorbed(1)
                    if i >= 4:
                        act.wait_ge(tr, U * r + u + 1)
                        nc.scalar.activation(PTs[:, u % 2, 4:i + 1, :], PS[:, 5, 0:(i - 3) * P].rearrange("p (b n) -> p b n", n=P),
                                             ACT.Copy).then_inc(pta, 1)

        @block.vector
        def _(dve):
            link = Chain(dve, dch)
            nc.vector.tensor_copy(KTb[64:96, :], M.KT[64:96, 0:SEQ]).then_inc(kcp, 1)
            with link.loop(MLA_H // 2, 78) as r:
                def chunk(x, n):
                    g = CHUNKS[n]
                    dve.wait_ge(prj, 10 * r + 5 * x + n + 1)
                    xs = slice(g * GRP, (g + 1) * GRP)
                    q = QH[64:96, x, xs]
                    nc.vector.tensor_tensor(q, PS[64:96, bank(x, n), 0:GRP], M.T[64:96, xs], ALU.mult)
                    link(nc.vector.tensor_tensor(tmp[64:96, :], PS[96:128, bank(x, n), 0:GRP], M.T[96:128, xs], ALU.mult))
                    link(nc.vector.tensor_tensor(q, q, tmp[64:96, :], ALU.add))
                    dve.sem_inc(cd, 1)
                    if g == 2:
                        link(nc.vector.tensor_copy(M.qpe[64:96, bass.ds(2 * r + x, 1), :].squeeze(1), QH[64:96, x, TP * P:]))

                def largest(u):
                    dve.wait_ge(sc, U * r + u + 1)
                    link(softmax_max(nc, dve, link, mx[:, u % 4:u % 4 + 1], nm[:, u % 4:u % 4 + 1], scored(u), MLA_SCALE))
                    dve.sem_inc(nms, 1)

                def finish(u):
                    x, i = u // TP, u % TP
                    link(nc.vector.reciprocal(ri[:, u % 4:u % 4 + 1], rs[:, u % 4:u % 4 + 1]))
                    dve.wait_ge(pv, U * r + u + 1)
                    link(nc.vector.tensor_scalar(c.XM[:, i, bass.ds((2 * r + x) * 64, 64)], PS[:, 6, 0:64],
                                                 ri[:, u % 4:u % 4 + 1], None, ALU.mult))
                    dve.sem_inc(ow, 1)

                for n in range(3):
                    chunk(0, n)
                largest(0)
                for u in range(U):
                    if u + 1 < U:
                        largest(u + 1)
                    if u < 3:
                        chunk(1, u)
                    m = min(u % TP + 1, 4)
                    dve.wait_ge(tr, U * r + u + 1)
                    nc.vector.tensor_copy(PTs[:, u % 2, 0:m, :], PS[:, 4, 0:m * P].rearrange("p (b n) -> p b n", n=P)).then_inc(ptd, 1)
                    if u:
                        finish(u - 1)
                finish(U - 1)


def phase_mla_sample(c, M):
    nc, A, PS = c.nc, c.A, c.PS
    NK = PAST // P + 1
    ckv = c.sb("s_ckv", [P, NK - 1, 256])
    ckvT = c.sb("s_ckvT", [P, 2, 2, PAST])
    kpeT = (M.T, c.sb("s_kpeT", [P, PAST]))
    qb = c.sb("s_qb", [P, 2, 2, P])
    qpb = c.sb("s_qpb", [P, 2, P])
    Pb = c.sb("s_p", [P, 2, NK * P])
    PTs = c.sb("s_pT", [P, 2, NK, P])
    ol = c.sb("s_olat", [P, 256])
    olT = M.qabs
    mx, nm, rs, ri = (c.sb("s_" + s, [P, 2]) for s in ("mx", "nm", "rs", "ri"))
    names = ("k_loaded", "k_loaded1", "own_loaded", "v_loaded", "q_ready", "scored", "max_ready", "exp_done", "transposed", "pT_ready", "pv_done", "o_ready",
             "o_transposed", "oT_ready", "uv_done", "dve")
    (kl0, kl1, ol_, vl, qd, sc, nms, ex, tr, pt, pv, orr, otr, otd, uv, dch) = (c.sem("ms_" + s) for s in names)
    rcd = c.sem("ms_reciprocal")
    kl = (kl0, kl1)
    scored = PS[:, 0:3, :].rearrange("p b n -> p (b n)")[:, 0:NK * P]

    def ge(eng, sem, v):
        if not isinstance(v, int) or v > 0:
            eng.wait_ge(sem, v)

    def slots(eng, step):
        step(0, 0, True, False, False)
        step(1, 1, True, True, False)
        with eng.Fori(0, NB // 2 - 2) as r:
            for s in range(2):
                step(2 * r + 2 + s, s, True, True, True)
        for s in range(2):
            step(NB - 2 + s, s, True, True, True)
        step(NB, 0, False, True, True)
        step(NB + 1, 1, False, False, True)

    with nc.Block() as block:
        @block.gpsimd
        def _(pool):
            for started in (otr, otd):
                pool.sem_inc(started, 1)
            pool.dma_start(ckv[:], A["c_ckv"][0]).then_inc(vl, 16)
            with pool.Fori(0, NB - 1) as b:
                pool.wait_ge(pv, b + 1)
                pool.dma_start(ckv[:], one(A["c_ckv"], b + 1)).then_inc(vl, 16)

        @block.sync
        def _(sp):
            sp.dma_start(M.KT[96:97, 0:NB * P], A["mla_own"]).then_inc(ol_, 16)

            def load(b, s):
                sp.dma_start(ckvT[:, s], one(A["c_ckvT"], b)).then_inc(kl[s], 16)
                sp.dma_start(kpeT[s][64:96, 0:PAST], one(A["c_kpeT"], b)).then_inc(kl[s], 16)

            load(0, 0)
            load(1, 1)
            with sp.Fori(0, NB // 2 - 1) as r:
                for s in range(2):
                    sp.wait_ge(sc, 2 * r + s + 1)
                    load(2 * r + 2 + s, s)

        @block.tensor
        def _(pe):
            def step(b, s, now, last1, last2):
                if now:
                    pe.wait_ge(kl[s], b * 16 + (32 - 16 * s))
                    pe.wait_ge(qd, b + 1)
                    ge(pe, ex, b)
                    for g in range(3):
                        n = P if g == 2 else 512
                        for q in range(2):
                            rhs = M.latT[:, 2 + q, TP * P:] if g == 2 else ckvT[:, s, q, g * 512:(g + 1) * 512]
                            nc.tensor.matmul(PS[:, g, 0:n], qb[:, s, q, :], rhs, start=q == 0, stop=False)
                        rhs = M.KT[64:97, TP * P:] if g == 2 else kpeT[s][64:96, g * 512:(g + 1) * 512]
                        last = nc.tensor.matmul(PS[:, g, 0:n], qpb[64:97 if g == 2 else 96, s, :], rhs, start=False, stop=True)
                    last.then_inc(sc, 1)
                if last2:
                    pe.wait_ge(pt, 2 * b - 2)
                    pe.wait_ge(vl, 16 * b - 16)
                    for k in range(NK):
                        rhs = M.ckv_s[:] if k == NK - 1 else ckv[:, k, :]
                        last = nc.tensor.matmul(PS[:, 6, 0:256], PTs[:, s, k, :], rhs, start=k == 0, stop=k == NK - 1)
                    last.then_inc(pv, 1)
                if last1:
                    pe.wait_ge(ex, b)
                    for k in range(NK):
                        last = nc.tensor.transpose(PS[:, 3 + k // 4, (k % 4) * P:(k % 4 + 1) * P], Pb[:, 1 - s, k * P:(k + 1) * P], c.ident[:])
                    last.then_inc(tr, 1)
                if last2:
                    pe.wait_ge(orr, b - 1)
                    pe.wait_ge(otd, b - 1)
                    for q in range(2):
                        last = nc.tensor.transpose(PS[:, 7, q * P:(q + 1) * P], ol[:, q * P:(q + 1) * P], c.ident[:])
                    last.then_inc(otr, 1)

            slots(pe, step)
            pe.wait_ge(otd, NB + 1)
            for h in range(MLA_H):
                for q in range(2):
                    last = nc.tensor.matmul(PS[:, 0, h * 64:(h + 1) * 64], olT[:, q, h, :], M.wuv[:, q, h * 64:(h + 1) * 64],
                                            start=q == 0, stop=q == 1, skip_group_check=True)
            last.then_inc(uv, 1)

        @block.scalar
        def _(act):
            def step(b, s, now, last1, last2):
                if now:
                    act.wait_ge(nms, b + 1)
                    nc.scalar.activation(Pb[:, s, :], scored, ACT.Exp, bias=nm[:, s:s + 1], scale=MLA_SCALE, accum_out=rs[:, s:s + 1]).then_inc(ex, 1)
                if last1:
                    act.wait_ge(tr, b)
                    nc.scalar.activation(PTs[:, 1 - s, 4:NK, :], PS[:, 4:6, :].rearrange("p b n -> p (b n)")[:, 0:(NK - 4) * P]
                                         .rearrange("p (b n) -> p b n", n=P), ACT.Copy).then_inc(pt, 1)
                if last2:
                    act.wait_ge(otr, b)
                    for q in range(2):
                        last = nc.scalar.activation(olT[:, q, :, bass.ds((b - 2) * ST, ST)],
                                                    PS[:, 7, q * P:(q + 1) * P].rearrange("p (h t) -> p h t", h=MLA_H), ACT.Copy)
                    last.then_inc(otd, 1)

            slots(act, step)

        @block.vector
        def _(dve):
            def prepare(b, s):
                nc.vector.tensor_copy(M.KT[96:97, TP * P:], M.KT[96:97, bass.ds(b * P, P)])
                for q in range(2):
                    nc.vector.tensor_copy(qb[:, s, q, :].rearrange("p (h t) -> p h t", h=MLA_H), M.qabs[:, q, :, bass.ds(b * ST, ST)])
                nc.vector.tensor_copy(qpb[64:96, s, :].rearrange("p (h t) -> p h t", h=MLA_H),
                                      M.qpe[64:96, :, bass.ds(b * ST, ST)]).then_inc(qd, 1)

            def step(b, s, now, last1, last2):
                if now:
                    dve.wait_ge(sc, b + 1)
                    nc.vector.tensor_reduce(out=mx[:, s:s + 1], in_=scored, axis=AX.X, op=ALU.max).then_inc(dch, 1)
                    dve.wait_ge(dch, b + 1)
                    nc.vector.tensor_scalar(nm[:, s:s + 1], mx[:, s:s + 1], -MLA_SCALE, None, ALU.mult).then_inc(nms, 1)
                    if not isinstance(b, int) or b + 1 < NB:
                        prepare(b + 1, 1 - s)
                if last2:
                    dve.wait_ge(pv, b - 1)
                    dve.wait_ge(rcd, b - 1)
                    dve.wait_ge(otr, b - 1)
                    nc.vector.tensor_scalar(ol[:], PS[:, 6, 0:256], ri[:, s:s + 1], None, ALU.mult).then_inc(orr, 1)
                if last1:
                    dve.wait_ge(tr, b)
                    nc.vector.tensor_copy(PTs[:, 1 - s, 0:4, :], PS[:, 3, :].rearrange("p (b n) -> p b n", n=P)).then_inc(pt, 1)
                    nc.vector.reciprocal(ri[:, 1 - s:2 - s], rs[:, 1 - s:2 - s]).then_inc(rcd, 1)

            nc.vector.memset(qpb[96:97], 1.0)
            dve.wait_ge(ol_, 16)
            prepare(0, 0)
            slots(dve, step)
            dve.wait_ge(uv, 1)
            nc.vector.tensor_copy(c.XM[:, TP, 0:512], PS[:, 0, :])


def phase_linear(c, ret, G=None):
    nc, A, PS = c.nc, c.A, c.PS
    tag = "ret" if ret else "gla"
    DK = P if ret else 64
    HH = 2 if ret else 1
    W = 2 * DK + 2 * P
    w = Split(c, tag + "w", KD, W, lambda i, k: one(A["w_" + tag], i)[k] if not isinstance(i, int) else A["w_" + tag][i, k])
    qk = c.sb(tag + "_qk", [P, 3, 2 * DK])
    vz = c.sb(tag + "_v", [P, 4, HH * P])

    def values(t):
        return vz[:, t % 4, :].rearrange("p (b d) -> p b d", d=64)[:, 0::3, :] if ret else vz[:, t % 4, :]

    sg = c.sb(tag + "_gate", [P, NT, P])
    QK = c.sb(tag + "_qkT", [DK, 3, 2, P])
    PT = c.sb(tag + "_pT", [P, 2, HH, P])
    S = c.sb(tag + "_state", [DK, 3, P])
    tS = c.sb(tag + "_kv", [DK, P])
    os_ = c.sb(tag + "_o", [P, NT, P])
    S0 = c.sb(tag + "_s0", [DK, NB, P])
    SN = c.sb(tag + "_s1", [DK, NB, P])
    Qm = c.sb(tag + "_qTm", [DK, NB, P])
    vm = c.sb(tag + "_vm", [P, NB, P])
    squares = c.sb(tag + "_squares", [P, NT * P])
    st = c.sb(tag + "_stat", [P, NT * HH])
    nrm = c.sb(tag + "_normw", [P, 512])
    if ret:
        rC = c.sb("ret_cos", [P, NT, HD])
        rS = c.sb("ret_sin", [P, NT, HD])
        rp = c.sb("ret_pow", [P, 2, 4 * 4])
        rG = c.sb("ret_decay", [P, 4, 2, P])
        ta = c.sb("ret_ta", [P, 4, HD])
        tb = c.sb("ret_tb", [P, 4, HD])
    else:
        Sc = c.sb("gla_sc", [DK, 2, P])
    names = ("consts", "projected", "qk_ready", "vg_ready", "transposed", "qkT_ready", "scored", "pT_ready", "kv_done", "state_ready",
             "pv_done", "o_ready", "stats", "rstd", "turn_done", "vm_ready", "s0_loaded", "stored", "s1_ready", "dve", "act", "qm_zero", "s0_free", "sc_ready")
    (cl, prj, qkr, vgr, tr, qkT, sc, ptr, kv, sr, pv, orr, sti, sto, td, vmr, s0l, outs, s1r, dch, ach, qz, s0f, scr) = (c.sem(f"{tag}_{s}") for s in names)
    TURNS = 4
    N_OUT = 4 if ret else 2
    tri = c.masks[:, c.at["TRI"]:c.at["TRI"] + P]
    tris = c.masks[:, c.at["TRIS"]:c.at["TRIS"] + P]

    with nc.Block() as block:
        @block.sync
        def _(sp):
            sp.dma_start(nrm[:], A[tag + "_norm"].partition_broadcast(P)).then_inc(cl, 16)
            if ret:
                sp.dma_start(rC[:], A["ret_cos"]).then_inc(cl, 16)
                sp.dma_start(rS[:], A["ret_sin"]).then_inc(cl, 16)
                sp.dma_start(rp[:], A["ret_pow"]).then_inc(cl, 16)
                sp.dma_start(rG[:], A["ret_decay"]).then_inc(cl, 16)
            with sp.Fori(0, TURNS) as i:
                w.load(sp, i)
            sp.wait_ge(outs, 16 * N_OUT * TURNS + 1)

        @block.gpsimd
        def _(pool):
            for started in (prj, td, s0f, qkT, ptr, orr, outs):
                pool.sem_inc(started, 1)
            nc.gpsimd.memset(S0[:], 0.0)
            nc.gpsimd.memset(vz[:], 0.0)
            nc.gpsimd.memset(Qm[:], 0.0).then_inc(qz, 1)
            w.free_slots(pool)
            with pool.Fori(0, TURNS) as i:
                w.make_lo(pool, nc.gpsimd, 0, i)
                pool.wait_ge(vgr, 9 * i + 9)
                for b in range(NB):
                    dst = vm[:, b, :].rearrange("p (h d) -> p h d", h=2) if ret else vm[:, b, :]
                    own = c.masks[:, c.at["OWN8"] + b:c.at["OWN8"] + b + 1]
                    own = own.unsqueeze(2).broadcast_to([P, 2, 64]) if ret else own.broadcast_to([P, P])
                    last = nc.gpsimd.tensor_tensor(dst, values(TP), own, ALU.mult)
                last.then_inc(vmr, 1)

        @block.tensor
        def _(pe):
            with pe.Fori(0, TURNS) as i:
                def transposes(t):
                    pe.wait_ge(qkr, 9 * i + t + 1)
                    pe.wait_ge(qkT, 9 * i + t + 1)
                    for q in range(HH):
                        last = nc.tensor.transpose(PS[:, 2, q * P:(q + 1) * P], qk[:, t % 3, q * P:(q + 1) * P], c.ident[:])
                    last.then_inc(tr, 1)

                def scores(t):
                    pe.wait_ge(qkT, 9 * i + t + 2)
                    pe.wait_ge(ptr, 9 * i + t + 1)
                    for h in range(HH):
                        r = slice(64 * h, 64 * h + 64)
                        last = nc.tensor.matmul(PS[:, 3 + h, 0:P], QK[r, t % 3, 1, :], QK[r, t % 3, 0, :], start=True, stop=True)
                    last.then_inc(sc, 1)
                    pe.wait_ge(vgr, 9 * i + t + 1)
                    kt = qk[:, t % 3, DK:2 * DK]
                    if t < TP:
                        pe.wait_ge(sr, 9 * i + t + 1 if t else 9 * i + 1)
                        nc.tensor.matmul(PS[0:DK, 6, 0:P], kt, values(t), start=True, stop=True).then_inc(kv, 1)
                    else:
                        pe.wait_ge(vmr, i + 1)
                        pe.wait_ge(sr, 9 * i + 9)
                        for g in range(2):
                            last = nc.tensor.matmul(PS[0:DK, 6 + g, :], kt, vm[:, 4 * g:4 * g + 4, :].rearrange("p b v -> p (b v)"),
                                                    start=True, stop=True)
                        last.then_inc(kv, 1)

                def outputs(t):
                    pe.wait_ge(ptr, 9 * i + t + 2)
                    pe.wait_ge(orr, 9 * i + t + 1)
                    if t < TP:
                        if ret:
                            nc.tensor.matmul(PS[:, 5, 0:P], QK[:, t % 3, 0, :], S[:, t % 3, :], start=True, stop=False)
                        else:
                            pe.wait_ge(scr, 8 * i + t + 1)
                            nc.tensor.matmul(PS[:, 5, 0:P], QK[:, t % 3, 0, :], Sc[:, t % 2, :], start=True, stop=False)
                    else:
                        pe.wait_ge(s0l, 16 * HH * (i + 1))
                        for b in range(NB):
                            nc.tensor.matmul(PS[:, 5, 0:P], Qm[:, b, :], S0[:, b, :], start=b == 0, stop=False)
                    for h in range(HH):
                        last = nc.tensor.matmul(PS[:, 5, 0:P], PT[:, t % 2, h, :], vz[:, t % 4, h * P:(h + 1) * P],
                                                start=False, stop=h == HH - 1)
                    last.then_inc(pv, 1)

                for s in range(NT + 3):
                    if s < NT:
                        if s >= 2:
                            pe.wait_ge(qkr, 9 * i + s - 1)
                            pe.wait_ge(vgr, 9 * i + s - 1)
                        project_tile(c, pe, w, s, PS[:, s % 2, 0:W], slice(0, W), i).then_inc(prj, 1)
                    if 0 <= s - 1 < NT:
                        transposes(s - 1)
                    if 0 <= s - 2 < NT:
                        scores(s - 2)
                    if 0 <= s - 3 < NT:
                        outputs(s - 3)

        @block.scalar
        def _(act):
            act.wait_ge(qz, 1)
            with act.Fori(0, TURNS) as i:
                act.wait_ge(prj, 9 * i + 1)
                w.make_hi(act, i)
                act.wait_ge(s0f, i + 1)
                if ret:
                    for h in range(2):
                        act.dma_start(S0[64 * h:64 * h + 64, :, 64 * h:64 * h + 64],
                                      A["state_ret"][:, bass.ds(2 * i + h, 1)].squeeze(1).rearrange("b k v -> k b v")).then_inc(s0l, 16)
                else:
                    act.dma_start(S0[:], A["state_gla"][:, bass.ds(i, 1)].squeeze(1).rearrange("b k v -> k b v")).then_inc(s0l, 16)
                act.wait_ge(td, i + 1)
                for s in range(NT + 3):
                    if s < NT:
                        act.wait_ge(prj, 9 * i + s + 2)
                        src = PS[:, s % 2, 2 * DK:2 * DK + P]
                        nc.scalar.activation(values(s), src.rearrange("p (h d) -> p h d", h=2) if ret else src, ACT.Copy)
                        nc.scalar.activation(sg[:, s, :], PS[:, s % 2, 2 * DK + P:W], ACT.Silu).then_inc(vgr, 1)
                    if 0 <= s - 1 < NT:
                        t = s - 1
                        act.wait_ge(tr, 9 * i + t + 1)
                        if t == TP:
                            nc.scalar.activation(Qm[:].rearrange("p b (c t) -> p (b c) t", t=ST)[:, 0::NB + 1, :],
                                                 PS[0:DK, 2, 0:P].rearrange("p (b t) -> p b t", t=ST), ACT.Copy)
                        if ret:
                            nc.scalar.activation(QK[:, t % 3], PS[:, 2, 0:2 * P].rearrange("p (q n) -> p q n", q=2), ACT.Copy).then_inc(qkT, 1)
                        else:
                            nc.scalar.activation(QK[:, t % 3, 0, :], PS[0:64, 2, 0:P], ACT.Copy)
                            nc.scalar.activation(QK[:, t % 3, 1, :], PS[64:128, 2, 0:P], ACT.Copy).then_inc(qkT, 1)
                    if 0 <= s - 3 < NT:
                        t = s - 3
                        act.wait_ge(pv, 9 * i + t + 1)
                        nc.scalar.activation(os_[:, t, :], PS[:, 5, 0:P], ACT.Copy).then_inc(orr, 1)
                act.wait_ge(sti, i + 1)
                nc.scalar.activation(st[:], st[:], ACT.Ln).then_inc(ach, 1)
                act.wait_ge(ach, i + 1)
                nc.scalar.activation(st[:], st[:], ACT.Exp, scale=-0.5).then_inc(sto, 1)
                act.wait_ge(sr, 9 * i + 9)
                if ret:
                    for h in range(2):
                        act.dma_start(one(A["o_ret_p"], 2 * i + h), S[64 * h:64 * h + 64, TP % 3, 64 * h:64 * h + 64]).then_inc(outs, 16)
                else:
                    act.dma_start(one(A["o_gla_p"], i), S[:, TP % 3, :]).then_inc(outs, 16)
                act.wait_ge(s1r, i + 1)
                if ret:
                    for h in range(2):
                        act.dma_start(A["o_ret_s"][:, bass.ds(2 * i + h, 1)].squeeze(1).rearrange("b k v -> k b v"),
                                      SN[64 * h:64 * h + 64, :, 64 * h:64 * h + 64]).then_inc(outs, 16)
                else:
                    act.dma_start(A["o_gla_s"][:, bass.ds(i, 1)].squeeze(1).rearrange("b k v -> k b v"), SN[:]).then_inc(outs, 16)

        @block.vector
        def _(dve):
            link = Chain(dve, dch)
            dve.wait_ge(cl, 80 if ret else 16)
            with link.loop(TURNS, 55 if ret else 42) as i:
                w.make_lo(dve, nc.vector, 1, i)
                hs = lambda ap: ap.unsqueeze(1).broadcast_to([P, 4, ap.shape[-1]])

                def rotate(t):
                    dve.wait_ge(vgr, 9 * i + t + 1)
                    if ret:
                        src = PS[:, t % 2, 0:256].rearrange("p (h d) -> p h d", h=4)
                        nc.vector.tensor_tensor(ta[:], src, hs(rC[:, t, :]), ALU.mult)
                        nc.vector.tensor_tensor(tb[:, :, 0:32], src[:, :, 32:64], hs(rS[:, t, 0:32]), ALU.mult)
                        link(nc.vector.tensor_tensor(tb[:, :, 32:64], src[:, :, 0:32], hs(rS[:, t, 32:64]), ALU.mult))
                        link(nc.vector.tensor_tensor(ta[:], ta[:], tb[:], ALU.add))
                        pw = rp[:, t // TP, bass.ds(4 * i, 4)].unsqueeze(2).broadcast_to([P, 4, HD])
                        link(nc.vector.tensor_tensor(qk[:, t % 3, :].rearrange("p (h d) -> p h d", h=4), ta[:], pw, ALU.mult))
                        dve.sem_inc(qkr, 1)
                    else:
                        nc.vector.scalar_tensor_tensor(qk[:, t % 3, 0:64], PS[:, t % 2, 0:64], 64 ** -0.5,
                                                       G.eB[:, t, bass.ds(64 * i, 64)], ALU.mult, ALU.mult)
                        link(nc.vector.tensor_tensor(qk[:, t % 3, 64:128], PS[:, t % 2, 64:128],
                                                G.eN[:, t, bass.ds(64 * i, 64)], ALU.mult))
                        dve.sem_inc(qkr, 1)

                def scale_state(t):
                    link(nc.vector.tensor_scalar(Sc[:, t % 2, :], S[:, t % 3, :], G.dec[:, bass.ds(i * 24 + 3 * t, 1)], None, ALU.mult))
                    dve.sem_inc(scr, 1)

                def mask_and_state(t):
                    dve.wait_ge(sc, 9 * i + t + 1)
                    m = (tris if t == TP else tri).unsqueeze(1).broadcast_to([P, HH, P])
                    nc.vector.tensor_tensor(PT[:, t % 2], PS[:, 3:3 + HH, 0:P], m, ALU.mult).then_inc(ptr, 1)
                    if t < TP:
                        if not ret:
                            scale_state(t)
                        dve.wait_ge(kv, 9 * i + t + 1)
                        if ret:
                            link(nc.vector.tensor_tensor(tS[:], PS[:, 6, 0:P], S[:, t % 3, :], ALU.add))
                            link(nc.vector.tensor_tensor(S[:, (t + 1) % 3, :], tS[:], rG[:, bass.ds(i, 1), 0, :].squeeze(1), ALU.mult))
                        else:
                            link(nc.vector.tensor_scalar(tS[:], PS[0:DK, 6, 0:P], G.dec[:, bass.ds(i * 24 + 3 * t + 1, 1)], None, ALU.mult))
                            link(nc.vector.scalar_tensor_tensor(S[:, (t + 1) % 3, :], S[:, t % 3, :], G.dec[:, bass.ds(i * 24 + 3 * t + 2, 1)],
                                                                tS[:], ALU.mult, ALU.add))
                        dve.sem_inc(sr, 1)
                    else:
                        dve.wait_ge(kv, 9 * i + 9)
                        dve.wait_ge(s0l, 16 * HH * (i + 1))
                        dve.wait_ge(outs, 16 * N_OUT * i + 1)
                        link(nc.vector.tensor_tensor(SN[:].rearrange("p b v -> p (b v)"), PS[0:DK, 6:8, :].rearrange("p b n -> p (b n)"),
                                                     S0[:].rearrange("p b v -> p (b v)"), ALU.add))
                        if ret:
                            g = rG[:, bass.ds(i, 1), 1, :].broadcast_to([P, NB, P])
                        else:
                            g = G.decs[:, bass.ds(NB * i, NB)].unsqueeze(2).broadcast_to([DK, NB, P])
                        link(nc.vector.tensor_tensor(SN[:], SN[:], g, ALU.mult))
                        dve.sem_inc(s1r, 1)
                        dve.wait_ge(pv, 9 * i + 9)
                        dve.sem_inc(s0f, 1)

                dve.wait_ge(outs, 16 * N_OUT * i + 1)
                link(nc.vector.memset(S[:, 0, :], 0.0))
                dve.sem_inc(sr, 1)
                for s in range(NT + 2):
                    if s < NT:
                        rotate(s)
                    if s >= 2:
                        mask_and_state(s - 2)
                dve.wait_ge(orr, 9 * i + 9 + 1)
                o = os_[:].rearrange("p t (h d) -> p (t h) d", h=HH)
                dv = P // HH
                stb = st[:].unsqueeze(2).broadcast_to([P, NT * HH, dv])
                if ret:
                    link(nc.vector.tensor_reduce(out=st[:], in_=o, axis=AX.X, op=ALU.add))
                    link(nc.vector.tensor_scalar(st[:], st[:], -1.0 / dv, None, ALU.mult))
                    link(nc.vector.tensor_tensor(o, o, stb, ALU.add))
                big = squares[:].rearrange("p (h d) -> p h d", d=dv)
                link(nc.vector.tensor_tensor(big, o, o, ALU.mult))
                link(nc.vector.tensor_reduce(out=st[:], in_=big, axis=AX.X, op=ALU.add))
                link(nc.vector.tensor_scalar(st[:], st[:], 1.0 / dv, NORM_EPS, ALU.mult, ALU.add))
                dve.sem_inc(sti, 1)
                dve.wait_ge(sto, i + 1)
                link(nc.vector.tensor_tensor(o, o, stb, ALU.mult))
                nw = nrm[:, bass.ds(P * i, P)].unsqueeze(1).broadcast_to([P, NT, P])
                link(nc.vector.tensor_tensor(os_[:], os_[:], nw, ALU.mult))
                base = 512 if ret else 0
                link(nc.vector.tensor_tensor(c.XM[:, :, bass.ds(P * i + base, P)], os_[:], sg[:], ALU.mult))
                dve.sem_inc(td, 1)


def phase_gates(c, G):
    nc, A, PS = c.nc, c.A, c.PS
    w = Split(c, "wga", KD, P, lambda i, k: A["w_ga"][k])
    gaT = c.sb("gaT", [32, TOK])
    wa = c.sb("w_a2", [17, 256])
    g = c.sb("g_log", [P, NT, 256])
    a = c.sb("g_abs", [P, NT, 256])
    names = ("consts", "projected", "gaT_ready", "ones", "logits", "gates", "sums", "sum_read", "steps", "dve", "act", "x")
    (cl, prj, gr, on, lg, gt, su, srd, dn, dch, ach, _) = (c.sem("gate_" + s) for s in names)
    with nc.Block() as block:
        @block.sync
        def _(sp):
            sp.dma_start(wa[:], A["w_a2b"]).then_inc(cl, 16)
            w.load(sp)
            sp.wait_ge(cl, 16)

        @block.gpsimd
        def _(pool):
            w.free_slots(pool)
            w.make_lo(pool, nc.gpsimd, 0)
            nc.gpsimd.memset(gaT[:], 1.0).then_inc(on, 1)

        @block.tensor
        def _(pe):
            for q in range(3):
                xs = slice(q * GRP, (q + 1) * GRP)
                for k in range(KD):
                    w.wait(pe, k)
                    last = mm3(nc, PS[:, q, 0:GRP], (w.hi[:, k, :], w.lo[:, k, :]), (c.xTh[:, k, xs], c.xTl[:, k, xs]), k == 0, k == KD - 1)
                last.then_inc(prj, 1)
            pe.wait_ge(cl, 16)
            pe.wait_ge(gr, 3)
            for t in range(NT):
                last = nc.tensor.matmul(PS[:, 3 + t // 2, (t % 2) * 256:(t % 2) * 256 + 256], gaT[0:17, t * P:(t + 1) * P], wa[:],
                                        start=True, stop=True, skip_group_check=True)
            last.then_inc(lg, 1)
            pe.wait_ge(gt, 1)
            for t in range(NT):
                o = c.at["TRIS"] if t == TP else c.at["MID"]
                last = nc.tensor.matmul(PS[:, 3 + t // 2, (t % 2) * 256:(t % 2) * 256 + 256], c.masks[:, o:o + P], g[:, t, :],
                                        start=True, stop=True, skip_group_check=True)
            for h in range(4):
                for t in range(TP):
                    nc.tensor.matmul(PS[0:64, 0, 24 * h + 3 * t:24 * h + 3 * t + 3], g[:, t, 64 * h:64 * h + 64],
                                     c.masks[:, c.at["SEL"]:c.at["SEL"] + 3], start=True, stop=True, skip_group_check=True)
                last = nc.tensor.matmul(PS[0:64, 1, NB * h:NB * h + NB], g[:, TP, 64 * h:64 * h + 64], c.masks[:, c.at["OWN8"]:c.at["OWN8"] + NB],
                                        start=True, stop=True, skip_group_check=True)
            last.then_inc(su, 1)

        lgp = PS[:, 3:8, :].rearrange("p b n -> p (b n)")[:, 0:NT * 256]

        @block.scalar
        def _(act):
            w.make_hi(act)
            act.wait_ge(on, 1)
            for q in range(3):
                act.wait_ge(prj, q + 1)
                nc.scalar.activation(gaT[0:16, q * GRP:(q + 1) * GRP], PS[0:16, q, 0:GRP], ACT.Copy).then_inc(gr, 1)
            act.wait_ge(lg, 1)
            af = a[:].rearrange("p t n -> p (t n)")
            nc.scalar.activation(af, lgp, ACT.Abs).then_inc(ach, 1)
            act.wait_ge(ach, 1)
            nc.scalar.activation(af, af, ACT.Exp, scale=-1.0).then_inc(ach, 1)
            act.wait_ge(ach, 2)
            nc.scalar.activation(af, af, ACT.Ln, bias=1.0).then_inc(ach, 1)
            act.wait_ge(su, 1)
            eB = G.eB[:].rearrange("p t n -> p (t n)")
            eN = G.eN[:].rearrange("p t n -> p (t n)")
            act.wait_ge(dn, 1)
            nc.scalar.activation(eB, a[:].rearrange("p t n -> p (t n)"), ACT.Exp)
            nc.scalar.activation(eN, a[:].rearrange("p t n -> p (t n)"), ACT.Exp, scale=-1.0)
            nc.scalar.activation(G.dec[:], PS[0:64, 0, 0:96], ACT.Exp)
            nc.scalar.activation(G.decs[:], PS[0:64, 1, 0:32], ACT.Exp)

        @block.vector
        def _(dve):
            link = Chain(dve, dch)
            w.make_lo(dve, nc.vector, 1)
            dve.wait_ge(lg, 1)
            dve.wait_ge(ach, 1)
            gf = g[:].rearrange("p t n -> p (t n)")
            af = a[:].rearrange("p t n -> p (t n)")
            link(nc.vector.tensor_scalar(gf, lgp, 0.0, None, ALU.min))
            dve.wait_ge(ach, 3)
            link(nc.vector.tensor_tensor(gf, gf, af, ALU.subtract))
            nc.vector.tensor_scalar(gf, gf, 1.0 / 16.0, None, ALU.mult).then_inc(gt, 1)
            dve.wait_ge(su, 1)
            nc.vector.tensor_scalar(af, lgp, -80.0, 80.0, ALU.max, ALU.min).then_inc(dn, 1)


def phase_swa(c):
    nc, A, PS = c.nc, c.A, c.PS
    W = 384
    NK = NB + 1
    w = Split(c, "swaw", KD, 2 * W, lambda i, k: A["w_swa"][k])
    qk = c.sb("swa_qk", [P, 3, 320])
    kro = c.sb("swa_kro", [P, 2, HD])
    v = c.sb("swa_v", [P, NT, HD])
    KT = c.sb("swa_kT", [HD + 8, TOK])
    QT = c.sb("swa_qT", [HD + 8, 3, 4, P])
    Pb = w.raw[:].rearrange("p r n -> p (r n)")[:, 0:2 * NK * P].rearrange("p (s n) -> p s n", s=2)
    PTs = c.sb("swa_pT", [P, 2, NK, P])
    cK = c.sb("swa_cachekT", [HD + 8, NB * P])
    cV = c.sb("swa_cachev", [P, NB, HD])
    tab = c.sb("swa_tab", [P, NT, 32])
    ta = c.sb("swa_ta", [P, 5, 16])
    tb = c.sb("swa_tb", [P, 5, 16])
    sk = c.sb("swa_sink", [P, 8])
    mx, nm, rs, es, ri = (c.sb("swa_" + s, [P, 8]) for s in ("mx", "nm", "rs", "es", "ri"))
    names = ("consts", "cache_loaded", "projected", "qk_ready", "v_ready", "transposed", "qkT_ready", "scored", "max_ready", "exp_done",
             "p_transposed", "pT_ready", "pT_act", "pv_done", "o_written", "stored", "dve", "copied", "kout")
    (cl, chl, prj, qkr, vr, tr, qkT, sc, nms, ex, ptt, ptr, pta, pv, ow, outs, dch, cpy, ko) = (c.sem("swa_" + s) for s in names)
    SCALE = HD ** -0.5
    UN = TP + 4
    FIRST = NT
    SLOTS = FIRST + 6
    sample_scores = PS[:, 0:3, :].rearrange("p b n -> p (b n)")[:, 0:NK * P]
    slot = lambda t: 2 if t == TP else t % 2
    with nc.Block() as block:
        @block.sync
        def _(sp):
            w.load(sp)
            sp.dma_start(tab[:], A["swa_tab"]).then_inc(cl, 16)
            sp.dma_start(sk[:], A["sinks"].partition_broadcast(P)).then_inc(cl, 16)
            sp.dma_start(QT[HD:HD + 8].rearrange("p s h n -> p (s h n)"), A["swa_q_rows"]).then_inc(cl, 16)
            sp.dma_start(KT[HD:HD + 8, :], A["swa_k_rows"]).then_inc(cl, 16)
            sp.dma_start(cK[HD:HD + 8, :], A["swa_c_rows"]).then_inc(cl, 16)
            for n in ("k", "v"):
                sp.dma_start(A[f"o_swa_{n}_old"], A[f"c_swa_{n}_old"]).then_inc(cpy, 16)
            with sp.Fori(0, 2) as i:
                sp.wait_ge(pv, UN * i + 1)
                sp.dma_start(cK[0:HD, :], one(A["c_swa_kT"], i)).then_inc(chl, 16)
                sp.dma_start(cV[:], one(A["c_swa_v"], i)).then_inc(chl, 16)
            sp.wait_ge(outs, 64 + 1)
            sp.wait_ge(cpy, 32)

        @block.gpsimd
        def _(pool):
            for started in (pv, qkT, ow, prj, outs):
                pool.sem_inc(started, 1)
            w.free_slots(pool)
            w.make_lo(pool, nc.gpsimd, 0)

        @block.tensor
        def _(pe):
            with pe.Fori(0, 2) as i:
                def project(t):
                    xs = slice(t * P, (t + 1) * P)
                    for k in range(KD):
                        if t == 0:
                            w.wait(pe, k)
                        rhs = tuple(part[:, k, bass.ds(i * W, W)] for part in (w.hi, w.lo))
                        last = mm3(nc, PS[:, t % 2, 0:W], (c.xTh[:, k, xs], c.xTl[:, k, xs]), rhs, k == 0, k == KD - 1)
                    last.then_inc(prj, 1)

                def transposes(t):
                    pe.wait_ge(qkr, 9 * i + t + 1)
                    pe.wait_ge(qkT, 9 * i + t + 1)
                    for q in range(2):
                        nc.tensor.transpose(PS[:, 2, q * P:(q + 1) * P], qk[:, t % 3, q * P:(q + 1) * P], c.ident[:])
                    last = nc.tensor.transpose(PS[0:64, 3, 0:P], qk[:, t % 3, 256:320], c.ident[:])
                    last.then_inc(tr, 1)

                def scores(t):
                    pe.wait_ge(qkT, 9 * i + t + 2)
                    for h in range(4):
                        o = PS[:, 4 + h // 2, (h % 2) * 256:(h % 2) * 256 + 256]
                        keys = KT[0:HD + 4, max(t - 1, 0) * P:(t + 1) * P]
                        last = nc.tensor.matmul(o[:, 0:P] if t == 0 else o, QT[0:HD + 4, slot(t), h, :], keys, start=True, stop=True,
                                                skip_group_check=True)
                    last.then_inc(sc, 1)

                def p_transposes(t):
                    pe.wait_ge(ex, UN * i + t + 1)
                    pe.wait_ge(ow, UN * i + t + 1)
                    nb = 1 if t == 0 else 2
                    for h in range(4):
                        for b in range(nb):
                            n = h * nb + b
                            last = nc.tensor.transpose(PS[:, 6 + n // 4, (n % 4) * P:(n % 4 + 1) * P], Pb[:, t % 2, h * 256 + b * P:h * 256 + b * P + P],
                                                       c.ident[:])
                    last.then_inc(ptt, 1)

                def values(t):
                    nb = 1 if t == 0 else 2
                    pe.wait_ge(ptr, UN * i + t + 1)
                    pe.wait_ge(vr, 9 * i + t + 1)
                    for h in range(4):
                        for b in range(nb):
                            last = nc.tensor.matmul(PS[:, 6, h * 64:(h + 1) * 64], PTs[:, t % 2, h * nb + b, :], v[:, t - nb + 1 + b, :],
                                                    start=b == 0, stop=b == nb - 1, skip_group_check=True)
                    last.then_inc(pv, 1)

                def sample_scores_of(h):
                    if h:
                        pe.wait_ge(ex, UN * i + TP + h)
                    else:
                        pe.wait_ge(qkT, 9 * i + NT + 1)
                        pe.wait_ge(chl, 32 * i + 32)
                    for g in range(3):
                        wd = P if g == 2 else 512
                        rhs = KT[:, TP * P:] if g == 2 else cK[:, g * 512:(g + 1) * 512]
                        last = nc.tensor.matmul(PS[:, g, 0:wd], QT[:, 2, h, :], rhs, start=True, stop=True)
                    last.then_inc(sc, 1)

                def sample_transposes(h):
                    n = TP + h
                    pe.wait_ge(ex, UN * i + n + 1)
                    if h:
                        pe.wait_ge(ptr, UN * i + n)
                        pe.wait_ge(pta, 4 * i + h)
                    for k in range(NK):
                        last = nc.tensor.transpose(PS[:, 3 + k // 4, (k % 4) * P:(k % 4 + 1) * P], Pb[:, n % 2, k * P:(k + 1) * P], c.ident[:])
                    last.then_inc(ptt, 1)

                def sample_values(h):
                    n = TP + h
                    pe.wait_ge(ptr, UN * i + n + 1)
                    pe.wait_ge(pta, 4 * i + h + 1)
                    pe.wait_ge(ow, UN * i + n + 1)
                    for k in range(NK):
                        rhs = v[:, TP, :] if k == NK - 1 else cV[:, k, :]
                        last = nc.tensor.matmul(PS[:, 6, 0:64], PTs[:, n % 2, k, :], rhs, start=k == 0, stop=k == NK - 1)
                    last.then_inc(pv, 1)

                for s in range(SLOTS):
                    if s == 1:
                        pe.wait_ge(cl, 80)
                    if s < NT:
                        if s >= 2:
                            pe.wait_ge(qkr, 9 * i + s - 1)
                            pe.wait_ge(vr, 9 * i + s - 1)
                        project(s)
                    if 0 <= s - 1 < NT:
                        transposes(s - 1)
                    if 0 <= s - 3 < TP:
                        p_transposes(s - 3)
                    if 0 <= s - 2 < TP:
                        scores(s - 2)
                    if 0 <= s - FIRST < 4:
                        sample_scores_of(s - FIRST)
                    if 0 <= s - 3 < TP:
                        values(s - 3)
                    if 0 <= s - FIRST - 2 < 4:
                        sample_values(s - FIRST - 2)
                    if 0 <= s - FIRST - 1 < 4:
                        sample_transposes(s - FIRST - 1)

        @block.scalar
        def _(act):
            w.make_hi(act)
            with act.Fori(0, 2) as i:
                act.wait_ge(outs, 32 * i + 1)

                def softmax(n, heads, cols):
                    act.wait_ge(nms, UN * i + n + 1)
                    if heads == 4:
                        for h in range(4):
                            nc.scalar.activation(Pb[:, n % 2, h * 256:h * 256 + cols], PS[:, 4 + h // 2, (h % 2) * 256:(h % 2) * 256 + cols], ACT.Exp,
                                                 bias=nm[:, h:h + 1], scale=SCALE, accum_out=rs[:, h:h + 1])
                        last = nc.scalar.activation(es[:, 0:4], es[:, 0:4], ACT.Exp)
                    else:
                        h = slice(4 + n - TP, 5 + n - TP)
                        nc.scalar.activation(Pb[:, n % 2, :], sample_scores, ACT.Exp, bias=nm[:, h], scale=SCALE, accum_out=rs[:, h])
                        last = nc.scalar.activation(es[:, h], es[:, h], ACT.Exp)
                    last.then_inc(ex, 1)

                for s in range(SLOTS):
                    if s < NT:
                        act.wait_ge(prj, 9 * i + s + 2)
                        nc.scalar.activation(v[:, s, :], PS[:, s % 2, 320:384], ACT.Copy).then_inc(vr, 1)
                    if 0 <= s - 1 < NT:
                        t = s - 1
                        act.wait_ge(tr, 9 * i + t + 1)
                        if t == 0:
                            act.wait_ge(cl, 80)
                        for odd in range(2):
                            nc.scalar.activation(QT[0:HD, slot(t), odd::2, :], PS[64 * odd:64 * odd + 64, 2, 0:2 * P].rearrange("p (q n) -> p q n", q=2), ACT.Copy)
                        nc.scalar.activation(KT[0:HD, t * P:(t + 1) * P], PS[0:64, 3, 0:P], ACT.Copy).then_inc(qkT, 1)
                    if 0 <= s - 2 < TP:
                        softmax(s - 2, 4, P if s == 2 else 256)
                    if 0 <= s - FIRST < 4:
                        softmax(TP + s - FIRST, 1, 0)
                    if s == FIRST:
                        act.wait_ge(ko, 2 * i + 2)
                        act.wait_ge(vr, 9 * i + 9)
                        act.dma_start(one(A["o_swa_k"], i), kro[:]).then_inc(outs, 16)
                        act.dma_start(one(A["o_swa_v"], i), v[:, TP - 1:NT, :]).then_inc(outs, 16)
                    if 0 <= s - FIRST - 1 < 4:
                        n = TP + s - FIRST - 1
                        act.wait_ge(ptt, UN * i + n + 1)
                        nc.scalar.activation(PTs[:, n % 2, 4:NK, :], PS[:, 4:6, :].rearrange("p b n -> p (b n)")[:, 0:(NK - 4) * P]
                                             .rearrange("p (b n) -> p b n", n=P), ACT.Copy).then_inc(pta, 1)

        @block.vector
        def _(dve):
            link = Chain(dve, dch)
            w.make_lo(dve, nc.vector, 1)
            dve.wait_ge(cl, 80)
            with link.loop(2, 104) as i:
                hs = lambda ap: ap.unsqueeze(1).broadcast_to([P, 5, ap.shape[-1]])

                def rotate(t):
                    dve.wait_ge(vr, 9 * i + t + 1)
                    src = PS[:, t % 2, 0:320].rearrange("p (h d) -> p h d", h=5)
                    dst = qk[:, t % 3, :].rearrange("p (h d) -> p h d", h=5)
                    nc.vector.tensor_copy(dst[:, :, 16:64], src[:, :, 16:64])
                    nc.vector.tensor_tensor(ta[:], src[:, :, 0:16], hs(tab[:, t, 0:16]), ALU.mult)
                    nc.vector.tensor_tensor(tb[:, :, 0:8], src[:, :, 8:16], hs(tab[:, t, 16:24]), ALU.mult)
                    link(nc.vector.tensor_tensor(tb[:, :, 8:16], src[:, :, 0:8], hs(tab[:, t, 24:32]), ALU.mult))
                    link(nc.vector.tensor_tensor(dst[:, :, 0:16], ta[:], tb[:], ALU.add))
                    dve.sem_inc(qkr, 1)
                    if t >= TP - 1:
                        if t == TP - 1:
                            dve.wait_ge(outs, 32 * i + 1)
                        link(nc.vector.tensor_copy(kro[:, t - TP + 1, :], qk[:, t % 3, 256:320]))
                        dve.sem_inc(ko, 1)

                def attend(n):
                    dve.wait_ge(sc, UN * i + n + 1)
                    if n < TP:
                        cols, hh = (P if n == 0 else 256), slice(0, 4)
                        src = PS[:, 4:6, :].rearrange("p b (h n) -> p (b h) n", h=2)[:, :, 0:cols]
                        sks = sk[:, bass.ds(4 * i, 4)]
                    else:
                        h = n - TP
                        hh = slice(4 + h, 5 + h)
                        src = sample_scores
                        sks = sk[:, bass.ds(4 * i + h, 1)]
                    link(nc.vector.tensor_reduce(out=mx[:, hh], in_=src, axis=AX.X, op=ALU.max))
                    link(nc.vector.tensor_scalar(mx[:, hh], mx[:, hh], SCALE, None, ALU.mult))
                    link(nc.vector.tensor_tensor(mx[:, hh], mx[:, hh], sks, ALU.max))
                    nc.vector.tensor_tensor(es[:, hh], sks, mx[:, hh], ALU.subtract)
                    link(nc.vector.tensor_scalar(nm[:, hh], mx[:, hh], -1.0, None, ALU.mult))
                    dve.sem_inc(nms, 1)

                def take_pT(n):
                    dve.wait_ge(ptt, UN * i + n + 1)
                    nb, first, hh = (4 if n == 0 else 8, 6, slice(0, 4)) if n < TP else (4, 3, slice(4 + n - TP, 5 + n - TP))
                    nc.vector.tensor_copy(PTs[:, n % 2, 0:nb, :], PS[:, first:first + (nb + 3) // 4, :].rearrange("p b n -> p (b n)")[:, 0:nb * P]
                                          .rearrange("p (b n) -> p b n", n=P)).then_inc(ptr, 1)
                    link(nc.vector.tensor_tensor(rs[:, hh], rs[:, hh], es[:, hh], ALU.add))
                    link(nc.vector.reciprocal(ri[:, hh], rs[:, hh]))

                def write_out(n):
                    dve.wait_ge(pv, UN * i + n + 2)
                    if n < TP:
                        link(nc.vector.tensor_tensor(c.XM[:, n, bass.ds(256 * i + 512, 256)].rearrange("p (h d) -> p h d", h=4),
                                                     PS[:, 6, 0:256].rearrange("p (h d) -> p h d", h=4),
                                                     ri[:, 0:4].unsqueeze(2).broadcast_to([P, 4, 64]), ALU.mult))
                    else:
                        h = n - TP
                        link(nc.vector.tensor_scalar(c.XM[:, TP, bass.ds(256 * i + 512 + 64 * h, 64)], PS[:, 6, 0:64], ri[:, 4 + h:5 + h], None, ALU.mult))
                    dve.sem_inc(ow, 1)

                for s in range(SLOTS):
                    if s < NT:
                        rotate(s)
                    if 0 <= s - 3 < TP:
                        take_pT(s - 3)
                    if 0 <= s - 2 < TP:
                        attend(s - 2)
                    if 0 <= s - 3 < TP:
                        write_out(s - 3)
                    if 0 <= s - FIRST < 4:
                        attend(TP + s - FIRST)
                    if 0 <= s - FIRST - 2 < 4:
                        write_out(TP + s - FIRST - 2)
                    if 0 <= s - FIRST - 1 < 4:
                        take_pT(TP + s - FIRST - 1)


class Norm:

    def __init__(self, c, tag, gain, bias):
        self.c, self.nc, self.gain, self.bias = c, c.nc, gain, bias
        self.sts = c.sb(tag + "sts", [P, 2, 6])
        self.mv = c.sb(tag + "mv", [P, 2, 2])
        self.nb = c.sb(tag + "negmean", [P, 2])
        self.eps = c.sb(tag + "eps", [P, 1])
        names = ("eps", "stats", "std", "rstd", "normed", "scaled", "x_ready")
        self.ep, self.var, self.std, self.rs, self.nd, self.gd, self.xr = (c.sem(tag + s) for s in names)

    def set_eps(self, dve):
        self.nc.vector.memset(self.eps[:], LN_EPS).then_inc(self.ep, 1)

    def stats(self, dve, link, t):
        x, nc = self.c.XM[:, t, :], self.nc
        for q in range(2):
            last = nc.vector.bn_stats(self.sts[:, q, :], x[:, q * 512:(q + 1) * 512])
        link(last)
        link(nc.vector.bn_aggr(self.mv[:, t % 2, :], self.sts[:].rearrange("p a b -> p (a b)")))
        dve.sem_inc(self.var, 1)

    def root(self, act, t):
        if t == 0:
            act.wait_ge(self.ep, 1)
        act.wait_ge(self.var, t + 1)
        v = self.mv[:, t % 2, 1:2]
        self.nc.scalar.activation(v, v, ACT.Sqrt, bias=self.eps[:]).then_inc(self.std, 1)

    def rstd(self, dve, link, t):
        nc, mv = self.nc, self.mv
        dve.wait_ge(self.std, t + 1)
        link(nc.vector.reciprocal(mv[:, t % 2, 1:2], mv[:, t % 2, 1:2]))
        link(nc.vector.tensor_scalar(self.nb[:, t % 2:t % 2 + 1], mv[:, t % 2, 0:1], mv[:, t % 2, 1:2], -1.0, ALU.mult, ALU.mult))
        dve.sem_inc(self.rs, 1)

    def normalise(self, act, t):
        act.wait_ge(self.rs, t + 1)
        x = self.c.XM[:, t, :]
        self.nc.scalar.activation(x, x, ACT.Identity, bias=self.nb[:, t % 2:t % 2 + 1], scale=self.mv[:, t % 2, 1:2]).then_inc(self.nd, 1)

    def scale(self, pool, t):
        pool.wait_ge(self.nd, t + 1)
        x = self.c.XM[:, t, :]
        self.nc.gpsimd.tensor_tensor(x, x, self.gain, ALU.mult).then_inc(self.gd, 1)

    def add_bias(self, dve, t):
        dve.wait_ge(self.gd, t + 1)
        x = self.c.XM[:, t, :]
        self.nc.vector.tensor_tensor(x, x, self.bias, ALU.add).then_inc(self.xr, 1)


def phase_mix_out(c, layer):
    nc, A, PS = c.nc, c.A, c.PS
    tag = f"mo{layer}_"
    w = Split(c, tag + "w", KD, D, lambda i, k: A[f"w_out{layer}"][k])
    xin, gb = w.raw[:, 0:2, :], w.raw[:, 2:4, :]
    norm = Norm(c, tag, gb[:, 0, :], gb[:, 1, :])
    mTh = c.sb(tag + "mTh", [P, 2, KD, P], R)
    mTl = c.sb(tag + "mTl", [P, 2, KD, P], R)
    names = ("gb_loaded", "x_loaded", "x_used", "mix_transposed", "mixT_hi", "mixT_ready", "projected",
             "x_transposed", "xT_hi", "xT_ready", "dve")
    (gl, xl, xu, mt, mh, ml, om, xt, xh, xlo, dch) = (c.sem(tag + s) for s in names)
    xl = (xl, c.sem(tag + "x_loaded1"))
    resid = A["x_in"] if layer == 0 else A["x1"]
    flat = lambda a, b: PS[:, a:b, :].rearrange("p b n -> p (b n)")
    with nc.Block() as block:
        @block.sync
        def _(sp):
            w.load(sp)
            for t in range(NT):
                if t < 2:
                    sp.wait_ge(w.w_split[t], 6)
                if t >= 2:
                    sp.wait_ge(xu, t - 1)
                sp.dma_start(xin[:, t % 2, :], resid[t]).then_inc(xl[t % 2], 16)
                if t == 1:
                    for half, n in enumerate(("ln_mix_g", "ln_mix_b")):
                        w.wait(sp, 6 + half)
                        sp.dma_start(gb[:, half, :], A[n][layer].partition_broadcast(P)).then_inc(gl, 16)

        @block.gpsimd
        def _(pool):
            w.free_slots(pool)
            w.make_lo(pool, nc.gpsimd, 0)
            pool.wait_ge(gl, 32)
            for t in range(NT):
                norm.scale(pool, t)

        @block.tensor
        def _(pe):
            def mix_t(t):
                if t:
                    pe.wait_ge(ml, t)
                for k in range(KD):
                    last = nc.tensor.transpose(PS[:, k // 4, (k % 4) * P:(k % 4 + 1) * P], c.XM[:, t, k * P:(k + 1) * P], c.ident[:])
                last.then_inc(mt, 1)

            def x_t(t):
                pe.wait_ge(norm.xr, t + 1)
                if t:
                    pe.wait_ge(xlo, t)
                for k in range(KD):
                    last = nc.tensor.transpose(PS[:, 6 + k // 4, (k % 4) * P:(k % 4 + 1) * P], c.XM[:, t, k * P:(k + 1) * P], c.ident[:])
                last.then_inc(xt, 1)

            mix_t(0)
            for t in range(NT):
                pe.wait_ge(ml, t + 1)
                if t >= 2:
                    pe.wait_ge(xu, t - 1)
                for half in range(2):
                    cs = slice(half * 512, half * 512 + 512)
                    for k in range(KD):
                        if t == 0:
                            w.wait(pe, k)
                        last = mm3(nc, PS[:, 2 + 2 * (t % 2) + half, :], (mTh[:, t % 2, k, :], mTl[:, t % 2, k, :]), (w.hi[:, k, cs], w.lo[:, k, cs]),
                                   k == 0, k == KD - 1)
                    if half == 0 and t + 1 < NT:
                        mix_t(t + 1)
                last.then_inc(om, 1)
                if t >= 2:
                    x_t(t - 2)
            x_t(NT - 2)
            x_t(NT - 1)

        @block.scalar
        def _(act):
            def mix_hi(t):
                act.wait_ge(mt, t + 1)
                if t >= 2:
                    act.wait_ge(om, t - 1)
                nc.scalar.activation(mTh[:, t % 2].rearrange("p k n -> p (k n)"), flat(0, 2), ACT.Copy).then_inc(mh, 1)

            def x_hi(t):
                act.wait_ge(xt, t + 1)
                nc.scalar.activation(c.xTh[:, :, t * P:(t + 1) * P], flat(6, 8).rearrange("p (k n) -> p k n", n=P), ACT.Copy).then_inc(xh, 1)
                nc.scalar.activation(c.XM[:, t, :], c.XM[:, t, :], ACT.Copy, scale=ALPHA)

            mix_hi(0)
            w.make_hi(act)
            for t in range(NT):
                if t + 1 < NT:
                    mix_hi(t + 1)
                if t >= 3:
                    x_hi(t - 3)
                norm.root(act, t)
                norm.normalise(act, t)
            for t in range(NT - 3, NT):
                x_hi(t)

        @block.vector
        def _(dve):
            link = Chain(dve, dch)
            norm.set_eps(dve)

            def mix_lo(t):
                dve.wait_ge(mh, t + 1)
                nc.vector.tensor_tensor(mTl[:, t % 2].rearrange("p k n -> p (k n)"), flat(0, 2), mTh[:, t % 2].rearrange("p k n -> p (k n)").bitcast(F),
                                        ALU.subtract).then_inc(ml, 1)

            def x_lo(t):
                dve.wait_ge(xh, t + 1)
                ts = slice(t * P, (t + 1) * P)
                nc.vector.tensor_tensor(c.xTl[:, :, ts], flat(6, 8).rearrange("p (k n) -> p k n", n=P), c.xTh[:, :, ts].bitcast(F),
                                        ALU.subtract).then_inc(xlo, 1)

            mix_lo(0)
            w.make_lo(dve, nc.vector, 1)
            for t in range(NT):
                if t + 1 < NT:
                    mix_lo(t + 1)
                if t >= 3:
                    x_lo(t - 3)
                if t >= 1:
                    norm.add_bias(dve, t - 1)
                dve.wait_ge(om, t + 1)
                dve.wait_ge(xl[t % 2], 16 * (t // 2 + 1))
                link(nc.vector.scalar_tensor_tensor(c.XM[:, t, :], xin[:, t % 2, :], ALPHA, flat(2 + 2 * (t % 2), 4 + 2 * (t % 2)), ALU.mult, ALU.add))
                dve.sem_inc(xu, 1)
                norm.stats(dve, link, t)
                norm.rstd(dve, link, t)
            x_lo(NT - 3)
            norm.add_bias(dve, NT - 1)
            x_lo(NT - 2)
            x_lo(NT - 1)


def phase_ffn(c, layer):
    nc, A, PS = c.nc, c.A, c.PS
    tag = f"ff{layer}_"
    wraw = c.sb(tag + "wraw", [P, 2, D])
    whi = c.sb(tag + "whi", [P, 2, KD, P], R)
    wlo = c.sb(tag + "wlo", [P, 2, KD, P], R)
    draw = c.sb(tag + "draw", [P, D])
    dhi = c.sb(tag + "dhi", [P, 2, D], R)
    dlo = c.sb(tag + "dlo", [P, 2, D], R)
    u = c.sb(tag + "u", [P, 2, UW])
    cv = c.sb(tag + "c", [P, 2, UW])
    gf = c.sb(tag + "g", [P, TOK])
    gh = c.sb(tag + "gh", [P, 2, TOK], R)
    gl = c.sb(tag + "gl", [P, 2, TOK], R)
    cw = c.sb(tag + "cw", [P, 2, NJ * 4])
    old = c.sb(tag + "old", [P, 2, NJ * 16])
    new = c.sb(tag + "new", [P, 2, NJ * 18])
    names = ("consts", "a_loaded", "b_loaded", "d_loaded", "up_hi", "up_split", "d_hi", "d_split", "up_done", "u_ready", "c0_ready", "conv_done",
             "halo_ready", "state_kept", "silu_done", "g_ready", "g_hi", "g_split", "down_done", "added", "stored", "dve")
    (cl, la, lb, ld, uh, us, dh, dsp, um, ur, c0, cvd, hl, sk, si, gr, ghd, gs, dm, ad, outs, dch) = (c.sem(tag + s) for s in names)
    lab = (la, lb)

    def ge(eng, sem, v):
        if not isinstance(v, int) or v > 0:
            eng.wait_ge(sem, v)

    def chunks(eng, step):
        step(0, 0)
        with eng.Fori(0, (NJ - 2) // 2) as r:
            step(2 * r + 1, 1)
            step(2 * r + 2, 0)
        step(NJ - 1, 1)

    def pick(ap, j):
        return ap[j] if isinstance(j, int) else one(ap, j)

    def cols(j, a, n):
        return slice(j * a, j * a + n) if isinstance(j, int) else bass.ds(j * a, n)

    with nc.Block() as block:
        @block.sync
        def _(sp):
            def step(j, par):
                for ab in range(2):
                    ge(sp, us, 2 * j + ab - 1)
                    sp.dma_start(wraw[:, ab, :], pick(A["w_up"][layer, :, ab], j)).then_inc(lab[ab], 16)
                if isinstance(j, int) and j == 0:
                    sp.dma_start(cw[:], A["conv_w"][layer]).then_inc(cl, 16)
                    sp.dma_start(old[:], A["conv_old"][layer]).then_inc(cl, 16)
                ge(sp, dsp, j)
                sp.dma_start(draw[:], pick(A["w_down"][layer], j)).then_inc(ld, 16)

            chunks(sp, step)
            sp.wait_ge(sk, 2 * NJ)
            sp.dma_start(A["o_conv"][layer], new[:]).then_inc(outs, 16)
            sp.wait_ge(outs, 16)

        @block.gpsimd
        def _(pool):
            for started in (ad, dm):
                pool.sem_inc(started, 1)
            def split_up(j, ab):
                pool.wait_ge(uh, 2 * j + ab + 1)
                nc.gpsimd.tensor_tensor(wlo[:, ab].rearrange("p k n -> p (k n)"), wraw[:, ab, :],
                                        whi[:, ab].rearrange("p k n -> p (k n)").bitcast(F), ALU.subtract).then_inc(us, 1)

            def step(j, par):
                for ab in range(2):
                    ge(pool, cvd, 2 * j + ab - 1)
                    halo = u[:, ab, US:].rearrange("p (b t) -> p b t", b=NB)[:, :, 0:2]
                    nc.gpsimd.tensor_copy(halo, old[:, ab, cols(j, 16, 16)].rearrange("p (b t) -> p b t", b=NB)).then_inc(hl, 1)
                pool.wait_ge(dh, j + 1)
                nc.gpsimd.tensor_tensor(dlo[:, par, :], draw[:], dhi[:, par, :].bitcast(F), ALU.subtract).then_inc(dsp, 1)
                for ab in range(2):
                    pool.wait_ge(ur, 6 * j + 3 * ab + 3)
                    keep = new[:, ab, cols(j, 18, 18)]
                    nc.gpsimd.tensor_copy(keep[:, 0:2], u[:, ab, SEQ:SEQ + 2])
                    nc.gpsimd.tensor_copy(keep[:, 2:18].rearrange("p (b t) -> p b t", b=NB),
                                          u[:, ab, US:].rearrange("p (b t) -> p b t", b=NB)[:, :, ST:ST + 2]).then_inc(sk, 1)
                    if not isinstance(j, int) or j + 1 < NJ:
                        split_up(j + 1, ab)
                pool.wait_ge(ghd, j + 1)
                nc.gpsimd.tensor_tensor(gl[:, par, :], gf[:], gh[:, par, :].bitcast(F), ALU.subtract).then_inc(gs, 1)

            nc.gpsimd.memset(u[:, :, 0:2], 0.0)
            split_up(0, 0)
            split_up(0, 1)
            pool.wait_ge(cl, 32)
            chunks(pool, step)

        @block.tensor
        def _(pe):
            def up(j):
                for ab in range(2):
                    pe.wait_ge(us, 2 * j + ab + 1)
                    for q in range(3):
                        ge(pe, ur, 6 * j + 3 * ab + q - 2)
                        xs = slice(q * GRP, (q + 1) * GRP)
                        for k in range(KD):
                            last = mm3(nc, PS[:, q, 0:GRP], (whi[:, ab, k, :], wlo[:, ab, k, :]), (c.xTh[:, k, xs], c.xTl[:, k, xs]),
                                       k == 0, k == KD - 1)
                        last.then_inc(um, 1)

            def down(j, par):
                pe.wait_ge(gs, j + 1)
                pe.wait_ge(dsp, j + 1)
                for t in range(NT):
                    ge(pe, ad, 9 * j + max(t - 1, 0) + 1)
                    a = tuple(g[:, par, t * P:(t + 1) * P] for g in (gh, gl))
                    for half in range(2):
                        cs = slice(half * 512, half * 512 + 512)
                        last = mm3(nc, PS[:, 3 + 2 * ((t + par) % 2) + half, :], a, (dhi[:, par, cs], dlo[:, par, cs]), True, True)
                    last.then_inc(dm, 1)

            up(0)
            with pe.Fori(0, (NJ - 2) // 2) as r:
                up(2 * r + 1)
                down(2 * r, 0)
                up(2 * r + 2)
                down(2 * r + 1, 1)
            up(NJ - 1)
            down(NJ - 2, 0)
            down(NJ - 1, 1)

        @block.scalar
        def _(act):
            def hi_up(j, ab):
                act.wait_ge(lab[ab], 16 * j + 16)
                ge(act, um, 6 * j + 3 * ab - 3)
                nc.scalar.activation(whi[:, ab].rearrange("p k n -> p (k n)"), wraw[:, ab, :], ACT.Copy).then_inc(uh, 1)

            def step(j, par):
                act.wait_ge(ld, 16 * j + 16)
                ge(act, dm, 9 * j - 9 + 1)
                nc.scalar.activation(dhi[:, par, :], draw[:], ACT.Copy).then_inc(dh, 1)
                for ab in range(2):
                    ge(act, cvd, 2 * j + ab - 1)
                    ge(act, sk, 2 * j + ab - 1)
                    for q in range(3):
                        act.wait_ge(um, 6 * j + 3 * ab + q + 1)
                        if q < 2:
                            last = nc.scalar.activation(u[:, ab, 2 + q * GRP:2 + (q + 1) * GRP], PS[:, q, 0:GRP], ACT.Copy)
                        else:
                            nc.scalar.activation(u[:, ab, 2 + 2 * GRP:US], PS[:, 2, 0:SEQ - 2 * GRP], ACT.Copy)
                            last = nc.scalar.activation(u[:, ab, US:].rearrange("p (b t) -> p b t", b=NB)[:, :, 2:],
                                                        PS[:, 2, SEQ - 2 * GRP:GRP].rearrange("p (b t) -> p b t", b=NB), ACT.Copy)
                        last.then_inc(ur, 1)
                    act.wait_ge(ur, 6 * j + 3 * ab + 3)
                    act.wait_ge(hl, 2 * j + ab + 1)
                    ge(act, gr, j)
                    nc.scalar.activation(cv[:, ab, 2:], u[:, ab, 2:], ACT.Identity, bias=cw[:, ab, cols4(j, 3)], scale=cw[:, ab, cols4(j, 2)]).then_inc(c0, 1)
                    if not isinstance(j, int) or j + 1 < NJ:
                        hi_up(j + 1, ab)
                act.wait_ge(cvd, 2 * j + 1)
                nc.scalar.activation(cv[:, 0, 2:], cv[:, 0, 2:], ACT.Silu).then_inc(si, 1)
                act.wait_ge(gr, j + 1)
                nc.scalar.activation(gh[:, par, :], gf[:], ACT.Copy).then_inc(ghd, 1)

            def cols4(j, n):
                return slice(4 * j + n, 4 * j + n + 1) if isinstance(j, int) else bass.ds(4 * j + n, 1)

            hi_up(0, 0)
            hi_up(0, 1)
            act.wait_ge(cl, 32)
            chunks(act, step)

        @block.vector
        def _(dve):
            def col4(j, n):
                return slice(4 * j + n, 4 * j + n + 1) if isinstance(j, int) else bass.ds(4 * j + n, 1)

            def conv(j, ab):
                dve.wait_ge(c0, 2 * j + ab + 1)
                nc.vector.scalar_tensor_tensor(cv[:, ab, 2:], u[:, ab, 1:UW - 1], cw[:, ab, col4(j, 1)], cv[:, ab, 2:], ALU.mult, ALU.add).then_inc(dch, 1)
                dve.wait_ge(dch, 2 * j + ab + 1)
                nc.vector.scalar_tensor_tensor(cv[:, ab, 2:], u[:, ab, 0:UW - 2], cw[:, ab, col4(j, 0)], cv[:, ab, 2:], ALU.mult, ALU.add).then_inc(cvd, 1)

            def gate(j):
                dve.wait_ge(si, j + 1)
                dve.wait_ge(cvd, 2 * j + 2)
                ge(dve, gs, j)
                nc.vector.tensor_tensor(gf[:, 0:SEQ], cv[:, 0, 2:US], cv[:, 1, 2:US], ALU.mult)
                new_a, new_b = (cv[:, ab, US:].rearrange("p (b t) -> p b t", b=NB)[:, :, 2:] for ab in range(2))
                nc.vector.tensor_tensor(gf[:, SEQ:].rearrange("p (b t) -> p b t", b=NB), new_a, new_b, ALU.mult).then_inc(gr, 1)

            def add(j, t, par):
                dve.wait_ge(dm, 9 * j + t + 2)
                b = 3 + 2 * ((t + par) % 2)
                nc.vector.tensor_tensor(c.XM[:, t, :], c.XM[:, t, :], PS[:, b:b + 2, :].rearrange("p b n -> p (b n)"), ALU.add).then_inc(ad, 1)

            def step(j, par):
                conv(j, 0)
                for t in range(NT):
                    add(j - 1, t, 1 - par)
                conv(j, 1)
                gate(j)

            conv(0, 0)
            conv(0, 1)
            gate(0)
            with dve.Fori(0, (NJ - 2) // 2) as r:
                step(2 * r + 1, 1)
                step(2 * r + 2, 0)
            conv(NJ - 1, 0)
            conv(NJ - 1, 1)
            add(NJ - 2, 0, 0)
            add(NJ - 2, 1, 0)
            gate(NJ - 1)
            for t in range(2, NT):
                add(NJ - 2, t, 0)
            for t in range(NT):
                add(NJ - 1, t, 1)


def phase_ffn_norm(c, layer):
    nc, A, PS = c.nc, c.A, c.PS
    tag = f"fn{layer}_"
    gb = c.sb(tag + "gb", [P, 2, D])
    norm = Norm(c, tag, gb[:, 0, :], gb[:, 1, :])
    names = ("consts", "x_transposed", "xT_hi", "xT_ready", "dve", "stored")
    (cl, xt, xh, xlo, dch, outs) = (c.sem(tag + s) for s in names)
    dst = A["x1"] if layer == 0 else A["o_y"]
    flat = lambda a, b: PS[:, a:b, :].rearrange("p b n -> p (b n)")
    more = layer == 0
    with nc.Block() as block:
        @block.sync
        def _(sp):
            sp.dma_start(gb[:, 0, :], A["ln_ffn_g"][layer].partition_broadcast(P)).then_inc(cl, 16)
            sp.dma_start(gb[:, 1, :], A["ln_ffn_b"][layer].partition_broadcast(P)).then_inc(cl, 16)
            for t in range(NT):
                sp.wait_ge(norm.xr, t + 1)
                sp.dma_start(dst[t], c.XM[:, t, :]).then_inc(outs, 16)
            sp.wait_ge(outs, 16 * NT)

        @block.gpsimd
        def _(pool):
            pool.wait_ge(cl, 32)
            for t in range(NT):
                norm.scale(pool, t)

        if more:
            @block.tensor
            def _(pe):
                for t in range(NT):
                    pe.wait_ge(norm.xr, t + 1)
                    if t >= 2:
                        pe.wait_ge(xlo, t - 1)
                    for k in range(KD):
                        last = nc.tensor.transpose(PS[:, 2 * (t % 2) + k // 4, (k % 4) * P:(k % 4 + 1) * P], c.XM[:, t, k * P:(k + 1) * P], c.ident[:])
                    last.then_inc(xt, 1)

        @block.scalar
        def _(act):
            for t in range(NT + 3):
                if more and t >= 3:
                    s = t - 3
                    act.wait_ge(xt, s + 1)
                    nc.scalar.activation(c.xTh[:, :, s * P:(s + 1) * P], flat(2 * (s % 2), 2 * (s % 2) + 2).rearrange("p (k n) -> p k n", n=P),
                                         ACT.Copy).then_inc(xh, 1)
                if t < NT:
                    norm.root(act, t)
                    norm.normalise(act, t)

        @block.vector
        def _(dve):
            link = Chain(dve, dch)
            norm.set_eps(dve)
            for t in range(NT + 3):
                if t < NT:
                    norm.stats(dve, link, t)
                if 2 <= t < NT + 2:
                    norm.add_bias(dve, t - 2)
                if more and t >= 3:
                    s = t - 3
                    ts = slice(s * P, (s + 1) * P)
                    dve.wait_ge(xh, s + 1)
                    nc.vector.tensor_tensor(c.xTl[:, :, ts], flat(2 * (s % 2), 2 * (s % 2) + 2).rearrange("p (k n) -> p k n", n=P),
                                            c.xTh[:, :, ts].bitcast(F), ALU.subtract).then_inc(xlo, 1)
                if t < NT:
                    norm.rstd(dve, link, t)


class Bag:
    pass


def build(nc, A, mask_columns, stages=99):
    c = Ctx(nc, A)
    c.at = mask_columns
    c.xTh = c.sb("xT_hi", [P, KD, TOK], R)
    c.xTl = c.sb("xT_lo", [P, KD, TOK], R)
    c.XM = c.sb("x_or_mix", [P, NT, D])
    c.ident = c.sb("ident", [P, P])
    c.PS = nc.alloc_psum_tensor("psum", [P, 8, 512], F)
    c.masks = c.sb("masks", list(A["masks"].shape))

    def run(phase, *args):
        with nc.cleanup_on_exit():
            phase(c, *args)

    run(phase_start)
    with nc.cleanup_on_exit():
        M = Bag()
        M.latT = c.sb("latT", [P, 4, TOK])
        M.KT = c.sb("mla_kT", [P, TOK])
        M.T = c.sb("mla_tab", [P, TOK])
        M.ckv_s = c.sb("ckv_new", [P, 256])
        run(phase_latents, M)
        M.rows = c.sb("mla_rows", list(A["mla_rows"].shape))
        M.qabs = c.sb("q_abs", [P, 2, MLA_H, P])
        M.qpe = c.sb("q_pe", [P, MLA_H, P])
        M.wuv = c.sb("w_uv", [P, 2, 512])
        if stages > 1:
            run(phase_mla_prompt, M)
        if stages > 2:
            run(phase_mla_sample, M)
    if stages > 3:
        run(phase_linear, True)
    if stages > 4:
        run(phase_mix_out, 0)
    if stages > 5:
        run(phase_ffn, 0)
    if stages > 6:
        run(phase_ffn_norm, 0)
    if stages > 7:
        with nc.cleanup_on_exit():
            G = Bag()
            G.eB = c.sb("gla_eB", [P, NT, 256])
            G.eN = c.sb("gla_eN", [P, NT, 256])
            G.dec = c.sb("gla_dec", [64, 96])
            G.decs = c.sb("gla_decs", [64, 32])
            run(phase_gates, G)
            run(phase_linear, False, G)
    if stages > 8:
        run(phase_swa)
    if stages > 9:
        run(phase_mix_out, 1)
        run(phase_ffn, 1)
        run(phase_ffn_norm, 1)



def rope_angles(pos, dim, theta):
    inv = (np.float32(1.0) / (np.float32(theta) ** (np.arange(0, dim, 2, dtype=np.float32) / np.float32(dim)))).astype(np.float32)
    ang = pos.astype(np.float32)[:, None] * inv[None, :]
    return np.cos(ang).astype(np.float32), np.sin(ang).astype(np.float32)


def constants():
    tok = np.arange(P)
    pos = np.concatenate([np.arange(SEQ), np.tile(PAST + np.arange(ST), NB)])
    stream = tok // ST
    out = {"ident": np.eye(P, dtype=np.float32)}
    m = {}
    tri = (tok[:, None] <= tok[None, :]).astype(np.float32)
    m["TRI"] = tri
    m["TRIS"] = tri * (stream[:, None] == stream[None, :])
    m["MID"] = tri - (tok[:, None] < 64).astype(np.float32)
    m["OWN8"] = (stream[:, None] == np.arange(NB)[None, :]).astype(np.float32)
    m["SEL"] = np.stack([tok < 64, tok >= 64, tok >= 0], 1).astype(np.float32)
    m["ROW"] = (tok[None, :] < 64) * np.ones((1, 1), np.float32)
    m["NEG"] = NEG * (tok[None, :] >= 64)
    m["OWN"] = NEG * (stream[None, :] != np.arange(NB)[:, None]).reshape(1, NB * P)
    groups = {"masks": ("TRI", "TRIS", "MID", "OWN8", "SEL"), "mla_rows": ("ROW", "NEG"), "mla_own": ("OWN",)}
    cols = {}
    for group, members in groups.items():
        rows = max(m[n].shape[0] for n in members)
        parts, at = [], 0
        for n in members:
            full = np.zeros((rows, m[n].shape[1]), np.float32)
            full[:m[n].shape[0]] = m[n]
            cols[n] = at
            at += full.shape[1]
            parts.append(full)
        out[group] = np.concatenate(parts, 1)
    qr = np.zeros((8, 3, 4, P))
    kr = np.zeros((8, NT, P))
    for e in range(2):
        for half in range(2):
            qr[2 * e + half, e] = tok // 64 == half
        kr[2 * e, e:TP:2, 64:] = NEG
        kr[2 * e + 1, 1 - e:TP:2, :64] = NEG
    qr[:, 2] = (np.arange(NB)[:, None] == stream[None, :])[:, None]
    kr[:, TP] = NEG * (np.arange(NB)[:, None] != stream[None, :])
    out["swa_q_rows"], out["swa_k_rows"] = qr.reshape(8, -1), kr.reshape(8, -1)
    out["swa_c_rows"] = NEG * (np.arange(NB)[:, None] != np.repeat(np.arange(NB), P)[None, :])
    cos, sin = rope_angles(pos, ROPE, 500000.0)
    out["kpe_tab"] = np.concatenate([cos.T, cos.T, -sin.T, sin.T], 0)
    tiles = lambda a: np.ascontiguousarray(a.reshape(NT, P, -1).transpose(1, 0, 2))
    cos, sin = rope_angles(pos, HD, 10000.0)
    out["ret_cos"] = tiles(np.concatenate([cos, cos], 1))
    out["ret_sin"] = tiles(np.concatenate([-sin, sin], 1))
    cos, sin = rope_angles(pos, HD // 4, 500000.0)
    out["swa_tab"] = tiles(np.concatenate([cos, cos, -sin, sin], 1))
    gamma = np.log(1.0 - 2.0 ** (-5.0 - np.arange(8)))
    pw = np.zeros((P, 2, 4, 4))
    gd = np.zeros((P, 4, 2, P))
    for kind, (local, length) in enumerate(((tok, P), (tok % ST, ST))):
        for pair in range(4):
            for h in range(2):
                g = gamma[2 * pair + h]
                pw[:, kind, pair, h] = np.exp(g * (local + 1))
                pw[:, kind, pair, 2 + h] = np.exp(-g * (local + 1)) * HD ** -0.5
                gd[64 * h:64 * h + 64, pair, kind, 64 * h:64 * h + 64] = np.exp(g * length)
    out["ret_pow"] = pw.reshape(P, 2, 16)
    out["ret_decay"] = gd
    return {n: np.ascontiguousarray(a, dtype=np.float32) for n, a in out.items()}, cols


def layout(x):
    f = {n: np.asarray(a) for n, a in x.items()}
    out = {}
    xs = np.concatenate([f["x_prompt"].reshape(SEQ, D), f["x_sample"].reshape(P, D)])
    out["x_in"] = xs.reshape(NT, P, D)
    out["xT"] = xs.T.reshape(KD, P, TOK).transpose(1, 0, 2).reshape(P, KD * TOK)
    we = f["w_in_even"][0]
    kpe = we[:, 512:544]
    sw = np.concatenate([kpe[:, 16:], kpe[:, :16]], 1)
    out["w_lat"] = np.concatenate([we[:, :512], kpe, sw, kpe, sw], 1).reshape(KD, P, 640)
    parts = [we[:, 544 + 512 * n:544 + 512 * (n + 1)].reshape(D, 4, P) for n in range(4)]
    out["w_ret"] = np.stack(parts, 2).transpose(1, 0, 2, 3).reshape(4, KD, P, 512)
    uq = f["mla_w_uq"][0].reshape(2, P, MLA_H, 96)
    uq = np.concatenate([uq, uq[..., 80:96], uq[..., 64:80]], -1)
    out["w_uq"] = uq.transpose(2, 1, 0, 3)
    ukv = f["mla_w_ukv"][0].reshape(2, P, MLA_H, 128)
    out["w_uk"] = ukv[..., :64].transpose(2, 1, 0, 3)
    out["w_ukT"] = ukv[..., :64].transpose(2, 3, 0, 1).reshape(MLA_H, 64, 256)
    out["w_uv"] = ukv[..., 64:].transpose(1, 0, 2, 3).reshape(P, 2, 512)
    out["lat_norm"] = np.concatenate([f["mla_q_norm"][0], f["mla_kv_norm"][0]])
    ckv = f["cache_mla_ckv"][0]
    out["c_ckv"] = ckv.reshape(NB, PAST // P, P, 256).transpose(0, 2, 1, 3)
    out["c_ckvT"] = ckv.transpose(0, 2, 1).reshape(NB, 2, P, PAST).transpose(0, 2, 1, 3)
    out["c_kpeT"] = f["cache_mla_kpe"][0].transpose(0, 2, 1)
    out["state_ret"] = f["state_ret"][0]
    out["state_gla"] = f["state_gla"][0]
    out["ret_norm"] = f["ret_norm"][0]
    out["gla_norm"] = f["gla_norm"][0]
    out["w_out0"] = f["w_out_even"][0].reshape(KD, P, D)
    out["w_out1"] = f["w_out_odd"][0].reshape(KD, P, D)
    wo = f["w_in_odd"][0]
    q, k = (wo[:, 256 * n:256 * (n + 1)].reshape(D, 4, 64) for n in range(2))
    v, g = (wo[:, 512 * n:512 * (n + 1)].reshape(D, 4, P) for n in (1, 2))
    out["w_gla"] = np.concatenate([q, k, v, g], 2).transpose(1, 0, 2).reshape(4, KD, P, 384)
    out["w_ga"] = np.tile(wo[:, 1536:1552], (1, 8)).reshape(KD, P, P)
    out["w_a2b"] = np.concatenate([f["gla_w_a2"][0], f["gla_b_a"]], 0)
    q = wo[:, 1552:2064].reshape(D, 2, 256)
    k = wo[:, 2064:2192].reshape(D, 2, 64)
    v = wo[:, 2192:2320].reshape(D, 2, 64)
    out["w_swa"] = np.concatenate([q, k, v], 2).reshape(KD, P, 768)
    out["sinks"] = f["swa_sinks"][0]
    ck, cv = f["cache_swa_k"][0], f["cache_swa_v"][0]
    out["c_swa_kT"] = ck.transpose(2, 3, 0, 1).reshape(2, 64, NB * P)
    out["c_swa_v"] = cv.transpose(2, 1, 0, 3)
    out["c_swa_k_old"] = ck[:, ST:].reshape(NB, -1)
    out["c_swa_v_old"] = cv[:, ST:].reshape(NB, -1)
    up = f["ffn_w_up"].reshape(2, KD, P, 2, NJ, P)
    out["w_up"] = up.transpose(0, 4, 3, 2, 1, 5).reshape(2, NJ, 2, P, D)
    out["w_down"] = f["ffn_w_down"].reshape(2, NJ, P, D)
    cw = np.concatenate([f["ffn_conv_w"], f["ffn_conv_b"][:, None]], 1).reshape(2, 4, 2, NJ, P)
    out["conv_w"] = cw.transpose(0, 4, 2, 3, 1).reshape(2, P, 2, NJ * 4)
    old = f["state_ffn_conv"].reshape(2, NB * 2, 2, NJ, P)
    out["conv_old"] = old.transpose(0, 4, 2, 3, 1).reshape(2, P, 2, NJ * 16)
    for n in ("ln_mix_g", "ln_mix_b", "ln_ffn_g", "ln_ffn_b"):
        out[n] = f[n]
    return {n: np.ascontiguousarray(a) for n, a in out.items()}


OUTPUTS = {
    "o_y": (NT, P, D), "o_ckv_p": (SEQ, 256), "o_ckv_s": (P, 256), "o_kpe": (ROPE, TOK),
    "o_ret_p": (8, 64, 64), "o_ret_s": (NB, 8, 64, 64), "o_gla_p": (4, 64, P), "o_gla_s": (NB, 4, 64, P),
    "o_swa_k": (2, P, 2, HD), "o_swa_v": (2, P, 2, HD), "o_swa_k_old": (NB, 112 * 128), "o_swa_v_old": (NB, 112 * 128),
    "o_conv": (2, P, 2, NJ * 18),
}


def returned(o):
    y = o["o_y"].reshape(TOK, D)
    kpe = o["o_kpe"].T
    conv = o["o_conv"].reshape(2, P, 2, NJ, 18)
    conv = conv.transpose(0, 4, 2, 3, 1).reshape(2, 18, 2 * FF)
    kv = []
    for n in ("k", "v"):
        new = o["o_swa_" + n]
        kv.append(new[:, :, 0].transpose(1, 0, 2)[None, None])
        s = new[:, :, 1].transpose(1, 0, 2).reshape(NB, ST, 2, HD)
        kv.append(np.concatenate([o[f"o_swa_{n}_old"].reshape(NB, P - ST, 2, HD), s], 1)[None])
    kp, ks, vp, vs = kv
    c = np.ascontiguousarray
    return (c(y[:SEQ].reshape(1, SEQ, D)), c(y[SEQ:].reshape(NB, ST, D)), o["o_ckv_p"].reshape(1, 1, SEQ, 256),
            c(kpe[:SEQ]).reshape(1, 1, SEQ, ROPE), o["o_ret_p"][None, None], o["o_gla_p"][None, None], c(kp), c(vp),
            c(conv[:, :2]).reshape(2, 1, 2, 2 * FF), o["o_ckv_s"].reshape(1, NB, ST, 256), c(kpe[SEQ:]).reshape(1, NB, ST, ROPE),
            o["o_ret_s"][None], o["o_gla_s"][None], c(ks), c(vs), c(conv[:, 2:]).reshape(2, NB, 2, 2 * FF))


def kernel(**inputs):
    import concourse.bacc as bacc
    from concourse.bass_utils import run_bass_kernel_spmd as run

    nc = bacc.Bacc("TRN2", target_bir_lowering=False, num_devices=1)
    const, cols = constants()
    arrays = {"in_" + n: a for n, a in (layout(inputs) | const).items()}
    A = {n[3:]: nc.dram_tensor(n, a.shape, mybir.dt.from_np(a.dtype), kind="ExternalInput").ap() for n, a in arrays.items()}
    for n, shape in OUTPUTS.items():
        A[n] = nc.dram_tensor(n, shape, F, kind="ExternalOutput").ap()
    A["x1"] = nc.dram_tensor("x_between_layers", (NT, P, D), F, kind="Internal").ap()
    build(nc, A, cols)
    r = run(nc, [arrays], core_ids=[0])
    return returned({n: np.asarray(r.results[0][n]) for n in OUTPUTS})
```
